# Optimizing a Trainium2 kernel written in Bass

```python
import jax, jax.numpy as jnp
from jax import lax
import numpy as np

D_MODEL = 2048
BATCH = 1
SEQ = 512
DEPTH = 1

GRID_W = 64
CTX_LEN = 256
EPS = 1e-6
A_HEADS = 8
A_DK = 128
A_DV = 128
A_W = A_HEADS * A_DV
A_CONV = 5
A_CHUNK = 64
B_HEADS = 8
B_KV = 2
B_HD = 128
B_W = B_HEADS * B_HD
Q_BLOCK = 128
ROPE_THETA = 10000.0
CONV_CH = 2 * A_HEADS * A_DK + A_W
IN_COLS = 2 * A_HEADS * A_DK + 2 * A_W + 4 * A_HEADS + 2 * B_W + 2 * B_KV * B_HD + 2 * D_MODEL

kernel_name = 'hybrid_gdn_gqa_dit_block'

def rms_norm(x, w):
    xf = x.astype(jnp.float32)
    xf = xf * lax.rsqrt(jnp.mean(xf * xf, axis=-1, keepdims=True) + EPS)
    return (xf * w.astype(jnp.float32)).astype(x.dtype)

def l2_norm(x):
    return x * lax.rsqrt(jnp.sum(x * x, axis=-1, keepdims=True) + EPS)

def modulate(x, norm_w, shift, scale):
    return rms_norm(x, norm_w) * (1.0 + scale) + shift

def _flip(a):
    return a[:, ::-1]

def split_in(p):
    sizes = [A_HEADS * A_DK, A_HEADS * A_DK, A_W, A_W, 2 * A_HEADS, 2 * A_HEADS,
             B_W, B_KV * B_HD, B_KV * B_HD, B_W, 2 * D_MODEL]
    idx = np.cumsum(sizes)[:-1].tolist()
    return jnp.split(p, idx, axis=-1)

def short_conv(x, w):
    ch = x.shape[-1]
    return lax.conv_general_dilated(
        x, w[:, None, :], window_strides=(1,), padding=((A_CONV // 2, A_CONV // 2),),
        dimension_numbers=('NWC', 'WIO', 'NWC'), feature_group_count=ch)

def gdn_prep(aq, ak, av, ab, aa, conv_w, a_log, dt_bias):
    b, t, _ = aq.shape
    qkv = jax.nn.silu(short_conv(jnp.concatenate([aq, ak, av], axis=-1), conv_w)).astype(jnp.float32)
    q, k, v = jnp.split(qkv, [A_HEADS * A_DK, 2 * A_HEADS * A_DK], axis=-1)
    q = l2_norm(q.reshape(b, t, A_HEADS, A_DK)) * (A_DK ** -0.5)
    k = l2_norm(k.reshape(b, t, A_HEADS, A_DK))
    v = v.reshape(b, t, A_HEADS, A_DV)
    beta = jax.nn.sigmoid(ab.astype(jnp.float32).reshape(b, t, 2, A_HEADS))
    g = -jnp.exp(a_log.astype(jnp.float32)) * jax.nn.softplus(
        aa.astype(jnp.float32).reshape(b, t, 2, A_HEADS) + dt_bias.astype(jnp.float32))
    return q, k, v, beta, g

def gated_delta_chunked(q, k, v, beta, g, s0):
    b, t, h, _ = q.shape
    dv = v.shape[-1]
    n = t // A_CHUNK

    def to_chunks(a):
        a = a.reshape((b, n, A_CHUNK, h) + a.shape[3:])
        return jnp.moveaxis(a, (1, 3), (0, 2))

    qc, kc, vc, bc, gc = (to_chunks(a) for a in (q, k, v, beta, g))
    gcum = jnp.cumsum(gc, axis=-1)
    idx = jnp.arange(A_CHUNK)
    incl = idx[:, None] >= idx[None, :]
    strict = idx[:, None] > idx[None, :]
    diff = gcum[..., :, None] - gcum[..., None, :]
    decay_incl = jnp.where(incl, jnp.exp(jnp.where(incl, diff, 0.0)), 0.0)
    decay_strict = jnp.where(strict, decay_incl, 0.0)
    kb = kc * bc[..., None]
    l_mat = jnp.einsum('nbhid,nbhjd->nbhij', kb, kc) * decay_strict
    eye = jnp.eye(A_CHUNK, dtype=jnp.float32)
    rhs = jnp.concatenate([vc * bc[..., None], kb * jnp.exp(gcum)[..., None]], axis=-1)
    sol = lax.linalg.triangular_solve(eye + l_mat, rhs, left_side=True, lower=True,
                                      unit_diagonal=True)
    u, w = sol[..., :dv], sol[..., dv:]
    attn_intra = jnp.einsum('nbhid,nbhjd->nbhij', qc, kc) * decay_incl
    q_dec = qc * jnp.exp(gcum)[..., None]
    k_dec = kc * jnp.exp(gcum[..., -1:] - gcum)[..., None]
    g_last = jnp.exp(gcum[..., -1])

    def step(s, xs):
        u_n, w_n, a_n, qd_n, kd_n, gl_n = xs
        v_new = u_n - jnp.einsum('bhcd,bhde->bhce', w_n, s)
        o_n = jnp.einsum('bhcd,bhde->bhce', qd_n, s) + jnp.einsum('bhij,bhje->bhie', a_n, v_new)
        s = s * gl_n[..., None, None] + jnp.einsum('bhcd,bhce->bhde', kd_n, v_new)
        return s, o_n

    s_fin, o = lax.scan(step, s0, (u, w, attn_intra, q_dec, k_dec, g_last))
    o = jnp.moveaxis(o, (0, 2), (1, 3)).reshape(b, t, h, dv)
    return o, s_fin

def gdn_output(o, z, norm_w):
    b, t, _ = z.shape
    y = rms_norm(o, norm_w) * jax.nn.silu(z.astype(jnp.float32)).reshape(b, t, A_HEADS, A_DV)
    return y.reshape(b, t, A_W).astype(z.dtype)

def head_rms(a, heads, w):
    b, t, _ = a.shape
    return rms_norm(a.reshape(b, t, heads, -1), w)

def axial_rope_tables(t):
    rows = t // GRID_W
    row = jnp.repeat(jnp.arange(rows), GRID_W).astype(jnp.float32)
    col = jnp.tile(jnp.arange(GRID_W), rows).astype(jnp.float32)
    n_freq = B_HD // 4
    inv = ROPE_THETA ** (-jnp.arange(n_freq, dtype=jnp.float32) / n_freq)
    ang = jnp.concatenate([row[:, None] * inv, col[:, None] * inv], axis=-1)
    return jnp.cos(ang), jnp.sin(ang)

def axial_rope(x, cos, sin):
    xf = x.astype(jnp.float32)
    x1, x2 = xf[..., :B_HD // 2], xf[..., B_HD // 2:]
    c, s = cos[None, :, None, :], sin[None, :, None, :]
    return jnp.concatenate([x1 * c - x2 * s, x1 * s + x2 * c], axis=-1).astype(x.dtype)

def block_attention(q, k, v):
    b, tq, h, hd = q.shape
    grp = h // B_KV
    nb = tq // Q_BLOCK
    qb = q.reshape(b, nb, Q_BLOCK, B_KV, grp, hd).transpose(1, 0, 2, 3, 4, 5)
    scale = hd ** -0.5

    def one_block(qi):
        s = jnp.einsum('bqkgd,bskd->bkgqs', qi, k).astype(jnp.float32) * scale
        p = jax.nn.softmax(s, axis=-1).astype(v.dtype)
        return jnp.einsum('bkgqs,bskd->bqkgd', p, v)

    o = lax.map(one_block, qb)
    return o.transpose(1, 0, 2, 3, 4, 5).reshape(b, tq, h * hd)

def merge_branches(a_out, b_out, gate_logits, w_proj_a, w_proj_b, w_out):
    g_a, g_b = jnp.split(jax.nn.sigmoid(gate_logits), 2, axis=-1)
    return (g_a * (a_out @ w_proj_a) + g_b * (b_out @ w_proj_b)) @ w_out

def hybrid_layer(x, ctx, c, c_ctx, w_mod, b_mod, norm_w, w_in, conv_w, a_log, dt_bias,
                 a_norm_w, q_norm_w, k_norm_w, w_proj_a, w_proj_b, w_out, update_ctx):
    b, t, _ = x.shape
    shift, scale, gate = jnp.split((jax.nn.silu(c) @ w_mod + b_mod)[:, None, :], 3, axis=-1)
    shift_c, scale_c, gate_c = jnp.split(jax.nn.silu(c_ctx) @ w_mod + b_mod, 3, axis=-1)
    h = modulate(x, norm_w, shift, scale)
    hc = modulate(ctx, norm_w, shift_c, scale_c)
    aq, ak, av, az, ab, aa, bq, bk, bv, bz, br = split_in(h @ w_in)
    caq, cak, cav, caz, cab, caa, cbq, cbk, cbv, cbz, cbr = split_in(hc @ w_in)

    ql, kl, vl, betal, gl = gdn_prep(aq, ak, av, ab, aa, conv_w, a_log, dt_bias)
    qc, kc, vc, betac, gc = gdn_prep(caq, cak, cav, cab, caa, conv_w, a_log, dt_bias)
    s0 = jnp.zeros((b, A_HEADS, A_DK, A_DV), jnp.float32)
    oc_f, s_f = gated_delta_chunked(qc, kc, vc, betac[:, :, 0], gc[:, :, 0], s0)
    oc_b, s_b = gated_delta_chunked(_flip(qc), _flip(kc), _flip(vc),
                                    _flip(betac[:, :, 1]), _flip(gc[:, :, 1]), s0)
    ol_f, _ = gated_delta_chunked(ql, kl, vl, betal[:, :, 0], gl[:, :, 0], s_f)
    ol_b, _ = gated_delta_chunked(_flip(ql), _flip(kl), _flip(vl),
                                  _flip(betal[:, :, 1]), _flip(gl[:, :, 1]), s_b)
    a_lat = gdn_output(ol_f + _flip(ol_b), az, a_norm_w)

    cos, sin = axial_rope_tables(t)
    q_lat = axial_rope(head_rms(bq, B_HEADS, q_norm_w), cos, sin)
    k_lat = axial_rope(head_rms(bk, B_KV, k_norm_w), cos, sin)
    v_lat = bv.reshape(b, t, B_KV, B_HD)
    k_ctx = head_rms(cbk, B_KV, k_norm_w)
    v_ctx = cbv.reshape(b, -1, B_KV, B_HD)
    keys = jnp.concatenate([k_ctx, k_lat], axis=1)
    vals = jnp.concatenate([v_ctx, v_lat], axis=1)
    b_lat = block_attention(q_lat, keys, vals) * jax.nn.silu(bz)

    x_new = x + gate * merge_branches(a_lat, b_lat, br, w_proj_a, w_proj_b, w_out)
    if update_ctx:
        a_ctx = gdn_output(oc_f + _flip(oc_b), caz, a_norm_w)
        q_ctx = head_rms(cbq, B_HEADS, q_norm_w)
        b_ctx = block_attention(q_ctx, k_ctx, v_ctx) * jax.nn.silu(cbz)
        ctx = ctx + gate_c * merge_branches(a_ctx, b_ctx, cbr, w_proj_a, w_proj_b, w_out)
    return x_new, ctx

def setup_inputs(seed: int = 0) -> dict:
    key = jax.random.key(seed)
    ks = jax.random.split(key, 18)
    f32 = jnp.float32
    nrm = lambda k, shape, s: jax.random.normal(k, shape, f32) * s
    dt = jnp.exp(jax.random.uniform(ks[9], (DEPTH, 2, A_HEADS), f32,
                                    minval=float(np.log(1e-3)), maxval=float(np.log(1e-1))))
    return {
        'x': nrm(ks[0], (BATCH, SEQ, D_MODEL), 1.0),
        'c': nrm(ks[1], (BATCH, D_MODEL), 1.0),
        'ctx': nrm(ks[2], (BATCH, CTX_LEN, D_MODEL), 1.0),
        'c_ctx': nrm(ks[3], (D_MODEL,), 1.0),
        'w_mod': nrm(ks[4], (DEPTH, D_MODEL, 3 * D_MODEL), 0.5 * D_MODEL ** -0.5),
        'b_mod': nrm(ks[5], (DEPTH, 3 * D_MODEL), 0.01),
        'norm_w': 1.0 + nrm(ks[6], (DEPTH, D_MODEL), 0.02),
        'w_in': nrm(ks[7], (DEPTH, D_MODEL, IN_COLS), D_MODEL ** -0.5),
        'conv_w': nrm(ks[8], (DEPTH, A_CONV, CONV_CH), A_CONV ** -0.5),
        'a_log': jnp.log(jax.random.uniform(ks[10], (DEPTH, 2, A_HEADS), f32, minval=1.0, maxval=16.0)),
        'dt_bias': dt + jnp.log(-jnp.expm1(-dt)),
        'a_norm_w': 1.0 + nrm(ks[11], (DEPTH, A_DV), 0.02),
        'q_norm_w': 1.0 + nrm(ks[12], (DEPTH, B_HD), 0.02),
        'k_norm_w': 1.0 + nrm(ks[13], (DEPTH, B_HD), 0.02),
        'w_proj_a': nrm(ks[14], (DEPTH, A_W, D_MODEL), A_W ** -0.5),
        'w_proj_b': nrm(ks[15], (DEPTH, B_W, D_MODEL), B_W ** -0.5),
        'w_out': nrm(ks[16], (DEPTH, D_MODEL, D_MODEL), D_MODEL ** -0.5),
    }

def reference(x, c, ctx, c_ctx, w_mod, b_mod, norm_w, w_in, conv_w, a_log, dt_bias,
              a_norm_w, q_norm_w, k_norm_w, w_proj_a, w_proj_b, w_out):
    for layer in range(DEPTH):
        x, ctx = hybrid_layer(x, ctx, c, c_ctx, w_mod[layer], b_mod[layer], norm_w[layer],
                              w_in[layer], conv_w[layer], a_log[layer], dt_bias[layer],
                              a_norm_w[layer], q_norm_w[layer], k_norm_w[layer],
                              w_proj_a[layer], w_proj_b[layer], w_out[layer],
                              update_ctx=layer + 1 < DEPTH)
    return x


_drawn_inputs = setup_inputs


def setup_inputs(seed=0):
    import zlib

    import numpy as np

    out = dict(_drawn_inputs(seed))
    spreads = {}
    factors = {'ctx': 5.595,
     'c_ctx': 4.62,
     'b_mod': 8.0,
     'norm_w': 8.0,
     'a_log': 2.847,
     'a_norm_w': 8.0,
     'q_norm_w': 8.0,
     'k_norm_w': 8.0}
    for name, (base, spread) in spreads.items():
        noise = np.random.default_rng([zlib.crc32(name.encode()), seed]).standard_normal(out[name].shape)
        drawn = base * np.exp(spread * noise) if base else spread * noise
        out[name] = __import__('jax').numpy.asarray(drawn.astype(out[name].dtype))
    for name, factor in factors.items():
        out[name] = (out[name] * factor).astype(out[name].dtype)
    return out
```

```python
from contextlib import ExitStack

import numpy as np

import concourse.bass as bass
from concourse import mybir

P = 128
DM = 2048
SEQ = 512
CTX = 256
TOK = SEQ + CTX
HEADS = 8
CONV = 5
KV = 2
HD = 128
KT = DM // P
LT = SEQ // P
CT = CTX // P
NT = LT + CT
EPS = 1e-6
GRID_W = 64
ROPE_THETA = 10000.0

COL_AQ, COL_AK, COL_AV, COL_AZ = 0, 1024, 2048, 3072
COL_AB = 4096
COL_BQ, COL_BKV, COL_BZ, COL_BR = 4128, 5152, 5664, 6688

IDENT, LE, GE, GT, LT_, ONES, STAGE = 0, 128, 256, 384, 512, 640, 768
BLOCKS = [1, 2, 4, 8, 16, 32, 64]
NCONST = STAGE + len(BLOCKS) * 2 * 64


def shape_constants():
    a = np.arange(P)
    t, i = a[:, None], a[None, :]
    parts = [t == i, t <= i, t >= i, t > i, t < i, np.ones((P, P), bool)]
    for s in BLOCKS:
        block = a // s
        for backward in (0, 1):
            cols = a[(block % 2) == (0 if backward else 1)]
            want = cols // s + (1 if backward else -1)
            parts.append(block[:, None] == want[None, :])
    consts = np.concatenate(parts, axis=1).astype(np.float32)
    assert consts.shape == (P, NCONST)
    tok = np.arange(SEQ)
    inv = ROPE_THETA ** (-np.arange(HD // 4) / (HD // 4))
    ang = np.concatenate([(tok // GRID_W)[:, None] * inv, (tok % GRID_W)[:, None] * inv], axis=-1)
    rope = np.concatenate([np.cos(ang), np.sin(ang)], axis=1).astype(np.float32)
    return consts, rope


def projection_plan():
    groups, pieces = [], []

    def group(kind, col, width, per_piece, **more):
        g = dict(kind=kind, col=col, width=width, first=len(pieces), **more)
        for k0 in range(0, KT, per_piece):
            pieces.append(dict(g=len(groups), kind=kind, k0=k0, nk=per_piece, col=col, width=width))
        g["last"] = len(pieces) - 1
        groups.append(g)

    for what, col in (("k", COL_AK), ("v", COL_AV), ("q", COL_AQ)):
        for j in range(4):
            group("conv", col + 256 * j, 256, 4, what=what, pair=j)
    group("ab", COL_AB, 32, 16)
    group("bkv", COL_BKV, 512, 2)
    for first, col, n in ((0, COL_AZ, 4), (8, COL_BZ, 4), (16, COL_BR, 16)):
        for j in range(n):
            group("gate", col + 256 * j, 256, 4, row=first + 2 * j)
    for j in range(2):
        group("bq", COL_BQ + 512 * j, 512, 2, half=j)
    for j in range(8):
        for branch in (0, 1):
            g = dict(kind="merge", first=len(pieces), j=j, branch=branch)
            for k0 in (0, 4):
                pieces.append(dict(g=len(groups), kind="merge", k0=k0, nk=4, col=256 * j, width=256, branch=branch, j=j))
            g["last"] = len(pieces) - 1
            groups.append(g)
    for j in range(4):
        group("out", 512 * j, 512, 2, j=j)
    return groups, pieces


def scan_plan():
    pairs, slots = [], []
    fwd = [LT, LT + 1] + list(range(LT))
    bwd = [LT + 1, LT] + list(range(LT))[::-1]
    for step in range(NT):
        for half in range(2):
            lat, last = step >= CT, step == NT - 1
            pairs.append(dict(tiles=(fwd[step], bwd[step]), half=half, lat=lat, last=last, first=len(slots)))
            p = len(pairs) - 1
            kinds = [("decay", 0), ("gram", 0)] + [("qk", 0)] * lat
            for n in range(len(BLOCKS)):
                kinds += [("couple", n)] + [("correct", n)] * (n > 0) + [("flip", n)] * (n < len(BLOCKS) - 1)
            kinds += [("at", 0)] * lat + [("kt", 0)] * (not last) + [("ks", 0), ("z", 0)]
            kinds += [("qs", 0), ("az", 0)] * lat + [("kz", 0)] * (not last)
            slots += [dict(kind=k, n=n, pair=p, i=len(slots) + m) for m, (k, n) in enumerate(kinds)]
            pairs[-1]["end"] = len(slots)
    return pairs, slots


ON_SCALAR = ("decay", "flip", "at", "kt", "z")


def build(nc, x, c, ctx, c_ctx, w_mod, b_mod, norm_w, w_in, conv_w, a_log, dt_bias, a_norm_w, q_norm_w,
          k_norm_w, w_proj_a, w_proj_b, w_out, consts_in, rope_in, out):
    f32, f32r = mybir.dt.float32, mybir.dt.float32r
    ALU, ACT, AX = mybir.AluOpType, mybir.ActivationFunctionType, mybir.AxisListType
    GROUPS, PIECES = projection_plan()
    PAIRS, SLOTS = scan_plan()
    NP = len(PIECES)
    CONVS = [g for g in GROUPS if g["kind"] == "conv"]
    ITEMS = [dict(what=g["what"], head=2 * g["pair"] + j, g=gi, j=j) for gi, g in enumerate(CONVS) for j in (0, 1)]
    G_AB = len(CONVS)
    G_BKV = G_AB + 1
    GATES = [gi for gi, g in enumerate(GROUPS) if g["kind"] == "gate"]
    BQS = [gi for gi, g in enumerate(GROUPS) if g["kind"] == "bq"]
    OUTS = [gi for gi, g in enumerate(GROUPS) if g["kind"] == "out"]
    N_GATE0 = GROUPS[GATES[0]]["first"]
    N_BQ0 = GROUPS[BQS[0]]["first"]
    N_MERGE0 = GROUPS[BQS[-1]]["last"] + 1
    N_OUT0 = GROUPS[OUTS[0]]["first"]
    assert len(SLOTS) <= 4 * (N_BQ0 - N_GATE0)

    base = 16512
    A_CONST, A_SMALL, A_RING = 0, 6656, 11008
    A_H = A_RING + 24576
    A_C = A_H + 65536
    A_G = A_C + 32768
    A_T = A_G + 65536

    def at(name, shape, off, dt=f32):
        return nc.alloc_sbuf_tensor_at(name, shape, dt, offset=base + off)

    consts = at("consts", [P, NCONST], A_CONST)
    small_top = [A_SMALL]

    def small(name, shape):
        n = int(np.prod(shape[1:])) * 4
        n = (n + 31) // 32 * 32
        t = at(name, shape, small_top[0])
        small_top[0] += n
        assert small_top[0] <= A_RING, small_top[0] - A_RING
        return t

    cols = small("cols", [P, 97])
    convw = small("convw", [P, 120])
    GATE = small("gate_cols", [P, KT])
    stat = small("stat", [P, 16])
    beta = small("beta", [P, NT * 16])
    betar = beta
    off_wrow = small_top[0]
    gdec = small("gdec", [P, NT * 16])
    crow = small("crow", [P, NT * 16])
    ngr = small("ngr", [P, NT * 16])
    off_dec = small_top[0]
    DEC = small("decays", [P, NT * 2, 3, 8])
    rk = small("rk", [P, 48])
    rq = small("rq", [P, 32])
    alog = small("alog", [P, 16])
    dtb = small("dt_bias_rows", [P, 16])
    silu_cg = small("silu_c_gate", [P, KT])
    wrow = at("w_rows", [P, 256], off_wrow)
    ssq_o = at("ssq_o", [P, 32], off_dec)
    ssq_a = at("ssq_a", [P, 44], off_dec + 128)
    nmax = at("neg_max", [P, 32], off_dec + 320)
    rsum = at("row_sum", [P, 32], off_dec + 448)

    raw = [at(f"w_raw{i}", [P, 1024], A_RING + 4096 * i) for i in range(2)]
    whi = [at(f"w_hi{i}", [P, 1024], A_RING + 8192 + 4096 * i, f32r) for i in range(2)]
    wlo = [at(f"w_lo{i}", [P, 1024], A_RING + 16384 + 4096 * i, f32r) for i in range(2)]
    modr = [at(f"mod_w{i}", [P, 8, 256], A_RING + 8192 * i) for i in range(3)]
    h_hi = at("h_hi", [P, KT, SEQ], A_H, f32r)
    h_lo = at("h_lo", [P, KT, SEQ], A_H + 32768, f32r)
    hc_hi = at("hc_hi", [P, KT, CTX], A_C, f32r)
    hc_lo = at("hc_lo", [P, KT, CTX], A_C + 16384, f32r)
    xnT = at("xnT", [P, KT, TOK], A_G)
    xt = [at(f"x_rows{i}", [P, DM], A_G + 49152 + 8192 * i) for i in range(2)]
    junk = at("junk", [P, DM], A_T)
    rows = at("rows", [97, P], A_T + 8192)
    crows = at("conv_rows", [120, P], A_T + 8704)
    modv = at("mod_vec", [P, 2, KT, 2], A_T + 9216)
    sc2 = at("silu_c", [P, KT, 2], A_T + 9472)
    G_Q, G_K, G_V, G_O = A_G, A_G + 16384, A_G + 32768, A_G + 49152
    qT = at("qT", [P, HEADS, SEQ], G_Q)
    kTl = at("kT_latent", [P, HEADS, SEQ], G_K)
    vl = at("v_latent", [P, LT, 1024], G_V)
    kTc = at("kT_context", [P, HEADS, CTX], G_O)
    vc = at("v_context", [P, CT, 1024], G_O + 8192)
    RAWW = 776
    rawc = [at(f"conv_in{i}", [P, RAWW], A_T + 4 * RAWW * i) for i in range(2)]
    acc = [at(f"conv_acc{i}", [P, 772], A_T + 8 * RAWW + 3104 * i) for i in range(2)]
    ab_t = [at(f"logit_tmp{i}", [P, NT * 16], A_T + 8 * RAWW + 384 * i) for i in range(5)]
    kvst = [at(f"kv_stage{i}", [P, 512], A_T + 2048 * i) for i in range(2)]
    GM, DD, LL, XX, YY, RR, ZZ = ([at(f"{n}{b}", [P, 4, P], A_C + 14336 * b + 2048 * o) for b in (0, 1)] for o, n in
                                  enumerate(("decay_lhs", "decay", "L", "inv", "invT", "resid", "zval")))
    PM = [at(f"couple{b}", [P, 4, 64], A_C + 28672 + 1024 * b) for b in (0, 1)]
    SS = at("states", [P, 2, HEADS, P], A_T)
    gst = [at(f"gate_stage{i}", [P, 512], A_T + 8192 + 2048 * i) for i in range(2)]
    o_acc = at("o_acc", [P, LT, 1024], G_O)
    bqr = at("bq_rows", [P, LT, 1024], A_C)
    modg = [at(f"mod_gate_w{i}", [P, 8, 256], A_C + 16384 + 8192 * i) for i in range(2)]
    qhT = at("att_qT", [P, HEADS, SEQ], A_H)
    khT = at("att_kT", [P, KV, TOK], A_H + 16384)
    kvr = at("kv_rows", [P, NT, 512], A_H + 22528)
    PTt = at("probsT", [P, NT, SEQ], A_H + 34816)
    atmp = [at(f"a_tmp{i}", [P, 512], A_H + 34816 + 2048 * i) for i in range(2)]
    probs = [at(f"probs{i}", [P, TOK], A_H + 47104 + 3072 * i) for i in range(2)]
    cs = at("cos_sin", [P, LT, 128], A_H + 53248)
    qtab = at("q_tab", [P, LT, 256], A_H + 55296)
    ktab = at("k_tab", [P, LT, 256], A_H + 59392)
    btmp = at("b_tmp", [P, 512], A_H + 63488)
    rt = [at(f"rope{i}", [P, 8, 64], A_T + 2048 * i) for i in range(4)]
    zst = [at(f"z_stage{i}", [P, 512], A_T + 8192 + 2048 * i) for i in range(2)]
    a_hi = at("a_hi", [P, 8, SEQ], A_G, f32r)
    a_lo = at("a_lo", [P, 8, SEQ], A_G + 16384, f32r)
    b_hi = at("b_hi", [P, 8, SEQ], A_G + 32768, f32r)
    b_lo = at("b_lo", [P, 8, SEQ], A_G + 49152, f32r)
    m_hi = at("m_hi", [P, KT, SEQ], A_H, f32r)
    m_lo = at("m_lo", [P, KT, SEQ], A_H + 32768, f32r)
    gsig = [at(f"gates{i}", [P, 2, 512], A_C + 4096 * i) for i in range(4)]
    mtmp = [at(f"m_tmp{i}", [P, 512], A_T + 2048 * i) for i in range(4)]
    gcb = [at(f"gate_lhs{i}", [P, P], A_T + 8192 + 512 * i) for i in range(4)]
    grow = at("gate_rows", [P, DM], A_G)
    xr = at("x_again", [P, LT, DM], A_G + 8192)
    ost = [at(f"out_stage{i}", [P, 512], A_G + 40960 + 2048 * i) for i in range(4)]

    gate_scr = nc.dram_tensor("gate_scratch", [48, P, SEQ], f32, kind="Internal").ap()
    kv_scr = nc.dram_tensor("kv_scratch", [NT, P, 512], f32, kind="Internal").ap()

    with ExitStack() as stack:
        PS = stack.enter_context(nc.psum_tensor("psum", [P, 8 * 512], f32))
        sems = {}

        def S(name):
            if name not in sems:
                sems[name] = stack.enter_context(nc.semaphore(name))
            return sems[name]

        def bank(b, n=512, off=0):
            return PS[:, b * 512 + off:b * 512 + off + n]

        def bank4(b, w=128):
            return PS[:, b * 512:b * 512 + 4 * w].rearrange("p (u n) -> p u n", u=4)

        ident = consts[:, IDENT:IDENT + P]
        ones = consts[:, ONES:ONES + P]

        def odd(tile4, s, d):
            e = 0 if d else 1
            return tile4.rearrange("p u (b e s) -> p u b e s", e=2, s=s)[:, :, :, e, :]

        def odd1(t, s, d, e=None):
            e = (0 if d else 1) if e is None else e
            return t.rearrange("p (b e s) -> p b e s", e=2, s=s)[:, :, e, :]

        def kT_of(head, tile):
            if tile < LT:
                return kTl[:, head, tile * P:(tile + 1) * P]
            return kTc[:, head, (tile - LT) * P:(tile - LT + 1) * P]

        def v_of(head, tile):
            t = vl[:, tile] if tile < LT else vc[:, tile - LT]
            return t[:, head * P:(head + 1) * P]

        def unit_col(d, tile, head):
            return tile * 16 + d * 8 + head

        def src_of(p):
            w = {"merge": (w_proj_a, w_proj_b)[p.get("branch", 0)], "out": w_out}.get(p["kind"], w_in)
            return w[0, p["k0"] * P:(p["k0"] + p["nk"]) * P, p["col"]:p["col"] + p["width"]].rearrange(
                "(t p) n -> p t n", p=P)

        def part(t, p):
            return t[:, 0:p["nk"] * p["width"]]

        def part3(t, p):
            return part(t, p).rearrange("p (t n) -> p t n", n=p["width"])

        def accs_free_needed(eng, gi):
            g = GROUPS[gi]
            if g["kind"] == "conv" and gi >= 2:
                eng.wait_ge(S("conv_raw"), 2 * (gi - 1))
            if g["kind"] == "ab":
                eng.wait_ge(S("v_evac"), 8)
            if g["kind"] == "bkv":
                eng.wait_ge(S("conv_raw"), 24)
            if g["kind"] == "gate":
                k = GATES.index(gi)
                if k < 2:
                    eng.wait_ge(S("kv_evac"), NT)
                else:
                    eng.wait_ge(S("gate_evac"), 2 * (k - 1))
            if g["kind"] == "bq":
                k = BQS.index(gi)
                if k == 0:
                    eng.wait_ge(S("gate_evac"), 2 * len(GATES))
                else:
                    eng.wait_ge(S("bq_evac"), 4)
            if g["kind"] == "merge" and g["branch"] == 0:
                if g["j"] >= 2:
                    eng.wait_ge(S("m_psum"), 2 * (g["j"] - 1))
            if g["kind"] == "out":
                k = g["j"]
                if k < 2:
                    eng.wait_ge(S("grow_evac"), 4)
                    eng.wait_ge(S("m_psum"), 16)
                else:
                    eng.wait_ge(S("out_psum"), 4 * (k - 1))

        block = stack.enter_context(nc.Block())

        @block.sync
        def _(sp):
            sp.dma_start(consts[:], consts_in).then_inc(S("const_in"), 16)
            for r0, n, src in ((0, 16, c[0, :]), (16, 16, c_ctx), (32, 16, norm_w[0, :]), (48, 48, b_mod[0, :]),
                               (96, 1, a_norm_w[0, :])):
                sp.dma_start(rows[r0:r0 + n, :], src.rearrange("(t p) -> t p", p=P)).then_inc(S("rows_in"), 16)
            sp.dma_start(crows[:], conv_w[0].rearrange("t (c p) -> (t c) p", p=P)).then_inc(S("rows_in"), 16)
            for m in range(32):
                j, scale, half = m // 4, (m // 2) % 2, m % 2
                if m >= 3:
                    sp.wait_ge(S("mod_used"), m - 2)
                col = scale * DM + 256 * j
                sp.dma_start(modr[m % 3][:], w_mod[0, half * 1024:(half + 1) * 1024, col:col + 256].rearrange(
                    "(t p) n -> p t n", p=P)).then_inc(S(f"mod_in{m % 3}"), 16)
            sp.wait_ge(S("mod_used"), 32)
            for n, p in enumerate(PIECES):
                if n >= 2:
                    sp.wait_ge(S("w_hi"), n - 1)
                    sp.wait_ge(S("w_lo"), n - 1)
                sp.dma_start(part3(raw[n % 2], p), src_of(p)).then_inc(S(f"w_in{n % 2}"), 16)
                if N_BQ0 <= n < N_MERGE0:
                    m = n - N_BQ0
                    if m == 0:
                        sp.wait_ge(S("gd0"), len(SLOTS))
                        sp.wait_ge(S("gd1"), len(SLOTS))
                    if m >= 2:
                        sp.wait_ge(S("modg_used"), m - 1)
                    sp.dma_start(modg[m % 2][:], w_mod[0, (m % 2) * 1024:(m % 2 + 1) * 1024,
                                                       2 * DM + 256 * (m // 2):2 * DM + 256 * (m // 2 + 1)].rearrange(
                        "(t p) n -> p t n", p=P)).then_inc(S(f"modg_in{m % 2}"), 16)
            for i in range(4):
                sp.wait_ge(S(f"out_dma{i}"), 16 * 4)

        @block.gpsimd
        def _(pool):
            for t in range(NT):
                if t >= 2:
                    pool.wait_ge(S("xt_ready"), 4 * (t - 1))
                src = x[0, t * P:(t + 1) * P, :] if t < LT else ctx[0, (t - LT) * P:(t - LT + 1) * P, :]
                pool.dma_start(xt[t % 2][:], src).then_inc(S(f"x_in{t % 2}"), 16)
            pool.dma_start(alog[:], a_log[0].rearrange("d h -> (d h)").partition_broadcast(P)).then_inc(S("alog_in"), 16)
            pool.dma_start(dtb[:], dt_bias[0].rearrange("d h -> (d h)").partition_broadcast(P)).then_inc(S("alog_in"), 16)
            pool.wait_ge(S("h_lo"), 2 * KT)
            for i in range(2):
                pool.memset(rawc[i][:], 0.0).then_inc(S("pads"), 1)
            pool.wait_ge(S("prep"), 1)
            for i in range(2):
                pool.wait_ge(S(f"kv_spill{i}"), 16 * 3)
            pool.wait_ge(S("w_used"), N_GATE0)
            pool.memset(SS[:], 0.0).then_inc(S("states0"), 1)
            for pi, pr in enumerate(PAIRS):
                for d in (0, 1):
                    for u in range(4):
                        col = unit_col(d, pr["tiles"][d], 4 * pr["half"] + u)
                        m = (LE, GE)[d]
                        ins = pool.tensor_scalar(GM[d][:, u, :], consts[:, m:m + P], gdec[:, col:col + 1], None, ALU.mult)
                    ins.then_inc(S(f"gm{d}"), 1)
                if pr["lat"] and not PAIRS[pi - 1]["lat"]:
                    for d in (0, 1):
                        pool.wait_ge(S(f"gd{d}"), pr["first"])
                    pool.memset(o_acc[:], 0.0).then_inc(S("oacc0"), 1)
                for d in (0, 1):
                    pool.wait_ge(S(f"gd{d}"), pr["first"] + 1)
                    m = (GE, LE)[d]
                    pool.tensor_tensor(DD[d][:], DD[d][:], consts[:, m:m + P].unsqueeze(1).to_broadcast([P, 4, P]),
                                       ALU.mult).then_inc(S(f"dmask{d}"), 1)

            for d in (0, 1):
                pool.wait_ge(S(f"gd{d}"), len(SLOTS))
            pool.dma_start(wrow[:, 0:P], q_norm_w[0].partition_broadcast(P)).then_inc(S("tab_in"), 16)
            pool.dma_start(wrow[:, P:2 * P], k_norm_w[0].partition_broadcast(P)).then_inc(S("tab_in"), 16)
            for i in range(2):
                pool.wait_ge(S(f"gate_spill{i}"), 16 * 24)

            def z_load(k):
                if k >= 2:
                    if k - 2 < HEADS:
                        pool.wait_ge(S("a_tmp"), k - 1)
                    else:
                        pool.wait_ge(S("b_tmp"), k - 1 - HEADS)
                pool.dma_start(zst[k % 2][:], gate_scr[k]).then_inc(S(f"z_in{k % 2}"), 16)

            z_load(0)
            z_load(1)
            pool.wait_ge(S("w_used"), N_MERGE0)
            for t in range(NT):
                pool.dma_start(kvr[:, t, :], kv_scr[t]).then_inc(S("kv_in"), 16)
            pool.dma_start(cs[:], rope_in.rearrange("(t p) n -> p t n", p=P)).then_inc(S("tab_in"), 16)
            for k in range(2, 2 * HEADS):
                z_load(k)
                if k == HEADS:
                    pool.wait_ge(S("qt_ready"), HEADS)
                    for m in range(4):
                        for r in (0, 1):
                            pool.dma_start(gsig[m][:, r, :], gate_scr[16 + 16 * r + m]).then_inc(S(f"gates_in{m}"), 16)
            for m in range(4, KT):
                pool.wait_ge(S("m_psum"), m - 3)
                for r in (0, 1):
                    pool.dma_start(gsig[m % 4][:, r, :], gate_scr[16 + 16 * r + m]).then_inc(S(f"gates_in{m % 4}"), 16)
            pool.wait_ge(S("w_used"), N_OUT0)
            for t in range(LT):
                pool.dma_start(xr[:, t, :], x[0, t * P:(t + 1) * P, :]).then_inc(S("x_again"), 16)
            for j in range(4):
                for t in range(LT):
                    pool.wait_ge(S("out_ready"), 4 * j + t + 1)
                    pool.dma_start(out[0, t * P:(t + 1) * P, 512 * j:512 * j + 512], ost[t][:]).then_inc(
                        S(f"out_dma{t}"), 16)

        @block.scalar
        def _(act):
            link = [0]

            def ln(ins):
                link[0] += 1
                ins.then_inc(S("act_chain"), 1)
                act.wait_ge(S("act_chain"), link[0])

            def hi_part(n):
                if n >= NP:
                    return
                act.wait_ge(S(f"w_in{n % 2}"), 16 * (n // 2 + 1))
                if n >= 2:
                    act.wait_ge(S("w_used"), n - 1)
                p = PIECES[n]
                act.activation(part(whi[n % 2], p), part(raw[n % 2], p), ACT.Copy).then_inc(S("w_hi"), 1)

            act.wait_ge(S("cols"), 2)
            act.activation(sc2[:].rearrange("p k v -> p v k"), cols[:, 0:32].rearrange("p (v k) -> p v k", v=2),
                           ACT.Silu).then_inc(S("silu_c"), 1)
            act.activation(silu_cg[:], cols[:, 0:KT], ACT.Silu).then_inc(S("silu_cg"), 1)
            for t in range(NT):
                act.wait_ge(S(f"x_in{t % 2}"), 16 * (t // 2 + 1))
                if t > 0:
                    act.wait_ge(S("x_ssq"), t)
                act.activation(junk[:], xt[t % 2][:], ACT.Square, accum_out=stat[:, t:t + 1]).then_inc(S("x_ssq"), 1)
                act.wait_ge(S("x_var"), t + 1)
                act.activation(stat[:, 8 + t:9 + t], stat[:, t:t + 1], ACT.Sqrt).then_inc(S("x_std"), 1)
                for q4 in (1, 3):
                    n = 4 * t + q4
                    act.wait_ge(S("xt_ready"), n + 1)
                    act.activation(xnT[:, 4 * q4:4 * q4 + 4, t * P:(t + 1) * P], bank4(n % 4), ACT.Copy).then_inc(
                        S("xt_act"), 1)
            for k in range(KT):
                act.wait_ge(S("h_ready"), k + 1)
                act.activation(h_hi[:, k, :], xnT[:, k, 0:SEQ], ACT.Copy)
                act.activation(hc_hi[:, k, :], xnT[:, k, SEQ:TOK], ACT.Copy).then_inc(S("h_hi"), 1)

            def conv_raw(ci):
                it = ITEMS[ci]
                g = GROUPS[it["g"]]
                act.wait_ge(S("w_used"), g["last"] + 1)
                if ci == 0:
                    act.wait_ge(S("pads"), 2)
                if ci >= 2:
                    act.wait_ge(S("conv_done"), ci - 1)
                b0 = 3 * (it["g"] % 2)
                lat = act.activation(rawc[ci % 2][:, 2:2 + SEQ], bank(b0 + it["j"]), ACT.Copy)
                if it["what"] == "q":
                    lat.then_inc(S("conv_raw"), 1)
                else:
                    act.activation(rawc[ci % 2][:, 518:774], bank(b0 + 2, 256, 256 * it["j"]), ACT.Copy).then_inc(
                        S("conv_raw"), 1)

            def conv_silu(ci):
                it = ITEMS[ci]
                act.wait_ge(S("conv_done"), ci + 1)
                a = acc[ci % 2]
                if it["what"] == "v":
                    act.activation(a[:], a[:], ACT.Silu).then_inc(S("item_ready"), 1)
                    return
                h = it["head"]
                dst = qT if it["what"] == "q" else kTl
                ln(act.activation(dst[:, h, :], a[:, 0:SEQ], ACT.Silu))
                if it["what"] == "k":
                    ln(act.activation(kTc[:, h, :], a[:, 516:772], ACT.Silu))
                    ln(act.activation(a[:, 516:772], kTc[:, h, :], ACT.Square))
                act.activation(a[:, 0:SEQ], dst[:, h, :], ACT.Square).then_inc(S("item_ready"), 1)

            def gdn(slot):
                k, n, pr = slot["kind"], slot["n"], PAIRS[slot["pair"]]
                for d in (0, 1):
                    ps = bank4(4 + 2 * d + slot["i"] % 2)
                    done = S(f"gd{d}")
                    if k == "correct" and n == len(BLOCKS) - 1:
                        act.wait_ge(S(f"gy{d}"), slot["pair"] + 1)
                        for u in range(4):
                            col = unit_col(d, pr["tiles"][d], 4 * pr["half"] + u)
                            ins = act.activation(XX[d][:, u, :], YY[d][:, u, :], ACT.Copy, scale=betar[:, col:col + 1])
                        ins.then_inc(done, 1)
                        continue
                    act.wait_ge(S(f"gp{d}"), slot["i"] + 1)
                    if k == "decay":
                        act.activation(DD[d][:], ps, ACT.Exp).then_inc(done, 1)
                    elif k == "flip":
                        act.activation(XX[d][:], ps, ACT.Copy).then_inc(done, 1)
                    elif k == "at":
                        act.activation(YY[d][:], ps, ACT.Copy).then_inc(done, 1)
                    elif k == "z":
                        act.activation(ZZ[d][:], ps, ACT.Copy).then_inc(done, 1)
                    elif k == "kt":
                        for u in range(4):
                            h, tile = 4 * pr["half"] + u, pr["tiles"][d]
                            ins = act.activation(LL[d][:, u, :], ps[:, u, :], ACT.Copy,
                                                 scale=DEC[:, tile * 2 + d, 1, h:h + 1])
                        ins.then_inc(done, 1)

            def bq_rows(j):
                act.wait_ge(S("w_used"), GROUPS[BQS[j]]["last"] + 1)
                for d in (0, 1):
                    act.wait_ge(S(f"gd{d}"), len(SLOTS))
                for t in range(LT):
                    act.activation(bqr[:, t, 512 * j:512 * j + 512], bank(t), ACT.Copy).then_inc(S("bq_evac"), 1)

            spills = [0]
            hi_part(0)
            for n in range(N_MERGE0):
                p = PIECES[n]
                hi_part(n + 1)
                for gi, g in enumerate(CONVS):
                    e = n - g["last"]
                    if e == 1:
                        conv_raw(2 * gi)
                        conv_raw(2 * gi + 1)
                    if e in (2, 3):
                        conv_silu(2 * gi + e - 2)
                if n == GROUPS[G_BKV]["first"] + 4:
                    act.wait_ge(S("w_used"), GROUPS[G_AB]["last"] + 1)
                    ab = bank(6, NT * 32).rearrange("p (t c) -> p t c", t=NT)
                    act.activation(beta[:].rearrange("p (t c) -> p t c", t=NT), ab[:, :, 0:16], ACT.Sigmoid).then_inc(
                        S("beta"), 1)
                    act.wait_ge(S("negabs"), 1)
                    ln(act.activation(ab_t[1][:], ab_t[1][:], ACT.Exp))
                    ln(act.activation(ab_t[2][:], ab_t[1][:], ACT.Ln, bias=1.0))
                    act.wait_ge(S("alog_in"), 32)
                    act.activation(alog[:], alog[:], ACT.Exp).then_inc(S("ab_exp"), 1)
                    act.wait_ge(S("ssq_eps"), 1)
                    ln(act.activation(rk[:], rk[:], ACT.Sqrt))
                    act.activation(rq[:], rq[:], ACT.Sqrt).then_inc(S("ssq_std"), 1)
                    act.wait_ge(S("cum"), 1)
                    act.activation(DEC[:].rearrange("p a b c -> p (a b c)"), bank(6, NT * 2 * 24), ACT.Exp).then_inc(
                        S("decays"), 1)
                if n == N_GATE0:
                    g = GROUPS[G_BKV]
                    for t in range(NT):
                        if t == 0:
                            act.wait_ge(S("w_used"), g["last"] + 1)
                            act.wait_ge(S("conv_done"), 24)
                        if t >= 2:
                            act.wait_ge(S(f"kv_spill{t % 2}"), 16 * (t // 2))
                        act.activation(kvst[t % 2][:], bank(t), ACT.Copy).then_inc(S("kv_evac"), 1)
                        act.wait_ge(S("kv_evac"), t + 1)
                        act.dma_start(kv_scr[t], kvst[t % 2][:]).then_inc(S(f"kv_spill{t % 2}"), 16)
                    act.wait_ge(S("item_pe"), 24)
                for q in range(4):
                    if N_GATE0 <= n < N_BQ0:
                        i = 4 * (n - N_GATE0) + q
                        if i < len(SLOTS):
                            s = SLOTS[i]
                            if s["kind"] in ON_SCALAR or (s["kind"] == "correct" and s["n"] == len(BLOCKS) - 1):
                                gdn(s)
                    pg = PIECES[n - 1]["g"] if n else 0
                    if q in (0, 2) and n and GROUPS[pg]["kind"] == "gate" and n - 1 == GROUPS[pg]["last"]:
                        j = q // 2
                        k = spills[0]
                        spills[0] += 1
                        row = GROUPS[pg]["row"] + j
                        if j == 0:
                            act.wait_ge(S("w_used"), n)
                        if k >= 2:
                            act.wait_ge(S(f"gate_spill{k % 2}"), 16 * (k // 2))
                        act.activation(gst[k % 2][:], bank(2 * (GATES.index(pg) % 2) + j),
                                       ACT.Silu if row < 16 else ACT.Sigmoid).then_inc(S("gate_evac"), 1)
                        act.wait_ge(S("gate_evac"), k + 1)
                        act.dma_start(gate_scr[row], gst[k % 2][:]).then_inc(S(f"gate_spill{k % 2}"), 16)
                if n - 1 == GROUPS[BQS[0]]["last"]:
                    bq_rows(0)
            bq_rows(1)
            act.wait_ge(S("gd1"), len(SLOTS))
            act.wait_ge(S("gd0"), len(SLOTS))
            for t in range(LT):
                for h in range(HEADS):
                    if t or h:
                        act.wait_ge(S("o_ssq"), t * 8 + h)
                    act.activation(probs[0][:, 0:P], o_acc[:, t, h * P:(h + 1) * P], ACT.Square,
                                   accum_out=ssq_o[:, t * 8 + h:t * 8 + h + 1]).then_inc(S("o_ssq"), 1)
            act.wait_ge(S("o_var"), 1)
            act.activation(ssq_o[:], ssq_o[:], ACT.Sqrt).then_inc(S("o_std"), 1)
            for i in range(44):
                if i < 32:
                    t, h = divmod(i, 8)
                    src = bqr[:, t, h * P:(h + 1) * P]
                else:
                    if i == 32:
                        act.wait_ge(S("kv_in"), 16 * NT)
                    t, h = divmod(i - 32, 2)
                    src = kvr[:, t, h * P:(h + 1) * P]
                if i:
                    act.wait_ge(S("qk_ssq"), i)
                act.activation(probs[0][:, 0:P], src, ACT.Square, accum_out=ssq_a[:, i:i + 1]).then_inc(S("qk_ssq"), 1)
            for h in range(HEADS):
                act.wait_ge(S("a_tmp"), h + 1)
                act.activation(a_hi[:, h, :], atmp[h % 2][:], ACT.Copy).then_inc(S("a_hi"), 1)
            act.wait_ge(S("qk_var"), 1)
            act.activation(ssq_a[:], ssq_a[:], ACT.Sqrt).then_inc(S("qk_std"), 1)
            for h in range(HEADS):
                act.wait_ge(S("qt_ready"), h + 1)
                act.activation(qhT[:, h, :], bank(h % 4), ACT.Copy).then_inc(S("qt_evac"), 1)
            for kv in range(KV):
                act.wait_ge(S("kt_ready"), kv + 1)
                act.activation(khT[:, kv, :], PS[:, (4 + 2 * kv) * 512:(4 + 2 * kv) * 512 + TOK], ACT.Copy).then_inc(
                    S("kt_evac"), 1)

            def att_exp(i):
                act.wait_ge(S("negmax"), i + 1)
                if i >= 2:
                    act.wait_ge(S("pt_ready"), i - 1)
                if i == 0:
                    act.wait_ge(S("qk_ssq"), 44)
                act.activation(probs[i % 2][:], PS[:, (i % 2) * 1024:(i % 2) * 1024 + TOK], ACT.Exp,
                               bias=nmax[:, i:i + 1], scale=HD ** -0.5, accum_out=rsum[:, i:i + 1]).then_inc(
                    S("exp_done"), 1)

            att_exp(0)
            for i in range(32):
                if i < 31:
                    att_exp(i + 1)
                h, qt = divmod(i, 4)
                if qt == 0 and h >= 1:
                    act.wait_ge(S("pv_done"), h)
                if i == 0:
                    act.wait_ge(S("a_lo"), HEADS)
                act.wait_ge(S("pt_ready"), i + 1)
                act.activation(PTt[:, :, qt * P:(qt + 1) * P],
                               PS[:, 2048:2048 + TOK].rearrange("p (t n) -> p t n", t=NT), ACT.Copy).then_inc(
                    S("pt_evac"), 1)
                if qt == 1 and h >= 1:
                    act.wait_ge(S("b_tmp"), h)
                    act.activation(b_hi[:, h - 1, :], btmp[:], ACT.Copy).then_inc(S("b_hi"), 1)
            act.wait_ge(S("b_tmp"), HEADS)
            act.activation(b_hi[:, HEADS - 1, :], btmp[:], ACT.Copy).then_inc(S("b_hi"), 1)
            for n in range(N_MERGE0, NP):
                hi_part(n + 1)
                for j in (n - N_MERGE0 - 4,):
                    if j >= 0 and j % 4 == 0 and j // 4 < 8:
                        for jj in (0, 1):
                            m = 2 * (j // 4) + jj
                            act.wait_ge(S("m_tmp"), m + 1)
                            act.activation(m_hi[:, m, :], mtmp[2 * (m % 2)][:], ACT.Copy).then_inc(S("m_hi"), 1)

        @block.vector
        def _(dve):
            link = [0]

            def ln(ins):
                link[0] += 1
                ins.then_inc(S("dve_chain"), 1)
                dve.wait_ge(S("dve_chain"), link[0])

            def lo_part(n):
                if n >= NP:
                    return
                dve.wait_ge(S("w_hi"), n + 1)
                p = PIECES[n]
                dve.tensor_tensor(part(wlo[n % 2], p), part(raw[n % 2], p), part(whi[n % 2], p).bitcast(f32),
                                  ALU.subtract).then_inc(S("w_lo"), 1)

            dve.wait_ge(S("rowsT"), 2)
            dve.tensor_copy(cols[:], bank(7, 97)).then_inc(S("cols"), 1)
            dve.tensor_copy(convw[:], bank(6, 120)).then_inc(S("cols"), 1)
            for t in range(NT):
                dve.wait_ge(S("x_ssq"), t + 1)
                dve.tensor_scalar(stat[:, t:t + 1], stat[:, t:t + 1], 1.0 / DM, EPS, ALU.mult, ALU.add).then_inc(
                    S("x_var"), 1)
                dve.wait_ge(S("x_std"), t + 1)
                ln(dve.reciprocal(stat[:, 8 + t:9 + t], stat[:, 8 + t:9 + t]))
                dve.tensor_scalar(xt[t % 2][:], xt[t % 2][:], stat[:, 8 + t:9 + t], None, ALU.mult).then_inc(
                    S("xn"), 1)
                for q4 in (0, 2):
                    n = 4 * t + q4
                    dve.wait_ge(S("xt_ready"), n + 1)
                    dve.tensor_copy(xnT[:, 4 * q4:4 * q4 + 4, t * P:(t + 1) * P], bank4(n % 4)).then_inc(
                        S("xt_dve"), 1)
            dve.wait_ge(S("xt_act"), 2 * NT)
            dve.wait_ge(S("xt_dve"), 2 * NT)
            for g in range(16):
                j, scale = g // 2, g % 2
                dve.wait_ge(S("mod_used"), 2 * (g + 1))
                for ch in (0, 1):
                    k = 2 * j + ch
                    b = cols[:, 48 + 16 * scale + k:49 + 16 * scale + k]
                    src = bank(4 + 2 * (g % 2) + ch, 2)
                    if scale:
                        ins = dve.tensor_scalar(modv[:, 1, k, :], src, b, 1.0, ALU.add, ALU.add)
                    else:
                        ins = dve.tensor_scalar(modv[:, 0, k, :], src, b, None, ALU.add)
                ins.then_inc(S("mod_evac"), 1)
                if scale:
                    dve.wait_ge(S("mod_evac"), g + 1)
                    for ch in (0, 1):
                        k = 2 * j + ch
                        ln(dve.tensor_scalar(modv[:, 1, k, :], modv[:, 1, k, :], cols[:, 32 + k:33 + k], None, ALU.mult))
                    for ch in (0, 1):
                        k = 2 * j + ch
                        for v, (a0, a1) in enumerate(((0, SEQ), (SEQ, TOK))):
                            ins = dve.tensor_scalar(xnT[:, k, a0:a1], xnT[:, k, a0:a1], modv[:, 1, k, v:v + 1],
                                                    modv[:, 0, k, v:v + 1], ALU.mult, ALU.add)
                        ins.then_inc(S("h_ready"), 1)
                    for ch in (0, 1):
                        k = 2 * j + ch
                        dve.wait_ge(S("h_hi"), k + 1)
                        dve.tensor_tensor(h_lo[:, k, :], xnT[:, k, 0:SEQ], h_hi[:, k, :].bitcast(f32),
                                          ALU.subtract).then_inc(S("h_lo"), 1)
                        dve.tensor_tensor(hc_lo[:, k, :], xnT[:, k, SEQ:TOK], hc_hi[:, k, :].bitcast(f32),
                                          ALU.subtract).then_inc(S("h_lo"), 1)

            def conv(ci):
                it = ITEMS[ci]
                dve.wait_ge(S("conv_raw"), ci + 1)
                if ci >= 2:
                    dve.wait_ge(S("item_pe"), ci - 1)
                ct = {"q": 0, "k": 8, "v": 16}[it["what"]] + it["head"]
                a, r = acc[ci % 2], rawc[ci % 2]
                for tap in range(CONV):
                    w = convw[:, tap * 24 + ct:tap * 24 + ct + 1]
                    if tap == 0:
                        ln(dve.tensor_scalar(a[:], r[:, 0:772], w, None, ALU.mult))
                    else:
                        ins = dve.scalar_tensor_tensor(out=a[:], in0=r[:, tap:tap + 772], scalar=w, in1=a[:],
                                                       op0=ALU.mult, op1=ALU.add)
                        if tap < CONV - 1:
                            ln(ins)
                        else:
                            ins.then_inc(S("conv_done"), 1)

            def v_rows(ci):
                vi = ci - 8
                h = ITEMS[ci]["head"]
                dve.wait_ge(S("item_pe"), ci + 1)
                dve.tensor_copy(vl[:, :, h * P:(h + 1) * P], bank4(6))
                dve.tensor_copy(vc[:, :, h * P:(h + 1) * P], bank(7, 256, 128).rearrange("p (t n) -> p t n", t=CT)).then_inc(
                    S("v_evac"), 1)

            def gdn(slot):
                k, n, pr = slot["kind"], slot["n"], PAIRS[slot["pair"]]
                half = pr["half"]
                for d in (0, 1):
                    tile = pr["tiles"][d]
                    b = 4 + 2 * d + slot["i"] % 2
                    ps = bank4(b)
                    done = S(f"gd{d}")
                    dve.wait_ge(S(f"gp{d}"), slot["i"] + 1)
                    if k == "gram":
                        dve.wait_ge(S(f"dmask{d}"), slot["pair"] + 1)
                        for u in range(4):
                            col = unit_col(d, tile, 4 * half + u)
                            ins = dve.scalar_tensor_tensor(out=LL[d][:, u, :], in0=ps[:, u, :], scalar=crow[:, col:col + 1],
                                                           in1=DD[d][:, u, :], op0=ALU.mult, op1=ALU.mult)
                        ins.then_inc(done, 1)
                    elif k == "qk":
                        dve.tensor_tensor(DD[d][:], ps, DD[d][:], ALU.mult).then_inc(done, 1)
                    elif k == "couple":
                        mo = STAGE + (2 * n + d) * 64
                        mask = consts[:, mo:mo + 64].unsqueeze(1).to_broadcast([P, 4, 64])
                        ins = dve.tensor_tensor(PM[d][:], bank4(b, 64), mask, ALU.mult)
                        if n > 0:
                            ins.then_inc(done, 1)
                            continue
                        ln(ins)
                        for e in (0, 1):
                            iv = odd1(ident, 1, d, e).unsqueeze(1).to_broadcast([P, 4, 64, 1])
                            yv = YY[d][:].rearrange("p u (b e s) -> p u b e s", e=2, s=1)[:, :, :, e, :]
                            if e == (0 if d else 1):
                                last = dve.tensor_tensor(yv, iv, PM[d][:].unsqueeze(3), ALU.subtract)
                            else:
                                last = dve.tensor_copy(yv, iv)
                            if e == 0:
                                ln(last)
                        last.then_inc(done, 1)
                    elif k == "correct":
                        yv = odd(YY[d][:], BLOCKS[n], d)
                        pv = bank4(b, 64).rearrange("p u (b s) -> p u b s", s=BLOCKS[n])
                        ins = dve.tensor_tensor(yv, yv, pv, ALU.subtract)
                        ins.then_inc(S(f"gy{d}") if n == len(BLOCKS) - 1 else done, 1)
                    elif k == "ks":
                        for u in range(4):
                            h = 4 * half + u
                            col = unit_col(d, tile, h)
                            ins = dve.scalar_tensor_tensor(out=RR[d][:, u, :], in0=ps[:, u, :], scalar=ngr[:, col:col + 1],
                                                           in1=v_of(h, tile), op0=ALU.mult, op1=ALU.add)
                        ins.then_inc(done, 1)
                    elif k == "qs":
                        if slot["pair"] == 2 * CT:
                            dve.wait_ge(S("oacc0"), 1)
                        for u in range(4):
                            h = 4 * half + u
                            o = o_acc[:, tile, h * P:(h + 1) * P]
                            ins = dve.scalar_tensor_tensor(out=o, in0=ps[:, u, :], scalar=DEC[:, tile * 2 + d, 0, h:h + 1],
                                                           in1=o, op0=ALU.mult, op1=ALU.add)
                        ins.then_inc(done, 1)
                    elif k == "az":
                        o = o_acc[:, tile, 4 * half * P:(4 * half + 4) * P].rearrange("p (u n) -> p u n", u=4)
                        dve.tensor_tensor(o, ps, o, ALU.add).then_inc(done, 1)
                    elif k == "kz":
                        for u in range(4):
                            h = 4 * half + u
                            s = SS[:, d, h, :]
                            ins = dve.scalar_tensor_tensor(out=s, in0=s, scalar=DEC[:, tile * 2 + d, 2, h:h + 1],
                                                           in1=ps[:, u, :], op0=ALU.mult, op1=ALU.add)
                        ins.then_inc(done, 1)

            def out_rows(j):
                dve.wait_ge(S("w_used"), GROUPS[OUTS[j]]["last"] + 1)
                dve.wait_ge(S("x_again"), 16 * LT)
                for t in range(LT):
                    if j:
                        dve.wait_ge(S(f"out_dma{t}"), 16 * j)
                    dve.tensor_tensor(ost[t][:], bank(4 * (j % 2) + t), grow[:, 512 * j:512 * j + 512], ALU.mult).then_inc(
                        S("out_psum"), 1)
                    dve.wait_ge(S("out_psum"), 4 * j + t + 1)
                    dve.tensor_tensor(ost[t][:], ost[t][:], xr[:, t, 512 * j:512 * j + 512], ALU.add).then_inc(
                        S("out_ready"), 1)

            lo_part(0)
            for n in range(N_MERGE0):
                lo_part(n + 1)
                for gi, g in enumerate(CONVS):
                    e = n - g["last"]
                    if e in (1, 2):
                        conv(2 * gi + e - 1)
                    if e in (3, 4) and g["what"] == "v":
                        v_rows(2 * gi + e - 3)
                if n == GROUPS[G_BKV]["first"] + 4:
                    dve.wait_ge(S("w_used"), GROUPS[G_AB]["last"] + 1)
                    dve.wait_ge(S("beta"), 1)
                    ab = bank(6, NT * 32).rearrange("p (t c) -> p t c", t=NT)
                    v3 = lambda t: t[:].rearrange("p (t c) -> p t c", t=NT)
                    dve.wait_ge(S("alog_in"), 32)
                    dve.wait_ge(S("item_pe"), 24)
                    ln(dve.tensor_tensor(v3(ab_t[0]), ab[:, :, 16:32], dtb[:].unsqueeze(1).to_broadcast([P, NT, 16]), ALU.add))
                    ln(dve.tensor_scalar(ab_t[1][:], ab_t[0][:], -1.0, None, ALU.mult))
                    dve.tensor_tensor(ab_t[1][:], ab_t[0][:], ab_t[1][:], ALU.min).then_inc(S("negabs"), 1)
                    dve.wait_ge(S("ab_exp"), 1)
                    ln(dve.tensor_scalar(ab_t[3][:], ab_t[1][:], 1.0, None, ALU.add))
                    ln(dve.tensor_scalar(ab_t[3][:], ab_t[3][:], -1.0, None, ALU.add))
                    ln(dve.tensor_scalar(ab_t[4][:], ab_t[3][:], 0.0, None, ALU.is_equal))
                    ln(dve.tensor_tensor(ab_t[2][:], ab_t[2][:], ab_t[4][:], ALU.add))
                    ln(dve.tensor_tensor(ab_t[3][:], ab_t[3][:], ab_t[4][:], ALU.add))
                    ln(dve.reciprocal(ab_t[3][:], ab_t[3][:]))
                    ln(dve.tensor_tensor(ab_t[1][:], ab_t[1][:], ab_t[2][:], ALU.mult))
                    ln(dve.tensor_tensor(ab_t[1][:], ab_t[1][:], ab_t[3][:], ALU.mult))
                    ln(dve.scalar_tensor_tensor(out=ab_t[0][:], in0=ab_t[0][:], scalar=0.0, in1=ab_t[1][:],
                                                op0=ALU.max, op1=ALU.add))
                    dve.scalar_tensor_tensor(out=v3(gdec), in0=v3(ab_t[0]), scalar=-1.0,
                                             in1=alog[:].unsqueeze(1).to_broadcast([P, NT, 16]),
                                             op0=ALU.mult, op1=ALU.mult).then_inc(S("g_ready"), 1)
                    dve.wait_ge(S("item_pe"), 24)
                    ln(dve.tensor_scalar(rk[:], bank(7, 48), EPS, None, ALU.add))
                    dve.tensor_scalar(rq[:], bank(7, 32, 48), EPS, None, ALU.add).then_inc(S("ssq_eps"), 1)
                    dve.wait_ge(S("ssq_std"), 1)
                    ln(dve.reciprocal(rk[:], rk[:]))
                    ln(dve.reciprocal(rq[:], rq[:]))
                    ln(dve.tensor_scalar(rq[:], rq[:], float(HD ** -0.5), None, ALU.mult))
                    v4 = lambda t: t[:].rearrange("p (t d h) -> p t d h", t=NT, d=2)
                    rkb = rk[:].rearrange("p (t h) -> p t h", t=NT).unsqueeze(2).to_broadcast([P, NT, 2, 8])
                    ln(dve.tensor_tensor(v4(betar), v4(beta), rkb, ALU.mult))
                    ln(dve.tensor_tensor(v4(crow), v4(betar), rkb, ALU.mult))
                    dve.wait_ge(S("decays"), 1)
                    ln(dve.tensor_scalar(ngr[:].rearrange("p (a h) -> p a h", h=8), DEC[:, :, 0, :], -1.0, None, ALU.mult))
                    dve.tensor_tensor(v4(ngr), v4(ngr), rkb, ALU.mult).then_inc(S("prep"), 1)
                for q in range(4):
                    if N_GATE0 <= n < N_BQ0:
                        i = 4 * (n - N_GATE0) + q
                        if i < len(SLOTS) and SLOTS[i]["kind"] not in ON_SCALAR:
                            gdn(SLOTS[i])
                if N_BQ0 <= n < N_MERGE0 and (n - N_BQ0) % 2 == 1:
                    g = (n - N_BQ0) // 2
                    dve.wait_ge(S("modg_used"), 2 * (g + 1))
                    for ch in (0, 1):
                        k = 2 * g + ch
                        ins = dve.tensor_scalar(GATE[:, k:k + 1], bank(4 + 2 * (g % 2) + ch, 1), cols[:, 80 + k:81 + k],
                                                None, ALU.add)
                    ins.then_inc(S("modg_evac"), 1)
            dve.wait_ge(S("o_ssq"), 32)
            ln(dve.tensor_tensor(ssq_o[:], ssq_o[:], rq[:], ALU.mult))
            ln(dve.tensor_tensor(ssq_o[:], ssq_o[:], rq[:], ALU.mult))
            dve.tensor_scalar(ssq_o[:], ssq_o[:], 1.0 / P, EPS, ALU.mult, ALU.add).then_inc(S("o_var"), 1)
            dve.wait_ge(S("o_std"), 1)
            ln(dve.reciprocal(ssq_o[:], ssq_o[:]))
            ln(dve.tensor_tensor(ssq_o[:], ssq_o[:], rq[:], ALU.mult))
            for t in range(LT):
                o = o_acc[:, t, :].rearrange("p (h n) -> p h n", h=8)
                dve.tensor_tensor(o, o, ssq_o[:, 8 * t:8 * t + 8].unsqueeze(2).to_broadcast([P, 8, P]), ALU.mult).then_inc(
                    S("y_ready"), 1)
            for h in range(HEADS):
                dve.wait_ge(S("yt_ready"), h + 1)
                dve.wait_ge(S(f"z_in{h % 2}"), 16 * (h // 2 + 1))
                if h >= 2:
                    dve.wait_ge(S("a_lo"), h - 1)
                dve.scalar_tensor_tensor(out=atmp[h % 2][:], in0=bank(4 + h % 4), scalar=cols[:, 96:97], in1=zst[h % 2][:],
                                         op0=ALU.mult, op1=ALU.mult).then_inc(S("a_tmp"), 1)
                dve.wait_ge(S("a_hi"), h + 1)
                dve.tensor_tensor(a_lo[:, h, :], atmp[h % 2][:], a_hi[:, h, :].bitcast(f32), ALU.subtract).then_inc(
                    S("a_lo"), 1)
            dve.wait_ge(S("qk_ssq"), 44)
            dve.tensor_scalar(ssq_a[:], ssq_a[:], 1.0 / P, EPS, ALU.mult, ALU.add).then_inc(S("qk_var"), 1)
            dve.wait_ge(S("qk_std"), 1)
            ln(dve.reciprocal(ssq_a[:], ssq_a[:]))
            dve.wait_ge(S("tab_in"), 48)
            for w0, tab in ((0, qtab), (128, ktab)):
                for hf in (0, 1):
                    wv = wrow[:, w0 + 64 * hf:w0 + 64 * hf + 64].unsqueeze(1).to_broadcast([P, LT, 64])
                    for sn in (0, 1):
                        ln(dve.tensor_tensor(tab[:, :, 128 * hf + 64 * sn:128 * hf + 64 * sn + 64],
                                             cs[:, :, 64 * sn:64 * sn + 64], wv, ALU.mult))

            def rope(rows_t, tab_t, nh):
                x1, x2 = rows_t[:, :, 0:64], rows_t[:, :, 64:128]
                tv = lambda k: tab_t[:, 64 * k:64 * k + 64].unsqueeze(1).to_broadcast([P, nh, 64])
                ln(dve.tensor_tensor(rt[0][:, 0:nh, :], x1, tv(0), ALU.mult))
                ln(dve.tensor_tensor(rt[1][:, 0:nh, :], x2, tv(3), ALU.mult))
                ln(dve.tensor_tensor(rt[2][:, 0:nh, :], x1, tv(1), ALU.mult))
                ln(dve.tensor_tensor(rt[3][:, 0:nh, :], x2, tv(2), ALU.mult))
                ln(dve.tensor_tensor(x1, rt[0][:, 0:nh, :], rt[1][:, 0:nh, :], ALU.subtract))
                return dve.tensor_tensor(x2, rt[2][:, 0:nh, :], rt[3][:, 0:nh, :], ALU.add)

            for t in range(LT):
                rv = bqr[:, t, :].rearrange("p (h n) -> p h n", h=8)
                ln(dve.tensor_tensor(rv, rv, ssq_a[:, 8 * t:8 * t + 8].unsqueeze(2).to_broadcast([P, 8, P]), ALU.mult))
                ln(rope(rv, qtab[:, t, :], 8))
            for t in range(NT):
                rv = kvr[:, t, 0:256].rearrange("p (h n) -> p h n", h=2)
                sv = ssq_a[:, 32 + 2 * t:34 + 2 * t].unsqueeze(2).to_broadcast([P, 2, P])
                ln(dve.tensor_tensor(rv, rv, sv, ALU.mult))
                if t < LT:
                    ln(rope(rv, ktab[:, t, :], 2))
                else:
                    ins = dve.tensor_tensor(rv, rv, wrow[:, 128:256].unsqueeze(1).to_broadcast([P, 2, P]), ALU.mult)
                    ins.then_inc(S("k_ctx_rows"), 1)

            def att_max(i):
                dve.wait_ge(S("sc_ready"), i + 1)
                ln(dve.reduce_max(nmax[:, i:i + 1], PS[:, (i % 2) * 1024:(i % 2) * 1024 + TOK], axis=AX.X))
                dve.tensor_scalar(nmax[:, i:i + 1], nmax[:, i:i + 1], -float(HD ** -0.5), None, ALU.mult).then_inc(
                    S("negmax"), 1)

            def b_parts(h):
                dve.wait_ge(S("pv_done"), h + 1)
                k = HEADS + h
                dve.wait_ge(S(f"z_in{k % 2}"), 16 * (k // 2 + 1))
                dve.tensor_tensor(btmp[:], bank(6 + h % 2), zst[k % 2][:], ALU.mult).then_inc(S("b_tmp"), 1)
                dve.wait_ge(S("b_hi"), h + 1)
                dve.tensor_tensor(b_lo[:, h, :], btmp[:], b_hi[:, h, :].bitcast(f32), ALU.subtract).then_inc(S("b_lo"), 1)

            att_max(0)
            for i in range(32):
                if i < 31:
                    att_max(i + 1)
                dve.wait_ge(S("exp_done"), i + 1)
                ln(dve.reciprocal(rsum[:, i:i + 1], rsum[:, i:i + 1]))
                dve.tensor_scalar(probs[i % 2][:], probs[i % 2][:], rsum[:, i:i + 1], None, ALU.mult).then_inc(
                    S("p_norm"), 1)
                if i % 4 == 1 and i >= 5:
                    b_parts(i // 4 - 1)
            b_parts(HEADS - 1)
            for n in range(N_MERGE0, NP):
                lo_part(n + 1)
                e = n - N_MERGE0
                if e >= 4 and e % 4 == 0 and e // 4 <= 8:
                    j = e // 4 - 1
                    for jj in (0, 1):
                        m = 2 * j + jj
                        b0 = 4 * (j % 2)
                        dve.wait_ge(S("w_used"), n)
                        dve.wait_ge(S(f"gates_in{m % 4}"), 32 * (m // 4 + 1))
                        if m >= 2:
                            dve.wait_ge(S("m_lo"), m - 1)
                        t0, t1 = mtmp[2 * (m % 2)], mtmp[2 * (m % 2) + 1]
                        ln(dve.tensor_tensor(t0[:], bank(b0 + jj), gsig[m % 4][:, 0, :], ALU.mult))
                        dve.tensor_tensor(t1[:], bank(b0 + 2 + jj), gsig[m % 4][:, 1, :], ALU.mult).then_inc(
                            S("m_psum"), 1)
                        dve.wait_ge(S("m_psum"), m + 1)
                        dve.tensor_tensor(t0[:], t0[:], t1[:], ALU.add).then_inc(S("m_tmp"), 1)
                    for jj in (0, 1):
                        m = 2 * j + jj
                        dve.wait_ge(S("m_hi"), m + 1)
                        dve.tensor_tensor(m_lo[:, m, :], mtmp[2 * (m % 2)][:], m_hi[:, m, :].bitcast(f32),
                                          ALU.subtract).then_inc(S("m_lo"), 1)
                if n == N_OUT0:
                    dve.wait_ge(S("w_used"), N_OUT0)
                    for k in range(KT):
                        if k >= 4:
                            dve.wait_ge(S("grow_mm"), k - 3)
                        dve.tensor_scalar(gcb[k % 4][:], ones, GATE[:, k:k + 1], None, ALU.mult).then_inc(S("gcb"), 1)
                    for q in range(4):
                        dve.wait_ge(S("grow_mm"), 4 * q + 4)
                        dve.tensor_copy(grow[:, 512 * q:512 * q + 512], bank(q)).then_inc(S("grow_evac"), 1)
                if n > N_OUT0 and (n - N_OUT0) % 8 == 0:
                    out_rows((n - N_OUT0) // 8 - 1)
            out_rows(3)

        @block.tensor
        def _(pe):
            pe.wait_ge(S("const_in"), 16)
            pe.wait_ge(S("rows_in"), 96)
            pe.transpose(bank(7, 97), rows[:], ident[0:97, 0:97]).then_inc(S("rowsT"), 1)
            pe.transpose(bank(6, 120), crows[:], ident[0:120, 0:120]).then_inc(S("rowsT"), 1)

            def x_transposes(t):
                pe.wait_ge(S("xn"), t + 1)
                for q4 in range(4):
                    n = 4 * t + q4
                    if n >= 4:
                        pe.wait_ge(S("xt_act" if q4 % 2 else "xt_dve"), (n - 4) // 2 + 1)
                    for u in range(4):
                        k = 4 * q4 + u
                        ins = pe.transpose(bank4(n % 4)[:, u, :], xt[t % 2][:, k * P:(k + 1) * P], ident)
                    ins.then_inc(S("xt_ready"), 1)

            def mod_piece(m):
                if m == 0:
                    pe.wait_ge(S("silu_c"), 1)
                g, half = m // 2, m % 2
                pe.wait_ge(S(f"mod_in{m % 3}"), 16 * (m // 3 + 1))
                if g >= 2 and half == 0:
                    pe.wait_ge(S("mod_evac"), g - 1)
                for ch in (0, 1):
                    for k in range(8):
                        ins = pe.matmul(bank(4 + 2 * (g % 2) + ch, 2), modr[m % 3][:, k, ch * P:(ch + 1) * P],
                                        sc2[:, half * 8 + k, :], start=(half == 0 and k == 0), stop=(half == 1 and k == 7))
                ins.then_inc(S("mod_used"), 1)

            for t in range(NT):
                x_transposes(t)
                if t < 3:
                    mod_piece(t)
            for m in range(3, 32):
                mod_piece(m)

            def item_work(ci):
                it = ITEMS[ci]
                pe.wait_ge(S("item_ready"), ci + 1)
                a = acc[ci % 2]
                if it["what"] == "v":
                    if ci > 8:
                        pe.wait_ge(S("v_evac"), ci - 8)
                    for t in range(LT):
                        pe.transpose(bank4(6)[:, t, :], a[:, t * P:(t + 1) * P], ident)
                    for t in range(CT):
                        ins = pe.transpose(bank(7, P, 128 + t * P), a[:, 516 + t * P:516 + (t + 1) * P], ident)
                else:
                    if it["what"] == "q":
                        pe.wait_ge(S("v_evac"), 8)
                    off = 48 if it["what"] == "q" else 0
                    for t in range(LT if off else NT):
                        a0 = t * P if t < LT else 516 + (t - LT) * P
                        ins = pe.matmul(bank(7, 1, off + t * 8 + it["head"]), a[:, a0:a0 + P], ones[:, 0:1],
                                        start=True, stop=True)
                ins.then_inc(S("item_pe"), 1)

            def three(out_ap, lhs, rhs, first, last, shared=False):
                (lh, ll), (rh, rl) = lhs, rhs
                pe.matmul(out_ap, lh, rh, start=first, stop=False, skip_group_check=shared)
                pe.matmul(out_ap, lh, rl, start=False, stop=False, skip_group_check=shared)
                return pe.matmul(out_ap, ll, rh, start=False, stop=last, skip_group_check=shared)

            def gdn(slot):
                k, n, pr, i = slot["kind"], slot["n"], PAIRS[slot["pair"]], slot["i"]
                half = pr["half"]
                for d in (0, 1):
                    tile = pr["tiles"][d]
                    b = 4 + 2 * d + i % 2
                    ps = bank4(b)
                    if i:
                        pe.wait_ge(S(f"gd{d}"), i)
                    if k == "decay":
                        pe.wait_ge(S(f"gm{d}"), slot["pair"] + 1)
                    if slot["pair"] == 0 and k == "ks":
                        pe.wait_ge(S("states0"), 1)
                    for u in range(4):
                        h = 4 * half + u
                        kt = kT_of(h, tile)
                        qt = qT[:, h, tile * P:(tile + 1) * P] if pr["lat"] else None
                        if k == "decay":
                            m = (GT, LT_)[d]
                            ins = pe.matmul(ps[:, u, :], GM[d][:, u, :], consts[:, m:m + P], start=True, stop=True)
                        elif k == "gram":
                            ins = pe.matmul(ps[:, u, :], kt, kt, start=True, stop=True)
                        elif k == "qk":
                            ins = pe.matmul(ps[:, u, :], qt, kt, start=True, stop=True)
                        elif k == "couple":
                            rhs = odd1(ident if n == 0 else YY[d][:, u, :], BLOCKS[n], d)
                            dst = bank4(b, 64)[:, u, :].rearrange("p (b s) -> p b s", s=BLOCKS[n])
                            ins = pe.matmul(dst, LL[d][:, u, :], rhs, start=True, stop=True)
                        elif k == "correct":
                            ins = pe.matmul(bank4(b, 64)[:, u, :], XX[d][:, u, :], PM[d][:, u, :], start=True, stop=True)
                        elif k == "flip":
                            ins = pe.transpose(ps[:, u, :], YY[d][:, u, :], ident)
                        elif k == "at":
                            ins = pe.transpose(ps[:, u, :], DD[d][:, u, :], ident)
                        elif k == "kt":
                            ins = pe.transpose(ps[:, u, :], kt, ident)
                        elif k == "ks":
                            ins = pe.matmul(ps[:, u, :], kt, SS[:, d, h, :], start=True, stop=True)
                        elif k == "z":
                            ins = pe.matmul(ps[:, u, :], XX[d][:, u, :], RR[d][:, u, :], start=True, stop=True)
                        elif k == "qs":
                            ins = pe.matmul(ps[:, u, :], qt, SS[:, d, h, :], start=True, stop=True)
                        elif k == "az":
                            ins = pe.matmul(ps[:, u, :], YY[d][:, u, :], ZZ[d][:, u, :], start=True, stop=True)
                        elif k == "kz":
                            ins = pe.matmul(ps[:, u, :], LL[d][:, u, :], ZZ[d][:, u, :], start=True, stop=True)
                    ins.then_inc(S(f"gp{d}"), 1)

            def piece(n):
                p = PIECES[n]
                gi = p["g"]
                g = GROUPS[gi]
                first, last = n == g["first"], n == g["last"]
                if first:
                    accs_free_needed(pe, gi)
                pe.wait_ge(S("w_lo"), n + 1)
                wh, wl = part3(whi[n % 2], p), part3(wlo[n % 2], p)
                kind = p["kind"]
                for kk in range(p["nk"]):
                    k = p["k0"] + kk
                    st, sp_ = first and kk == 0, last and kk == p["nk"] - 1
                    if gi == 0:
                        pe.wait_ge(S("h_lo"), 2 * (k + 1))
                    if kind in ("conv", "gate", "merge"):
                        src = (h_hi, h_lo)
                        b0 = 3 * (gi % 2)
                        if kind == "gate":
                            b0 = 2 * (GATES.index(gi) % 2)
                        if kind == "merge":
                            src = ((a_hi, a_lo), (b_hi, b_lo))[p["branch"]]
                            b0 = 4 * (p["j"] % 2) + 2 * p["branch"]
                        for j in (0, 1):
                            w = (wh[:, kk, j * P:(j + 1) * P], wl[:, kk, j * P:(j + 1) * P])
                            ins = three(bank(b0 + j), w, (src[0][:, k, :], src[1][:, k, :]), st, sp_)
                        if kind == "conv" and g["what"] != "q":
                            for j in (0, 1):
                                w = (wh[:, kk, j * P:(j + 1) * P], wl[:, kk, j * P:(j + 1) * P])
                                ins = three(bank(b0 + 2, 256, 256 * j), w, (hc_hi[:, k, :], hc_lo[:, k, :]),
                                            st and j == 0, sp_, shared=True)
                        if kind == "gate":
                            i = 4 * (n - N_GATE0) + kk
                            if kk == p["nk"] - 1:
                                ins.then_inc(S("w_used"), 1)
                            if i < len(SLOTS):
                                if i == 0:
                                    pe.wait_ge(S("prep"), 1)
                                gdn(SLOTS[i])
                    elif kind in ("bkv", "bq", "out"):
                        b0 = 4 * ((g["j"]) % 2) if kind == "out" else 0
                        for t in range(NT if kind == "bkv" else LT):
                            if kind == "out":
                                l = (m_hi[:, k, t * P:(t + 1) * P], m_lo[:, k, t * P:(t + 1) * P])
                            elif t < LT:
                                l = (h_hi[:, k, t * P:(t + 1) * P], h_lo[:, k, t * P:(t + 1) * P])
                            else:
                                l = (hc_hi[:, k, (t - LT) * P:(t - LT + 1) * P], hc_lo[:, k, (t - LT) * P:(t - LT + 1) * P])
                            ins = three(bank(b0 + t), l, (wh[:, kk, :], wl[:, kk, :]), st, sp_)
                if kind == "ab":
                    for t in range(NT):
                        for k in range(KT):
                            if t < LT:
                                l = (h_hi[:, k, t * P:(t + 1) * P], h_lo[:, k, t * P:(t + 1) * P])
                            else:
                                l = (hc_hi[:, k, (t - LT) * P:(t - LT + 1) * P], hc_lo[:, k, (t - LT) * P:(t - LT + 1) * P])
                            ins = three(bank(6, 32, t * 32), l, (wh[:, k, :], wl[:, k, :]), k == 0, k == KT - 1)
                if kind != "gate":
                    ins.then_inc(S("w_used"), 1)

            for n in range(N_MERGE0):
                piece(n)
                for gi, g in enumerate(CONVS):
                    e = n - g["last"]
                    if e in (3, 4):
                        item_work(2 * gi + e - 3)
                if n == GROUPS[G_BKV]["first"] + 5:
                    pe.wait_ge(S("g_ready"), 1)
                    for t in range(NT):
                        for d in (0, 1):
                            for w, m in enumerate(((LE, GT, ONES), (GE, LT_, ONES))[d]):
                                ins = pe.matmul(bank(6, 8, ((t * 2 + d) * 3 + w) * 8), consts[:, m:m + P],
                                                gdec[:, t * 16 + d * 8:t * 16 + d * 8 + 8], start=True, stop=True)
                    ins.then_inc(S("cum"), 1)
                if N_BQ0 <= n < N_MERGE0:
                    m = n - N_BQ0
                    gg, half = m // 2, m % 2
                    pe.wait_ge(S(f"modg_in{m % 2}"), 16 * (m // 2 + 1))
                    if m == 0:
                        for d in (0, 1):
                            pe.wait_ge(S(f"gd{d}"), len(SLOTS))
                    if gg >= 2 and half == 0:
                        pe.wait_ge(S("modg_evac"), gg - 1)
                    for ch in (0, 1):
                        for k in range(8):
                            ins = pe.matmul(bank(4 + 2 * (gg % 2) + ch, 1), modg[m % 2][:, k, ch * P:(ch + 1) * P],
                                            silu_cg[:, half * 8 + k:half * 8 + k + 1],
                                            start=(half == 0 and k == 0), stop=(half == 1 and k == 7))
                    ins.then_inc(S("modg_used"), 1)
            pe.wait_ge(S("modg_evac"), 8)
            pe.wait_ge(S("y_ready"), LT)
            for h in range(HEADS):
                if h >= 4:
                    pe.wait_ge(S("a_tmp"), h - 3)
                for t in range(LT):
                    ins = pe.transpose(bank4(4 + h % 4)[:, t, :], o_acc[:, t, h * P:(h + 1) * P], ident)
                ins.then_inc(S("yt_ready"), 1)
            pe.wait_ge(S("k_ctx_rows"), CT)
            for h in range(HEADS):
                if h < 4:
                    pe.wait_ge(S("bq_evac"), 8)
                else:
                    pe.wait_ge(S("qt_evac"), h - 3)
                for t in range(LT):
                    ins = pe.transpose(bank4(h % 4)[:, t, :], bqr[:, t, h * P:(h + 1) * P], ident)
                ins.then_inc(S("qt_ready"), 1)
            pe.wait_ge(S("a_tmp"), HEADS)
            for kv in range(KV):
                for t in range(NT):
                    ins = pe.transpose(PS[:, (4 + 2 * kv) * 512 + t * P:(4 + 2 * kv) * 512 + (t + 1) * P],
                                       kvr[:, t, kv * P:(kv + 1) * P], ident)
                ins.then_inc(S("kt_ready"), 1)
            pe.wait_ge(S("qt_evac"), HEADS)
            pe.wait_ge(S("kt_evac"), KV)

            def scores(i):
                h, qt = divmod(i, 4)
                if i >= 2:
                    pe.wait_ge(S("exp_done"), i - 1)
                b = 2 * (i % 2)
                q = qhT[:, h, qt * P:(qt + 1) * P]
                kv = h // (HEADS // KV)
                pe.matmul(bank(b), q, khT[:, kv, 0:512], start=True, stop=True)
                pe.matmul(bank(b + 1, 256), q, khT[:, kv, 512:TOK], start=True, stop=True).then_inc(S("sc_ready"), 1)

            scores(0)
            for i in range(32):
                if i < 31:
                    scores(i + 1)
                h, qt = divmod(i, 4)
                pe.wait_ge(S("p_norm"), i + 1)
                if i:
                    pe.wait_ge(S("pt_evac"), i)
                for t in range(NT):
                    ins = pe.transpose(PS[:, 2048 + t * P:2048 + (t + 1) * P], probs[i % 2][:, t * P:(t + 1) * P], ident)
                ins.then_inc(S("pt_ready"), 1)
                if qt == 3:
                    pe.wait_ge(S("pt_evac"), i + 1)
                    if h >= 2:
                        pe.wait_ge(S("b_tmp"), h - 1)
                    kv = h // (HEADS // KV)
                    for t in range(NT):
                        ins = pe.matmul(bank(6 + h % 2), kvr[:, t, 256 + kv * P:256 + (kv + 1) * P], PTt[:, t, :],
                                        start=(t == 0), stop=(t == NT - 1))
                    ins.then_inc(S("pv_done"), 1)
            pe.wait_ge(S("a_lo"), HEADS)
            pe.wait_ge(S("b_lo"), HEADS)
            for n in range(N_MERGE0, NP):
                if n == N_OUT0:
                    pe.wait_ge(S("m_psum"), 16)
                    for k in range(KT):
                        pe.wait_ge(S("gcb"), k + 1)
                        pe.matmul(bank(k // 4, P, (k % 4) * P), gcb[k % 4][:], ident, start=True, stop=True).then_inc(
                            S("grow_mm"), 1)
                    pe.wait_ge(S("m_lo"), KT)
                piece(n)


INPUTS = ["x", "c", "ctx", "c_ctx", "w_mod", "b_mod", "norm_w", "w_in", "conv_w", "a_log", "dt_bias", "a_norm_w",
          "q_norm_w", "k_norm_w", "w_proj_a", "w_proj_b", "w_out"]


def kernel(**inputs):
    import concourse.bacc as bacc
    from concourse.bass_utils import run_bass_kernel_spmd

    nc = bacc.Bacc("TRN2", target_bir_lowering=False, num_devices=1)
    arrays = {f"{name}_dram": np.ascontiguousarray(inputs[name]) for name in INPUTS}
    arrays["consts_dram"], arrays["rope_dram"] = shape_constants()
    args = [nc.dram_tensor(name, a.shape, mybir.dt.float32, kind="ExternalInput").ap() for name, a in arrays.items()]
    out = nc.dram_tensor("out_dram", (1, SEQ, DM), mybir.dt.float32, kind="ExternalOutput").ap()
    build(nc, *args, out)
    return run_bass_kernel_spmd(nc, [arrays], core_ids=[0]).results[0]["out_dram"]
```

```python
from contextlib import ExitStack

import numpy as np

import concourse.bass as bass
from concourse import mybir

P = 128
DM = 2048
SEQ = 512
CTX = 256
TOK = SEQ + CTX
HEADS = 8
CONV = 5
KV = 2
HD = 128
KT = DM // P
LT = SEQ // P
CT = CTX // P
NT = LT + CT
EPS = 1e-6
GRID_W = 64
ROPE_THETA = 10000.0

COL_AQ, COL_AK, COL_AV, COL_AZ = 0, 1024, 2048, 3072
COL_AB = 4096
COL_BQ, COL_BKV, COL_BZ, COL_BR = 4128, 5152, 5664, 6688

IDENT, LE, GE, GT, LT_, ONES, STAGE = 0, 128, 256, 384, 512, 640, 768
BLOCKS = [1, 2, 4, 8, 16, 32, 64]
SEL = STAGE + len(BLOCKS) * 2 * 64
NCONST = SEL + 2


def shape_constants():
    a = np.arange(P)
    t, i = a[:, None], a[None, :]
    parts = [t == i, t <= i, t >= i, t > i, t < i, np.ones((P, P), bool)]
    for s in BLOCKS:
        block = a // s
        for backward in (0, 1):
            cols = a[(block % 2) == (0 if backward else 1)]
            want = cols // s + (1 if backward else -1)
            parts.append(block[:, None] == want[None, :])
    parts.append(a[:, None] // 2 == np.arange(2)[None, :])
    consts = np.concatenate(parts, axis=1).astype(np.float32)
    assert consts.shape == (P, NCONST)
    tok = np.arange(SEQ)
    inv = ROPE_THETA ** (-np.arange(HD // 4) / (HD // 4))
    ang = np.concatenate([(tok // GRID_W)[:, None] * inv, (tok % GRID_W)[:, None] * inv], axis=-1)
    rope = np.concatenate([np.cos(ang), np.sin(ang)], axis=1).astype(np.float32)
    return consts, rope


def projection_plan():
    groups, pieces = [], []

    def group(kind, col, width, per_piece, **more):
        g = dict(kind=kind, col=col, width=width, first=len(pieces), **more)
        for k0 in range(0, KT, per_piece):
            pieces.append(dict(g=len(groups), kind=kind, k0=k0, nk=per_piece, col=col, width=width))
        g["last"] = len(pieces) - 1
        groups.append(g)

    for j in range(4):
        group("mod", 512 * j, 512, 2, j=j, scale=0)
        group("mod", DM + 512 * j, 512, 2, j=j, scale=1)
    for what, col in (("k", COL_AK), ("v", COL_AV), ("q", COL_AQ)):
        for j in range(4):
            group("conv", col + 256 * j, 256, 4, what=what, pair=j)
    group("ab", COL_AB, 32, 16)
    group("bkv", COL_BKV, 512, 2)
    for first, col, n in ((0, COL_AZ, 4), (8, COL_BZ, 4), (16, COL_BR, 16)):
        for j in range(n):
            group("gate", col + 256 * j, 256, 4, row=first + 2 * j)
    bq0 = len(groups)
    groups += [dict(kind="bq", half=j) for j in (0, 1)] + [dict(kind="modg", j=j) for j in range(4)]
    for i in range(16):
        pieces.append(dict(g=bq0 + i // 8, kind="bq", k0=2 * (i % 8), nk=2, col=COL_BQ + 512 * (i // 8), width=512))
        for m in (2 * i, 2 * i + 1):
            pieces.append(dict(g=bq0 + 2 + m // 8, kind="modg", k0=2 * (m % 8), nk=2, col=2 * DM + 512 * (m // 8), width=512))
    for gi in range(bq0, len(groups)):
        mine = [n for n, p in enumerate(pieces) if p["g"] == gi]
        groups[gi].update(first=mine[0], last=mine[-1])
    for j in range(8):
        for branch in (0, 1):
            g = dict(kind="merge", first=len(pieces), j=j, branch=branch)
            for k0 in (0, 4):
                pieces.append(dict(g=len(groups), kind="merge", k0=k0, nk=4, col=256 * j, width=256, branch=branch, j=j))
            g["last"] = len(pieces) - 1
            groups.append(g)
    for j in range(4):
        group("out", 512 * j, 512, 2, j=j)
    return groups, pieces


def scan_plan():
    pairs, slots = [], []
    fwd = [LT, LT + 1] + list(range(LT))
    bwd = [LT + 1, LT] + list(range(LT))[::-1]
    for step in range(NT):
        for half in range(2):
            lat, last = step >= CT, step == NT - 1
            pairs.append(dict(tiles=(fwd[step], bwd[step]), half=half, lat=lat, last=last, first=len(slots)))
            p = len(pairs) - 1
            kinds = [("decay", 0), ("gram", 0)] + [("qk", 0)] * lat
            for n in range(len(BLOCKS)):
                kinds += [("couple", n)] + [("correct", n)] * (n > 0) + [("flip", n)] * (n < len(BLOCKS) - 1)
            kinds += [("at", 0)] * lat + [("kt", 0)] * (not last) + [("ks", 0), ("z", 0)]
            kinds += [("qs", 0), ("az", 0)] * lat + [("kz", 0)] * (not last)
            slots += [dict(kind=k, n=n, pair=p, i=len(slots) + m) for m, (k, n) in enumerate(kinds)]
            pairs[-1]["end"] = len(slots)
    return pairs, slots


ON_SCALAR = ("decay", "flip", "at", "kt", "z")


def build(nc, x, c, ctx, c_ctx, w_mod, b_mod, norm_w, w_in, conv_w, a_log, dt_bias, a_norm_w, q_norm_w,
          k_norm_w, w_proj_a, w_proj_b, w_out, consts_in, rope_in, out):
    f32, f32r = mybir.dt.float32, mybir.dt.float32r
    ALU, ACT, AX = mybir.AluOpType, mybir.ActivationFunctionType, mybir.AxisListType
    GROUPS, PIECES = projection_plan()
    PAIRS, SLOTS = scan_plan()
    NP = len(PIECES)
    CONVS = [g for g in GROUPS if g["kind"] == "conv"]
    ITEMS = [dict(what=g["what"], head=2 * g["pair"] + j, g=gi, j=j) for gi, g in enumerate(CONVS) for j in (0, 1)]
    G_CONV0 = [g["kind"] for g in GROUPS].index("conv")
    G_AB = G_CONV0 + len(CONVS)
    MODS = [g for g in GROUPS if g["kind"] == "mod"]
    NM = MODS[-1]["last"] + 1
    MODGS = [gi for gi, g in enumerate(GROUPS) if g["kind"] == "modg"]
    G_BKV = G_AB + 1
    GATES = [gi for gi, g in enumerate(GROUPS) if g["kind"] == "gate"]
    BQS = [gi for gi, g in enumerate(GROUPS) if g["kind"] == "bq"]
    OUTS = [gi for gi, g in enumerate(GROUPS) if g["kind"] == "out"]
    N_GATE0 = GROUPS[GATES[0]]["first"]
    N_BQ0 = GROUPS[BQS[0]]["first"]
    N_MERGE0 = GROUPS[MODGS[-1]]["last"] + 1
    N_OUT0 = GROUPS[OUTS[0]]["first"]
    N_FIN = N_GATE0 + 1 + -(-len(SLOTS) // 4)
    assert N_FIN + 13 <= N_BQ0, N_FIN - N_BQ0

    def slot_at(n, q):
        i = 4 * (n - N_GATE0 - 1) + q
        return SLOTS[i] if N_GATE0 < n < N_BQ0 and i < len(SLOTS) else None

    base = 16512
    A_CONST, A_SMALL, A_RING = 0, 6688, 11104
    A_H = A_RING + 24576
    A_C = A_H + 65536
    A_G = A_C + 32768
    A_T = A_G + 65536

    def at(name, shape, off, dt=f32):
        return nc.alloc_sbuf_tensor_at(name, shape, dt, offset=base + off)

    consts = at("consts", [P, NCONST], A_CONST)
    small_top = [A_SMALL]

    def small(name, shape):
        n = int(np.prod(shape[1:])) * 4
        n = (n + 31) // 32 * 32
        t = at(name, shape, small_top[0])
        small_top[0] += n
        assert small_top[0] <= A_RING, small_top[0] - A_RING
        return t

    cols = small("cols", [P, 97])
    convw = small("convw", [P, 120])
    GATE = small("gate_cols", [P, KT])
    stat = small("stat", [P, 16])
    beta = small("beta", [P, NT * 16])
    betar = beta
    off_wrow = small_top[0]
    gdec = small("gdec", [P, NT * 16])
    crow = small("crow", [P, NT * 16])
    ngr = small("ngr", [P, NT * 16])
    off_dec = small_top[0]
    DEC = small("decays", [P, NT * 2, 3, 8])
    rk = small("rk", [P, 48])
    rq = small("rq", [P, 32])
    alog = small("alog", [P, 16])
    dtb = small("dt_bias_rows", [P, 16])
    c4 = at("silu_c_parts", [P, KT, 4], small_top[0], f32r)
    small_top[0] += 256
    assert small_top[0] <= A_RING, small_top[0] - A_RING
    wrow = at("w_rows", [P, 256], off_wrow)
    ssq_o = at("ssq_o", [P, 32], off_dec)
    ssq_a = at("ssq_a", [P, 44], off_dec + 128)
    nmax = at("neg_max", [P, 32], off_dec + 320)
    rsum = at("row_sum", [P, 32], off_dec + 448)

    raw = [at(f"w_raw{i}", [P, 1024], A_RING + 4096 * i) for i in range(2)]
    whi = [at(f"w_hi{i}", [P, 1024], A_RING + 8192 + 4096 * i, f32r) for i in range(2)]
    wlo = [at(f"w_lo{i}", [P, 1024], A_RING + 16384 + 4096 * i, f32r) for i in range(2)]
    h_hi = at("h_hi", [P, KT, SEQ], A_H, f32r)
    h_lo = at("h_lo", [P, KT, SEQ], A_H + 32768, f32r)
    raw_mod = [at(f"w_raw_mod{i}", [P, 1024], A_H + 32768 * (i // 2) + 24576 + 4096 * (i % 2)) for i in range(4)]
    hc_hi = at("hc_hi", [P, KT, CTX], A_C, f32r)
    hc_lo = at("hc_lo", [P, KT, CTX], A_C + 16384, f32r)
    xnT = at("xnT", [P, KT, TOK], A_G)
    xt = [at(f"x_rows{i}", [P, DM], A_G + 49152 + 8192 * i) for i in range(2)]
    junk = at("junk", [P, DM], A_T)
    rows = at("rows", [97, P], A_T + 8192)
    crows = at("conv_rows", [120, P], A_T + 8704)
    modv = at("mod_vec", [P, 2, KT, 2], A_T + 9216)
    sc2 = at("silu_c", [P, 2, KT], A_T + 9472)
    mrow = at("mod_rows", [4, 512], A_T + 9728)
    G_Q, G_K, G_V, G_O = A_G, A_G + 16384, A_G + 32768, A_G + 49152
    qT = at("qT", [P, HEADS, SEQ], G_Q)
    kTl = at("kT_latent", [P, HEADS, SEQ], G_K)
    vl = at("v_latent", [P, LT, 1024], G_V)
    kTc = at("kT_context", [P, HEADS, CTX], G_O)
    vc = at("v_context", [P, CT, 1024], G_O + 8192)
    RAWW = 776
    rawc = [at(f"conv_in{i}", [P, RAWW], A_T + 4 * RAWW * i) for i in range(2)]
    acc = [at(f"conv_acc{i}", [P, 772], A_T + 8 * RAWW + 3104 * i) for i in range(2)]
    ab_t = [at(f"logit_tmp{i}", [P, NT * 16], A_T + 8 * RAWW + 384 * i) for i in range(5)]
    kvst = [at(f"kv_stage{i}", [P, 512], A_T + 2048 * i) for i in range(NT)]
    GM, DD, LL, XX, YY, RR, ZZ = ([at(f"{n}{b}", [P, 4, P], A_C + 14336 * b + 2048 * o) for b in (0, 1)] for o, n in
                                  enumerate(("decay_lhs", "decay", "L", "inv", "invT", "resid", "zval")))
    PM = [at(f"couple{b}", [P, 4, 64], A_C + 28672 + 1024 * b) for b in (0, 1)]
    SS = at("states", [P, 2, HEADS, P], A_T)
    gst = [at(f"gate_stage{i}", [P, 512], A_T + 8192 + 2048 * i) for i in range(2)]
    o_acc = at("o_acc", [P, LT, 1024], G_O)
    bqr = at("bq_rows", [P, LT, 1024], A_C)
    kvr = at("kv_rows", [P, NT, 512], A_C + 16384)
    mrow_g = at("mod_gate_rows", [4, 512], A_T + 8192)
    sqj = at("square_out", [P, P], A_T + 12288)
    qhT = at("att_qT", [P, HEADS, SEQ], A_H)
    khT = at("att_kT", [P, KV, TOK], A_H + 16384)
    PTt = at("probsT", [P, NT, SEQ], A_H + 34816)
    atmp = [at(f"a_tmp{i}", [P, 512], A_C + 2048 * i) for i in range(2)]
    probs = [at(f"probs{i}", [P, TOK], A_H + 47104 + 3072 * i) for i in range(2)]
    cs = at("cos_sin", [P, LT, 128], G_V)
    qtab = at("q_tab", [P, LT, 256], G_V + 2048)
    ktab = at("k_tab", [P, LT, 256], G_V + 6144)
    btmp = at("b_tmp", [P, 512], A_H + 63488)
    rt = [at(f"rope{i}", [P, 8, 64], A_T + 2048 * i) for i in range(4)]
    zst = [at(f"z_stage{i}", [P, 512], A_C + 28672 + 2048 * i) for i in range(2)]
    a_hi = at("a_hi", [P, 8, SEQ], A_G, f32r)
    a_lo = at("a_lo", [P, 8, SEQ], A_G + 16384, f32r)
    b_hi = at("b_hi", [P, 8, SEQ], A_G + 32768, f32r)
    b_lo = at("b_lo", [P, 8, SEQ], A_G + 49152, f32r)
    m_hi = at("m_hi", [P, KT, SEQ], A_H, f32r)
    m_lo = at("m_lo", [P, KT, SEQ], A_H + 32768, f32r)
    gsig = [at(f"gates{i}", [P, 2, 512], A_C + 4096 * i) for i in range(4)]
    mtmp = [at(f"m_tmp{i}", [P, 512], A_T + 2048 * i) for i in range(4)]
    gcb = [at(f"gate_lhs{i}", [P, P], A_T + 8192 + 512 * i) for i in range(4)]
    grow = at("gate_rows", [P, DM], A_C + 16384)
    xr = at("x_again", [P, LT, DM], A_G + 8192)
    ost = [at(f"out_stage{i}", [P, 512], A_G + 40960 + 2048 * i) for i in range(4)]

    gate_scr = nc.dram_tensor("gate_scratch", [48, P, SEQ], f32, kind="Internal").ap()
    kv_scr = nc.dram_tensor("kv_scratch", [NT, P, 512], f32, kind="Internal").ap()

    with ExitStack() as stack:
        PS = stack.enter_context(nc.psum_tensor("psum", [P, 8 * 512], f32))
        sems = {}

        def S(name):
            if name not in sems:
                sems[name] = stack.enter_context(nc.semaphore(name))
            return sems[name]

        def bank(b, n=512, off=0):
            return PS[:, b * 512 + off:b * 512 + off + n]

        def bank4(b, w=128):
            return PS[:, b * 512:b * 512 + 4 * w].rearrange("p (u n) -> p u n", u=4)

        ident = consts[:, IDENT:IDENT + P]
        ones = consts[:, ONES:ONES + P]

        def odd(tile4, s, d):
            e = 0 if d else 1
            return tile4.rearrange("p u (b e s) -> p u b e s", e=2, s=s)[:, :, :, e, :]

        def odd1(t, s, d, e=None):
            e = (0 if d else 1) if e is None else e
            return t.rearrange("p (b e s) -> p b e s", e=2, s=s)[:, :, e, :]

        def kT_of(head, tile):
            if tile < LT:
                return kTl[:, head, tile * P:(tile + 1) * P]
            return kTc[:, head, (tile - LT) * P:(tile - LT + 1) * P]

        def v_of(head, tile):
            t = vl[:, tile] if tile < LT else vc[:, tile - LT]
            return t[:, head * P:(head + 1) * P]

        def unit_col(d, tile, head):
            return tile * 16 + d * 8 + head

        def src_of(p):
            w = {"merge": (w_proj_a, w_proj_b)[p.get("branch", 0)], "out": w_out, "mod": w_mod, "modg": w_mod}.get(p["kind"], w_in)
            return w[0, p["k0"] * P:(p["k0"] + p["nk"]) * P, p["col"]:p["col"] + p["width"]].rearrange(
                "(t p) n -> p t n", p=P)

        def part(t, p):
            return t[:, 0:p["nk"] * p["width"]]

        def part3(t, p):
            return part(t, p).rearrange("p (t n) -> p t n", n=p["width"])

        def raw_of(n):
            if n < NM:
                return raw_mod[n % 4], S(f"w_in_mod{n % 4}"), 16 * (n // 4 + 1)
            return raw[n % 2], S(f"w_in{n % 2}"), 16 * ((n - NM) // 2 + 1)

        def accs_free_needed(eng, gi):
            g = GROUPS[gi]
            if g["kind"] in ("mod", "modg"):
                k = gi if g["kind"] == "mod" else MODGS.index(gi)
                if k >= 2:
                    eng.wait_ge(S("mod_rows" if g["kind"] == "mod" else "modg_rows"), k - 1)
                if g["kind"] == "modg":
                    eng.wait_ge(S("a_tmp"), HEADS)
            if g["kind"] == "conv" and gi - G_CONV0 >= 2:
                eng.wait_ge(S("conv_raw"), 2 * (gi - G_CONV0 - 1))
            if g["kind"] == "ab":
                eng.wait_ge(S("v_evac"), 8)
            if g["kind"] == "bkv":
                eng.wait_ge(S("conv_raw"), 24)
            if g["kind"] == "gate":
                k = GATES.index(gi)
                if k < 2:
                    eng.wait_ge(S("kv_evac"), NT)
                else:
                    eng.wait_ge(S("gate_evac"), 2 * (k - 1))
            if g["kind"] == "bq":
                k = BQS.index(gi)
                if k == 0:
                    eng.wait_ge(S("gate_evac"), 2 * len(GATES))
                else:
                    eng.wait_ge(S("bq_evac"), 4)
            if g["kind"] == "merge" and g["branch"] == 0:
                if g["j"] == 1:
                    eng.wait_ge(S("grow_evac"), 4)
                if g["j"] >= 2:
                    eng.wait_ge(S("m_psum"), 2 * (g["j"] - 1))
            if g["kind"] == "out":
                k = g["j"]
                if k < 2:
                    eng.wait_ge(S("m_psum"), 14 + 2 * k)
                else:
                    eng.wait_ge(S("out_psum"), 4 * (k - 1))

        block = stack.enter_context(nc.Block())

        @block.sync
        def _(sp):
            sp.dma_start(consts[:], consts_in).then_inc(S("const_in"), 16)
            for r0, n, src in ((0, 16, c[0, :]), (16, 16, c_ctx), (32, 16, norm_w[0, :]), (48, 48, b_mod[0, :]),
                               (96, 1, a_norm_w[0, :])):
                sp.dma_start(rows[r0:r0 + n, :], src.rearrange("(t p) -> t p", p=P)).then_inc(S("rows_in"), 16)
            sp.dma_start(crows[:], conv_w[0].rearrange("t (c p) -> (t c) p", p=P)).then_inc(S("rows_in"), 16)
            for n, p in enumerate(PIECES):
                before = n - 4 if n < NM else n - 2
                if before >= (0 if n < NM else NM):
                    sp.wait_ge(S("w_hi"), before + 1)
                    sp.wait_ge(S("w_lo"), before + 1)
                place, loaded, _ = raw_of(n)
                sp.dma_start(part3(place, p), src_of(p)).then_inc(loaded, 16)
            for i in range(4):
                sp.wait_ge(S(f"out_dma{i}"), 16 * 4)

        @block.gpsimd
        def _(pool):
            for t in range(NT):
                if t >= 2:
                    pool.wait_ge(S("xt_ready"), 4 * (t - 1))
                src = x[0, t * P:(t + 1) * P, :] if t < LT else ctx[0, (t - LT) * P:(t - LT + 1) * P, :]
                pool.dma_start(xt[t % 2][:], src).then_inc(S(f"x_in{t % 2}"), 16)
            pool.dma_start(alog[:], a_log[0].rearrange("d h -> (d h)").partition_broadcast(P)).then_inc(S("alog_in"), 16)
            pool.dma_start(dtb[:], dt_bias[0].rearrange("d h -> (d h)").partition_broadcast(P)).then_inc(S("alog_in"), 16)
            pool.wait_ge(S("h_lo"), 2 * KT)
            for i in range(2):
                pool.memset(rawc[i][:], 0.0).then_inc(S("pads"), 1)
            pool.wait_ge(S("prep"), 1)
            pool.wait_ge(S("kv_spill"), 16 * NT)
            pool.wait_ge(S("w_used"), N_GATE0)
            pool.memset(SS[:], 0.0).then_inc(S("states0"), 1)
            for pi, pr in enumerate(PAIRS):
                for d in (0, 1):
                    for u in range(4):
                        col = unit_col(d, pr["tiles"][d], 4 * pr["half"] + u)
                        m = (LE, GE)[d]
                        ins = pool.tensor_scalar(GM[d][:, u, :], consts[:, m:m + P], gdec[:, col:col + 1], None, ALU.mult)
                    ins.then_inc(S(f"gm{d}"), 1)
                if pr["lat"] and not PAIRS[pi - 1]["lat"]:
                    for d in (0, 1):
                        pool.wait_ge(S(f"gd{d}"), pr["first"])
                    pool.memset(o_acc[:], 0.0).then_inc(S("oacc0"), 1)
                for d in (0, 1):
                    pool.wait_ge(S(f"gd{d}"), pr["first"] + 1)
                    m = (GE, LE)[d]
                    pool.tensor_tensor(DD[d][:], DD[d][:], consts[:, m:m + P].unsqueeze(1).to_broadcast([P, 4, P]),
                                       ALU.mult).then_inc(S(f"dmask{d}"), 1)

            for d in (0, 1):
                pool.wait_ge(S(f"gd{d}"), len(SLOTS))
            pool.dma_start(wrow[:, 0:P], q_norm_w[0].partition_broadcast(P)).then_inc(S("tab_in"), 16)
            pool.dma_start(wrow[:, P:2 * P], k_norm_w[0].partition_broadcast(P)).then_inc(S("tab_in"), 16)
            pool.dma_start(cs[:], rope_in.rearrange("(t p) n -> p t n", p=P)).then_inc(S("tab_in"), 16)
            for t in range(NT):
                pool.dma_start(kvr[:, t, :], kv_scr[t]).then_inc(S("kv_in"), 16)
            for i in range(2):
                pool.wait_ge(S(f"gate_spill{i}"), 16 * HEADS)

            def z_load(k):
                if k >= 2:
                    if k - 2 < HEADS:
                        pool.wait_ge(S("a_tmp"), k - 1)
                    else:
                        pool.wait_ge(S("b_tmp"), k - 1 - HEADS)
                pool.dma_start(zst[k % 2][:], gate_scr[k]).then_inc(S(f"z_in{k % 2}"), 16)

            def gates_load(m):
                if m >= 4:
                    pool.wait_ge(S("m_psum"), m - 3)
                for r in (0, 1):
                    pool.dma_start(gsig[m % 4][:, r, :], gate_scr[16 + 16 * r + m]).then_inc(S(f"gates_in{m % 4}"), 16)

            for k in range(HEADS + 2):
                z_load(k)
            pool.wait_ge(S("modg_cols"), 4)
            for i in range(2):
                pool.wait_ge(S(f"gate_spill{i}"), 16 * len(GATES))
            for k in range(4):
                pool.tensor_scalar(gcb[k][:], ones, GATE[:, k:k + 1], None, ALU.mult).then_inc(S("gcb"), 1)
            for k in range(HEADS + 2, 2 * HEADS):
                z_load(k)
            pool.wait_ge(S("qt_ready"), HEADS)
            for m in range(4):
                gates_load(m)
            for k in range(4, KT):
                pool.wait_ge(S("grow_mm"), k - 3)
                pool.tensor_scalar(gcb[k % 4][:], ones, GATE[:, k:k + 1], None, ALU.mult).then_inc(S("gcb"), 1)
            for m in range(4, KT):
                gates_load(m)
            pool.wait_ge(S("w_used"), N_OUT0)
            for t in range(LT):
                pool.dma_start(xr[:, t, :], x[0, t * P:(t + 1) * P, :]).then_inc(S("x_again"), 16)
            for j in range(4):
                for t in range(LT):
                    pool.wait_ge(S("out_ready"), 4 * j + t + 1)
                    pool.dma_start(out[0, t * P:(t + 1) * P, 512 * j:512 * j + 512], ost[t][:]).then_inc(
                        S(f"out_dma{t}"), 16)

        @block.scalar
        def _(act):
            link = [0]

            def ln(ins):
                link[0] += 1
                ins.then_inc(S("act_chain"), 1)
                act.wait_ge(S("act_chain"), link[0])

            def hi_part(n):
                if n >= NP:
                    return
                p = PIECES[n]
                place, loaded, count = raw_of(n)
                act.wait_ge(loaded, count)
                if n >= 2:
                    act.wait_ge(S("w_used"), n - 1)
                act.activation(part(whi[n % 2], p), part(place, p), ACT.Copy).then_inc(S("w_hi"), 1)

            def x_square(t):
                act.wait_ge(S(f"x_in{t % 2}"), 16 * (t // 2 + 1))
                if t > 0:
                    act.wait_ge(S("x_ssq"), t)
                act.activation(junk[:], xt[t % 2][:], ACT.Square, accum_out=stat[:, t:t + 1]).then_inc(S("x_ssq"), 1)

            def x_std(t):
                act.wait_ge(S("x_var"), t + 1)
                act.activation(stat[:, 8 + t:9 + t], stat[:, t:t + 1], ACT.Sqrt).then_inc(S("x_std"), 1)

            def x_columns(t):
                for q4 in range(4):
                    n = 4 * t + q4
                    act.wait_ge(S("xt_ready"), n + 1)
                    act.activation(xnT[:, 4 * q4:4 * q4 + 4, t * P:(t + 1) * P], bank4(n % 4), ACT.Copy).then_inc(
                        S("xt_evac"), 1)

            def h_hi_parts(j):
                for k in range(4 * j, 4 * j + 4):
                    act.wait_ge(S("h_ready"), k + 1)
                    act.activation(h_hi[:, k, :], xnT[:, k, 0:SEQ], ACT.Copy)
                    act.activation(hc_hi[:, k, :], xnT[:, k, SEQ:TOK], ACT.Copy).then_inc(S("h_hi"), 1)

            def conv_raw(ci):
                it = ITEMS[ci]
                g = CONVS[it["g"]]
                act.wait_ge(S("w_used"), g["last"] + 1)
                if ci == 0:
                    act.wait_ge(S("pads"), 2)
                if ci >= 2:
                    act.wait_ge(S("conv_done"), ci - 1)
                b0 = 3 * (it["g"] % 2)
                lat = act.activation(rawc[ci % 2][:, 2:2 + SEQ], bank(b0 + it["j"]), ACT.Copy)
                if it["what"] == "q":
                    lat.then_inc(S("conv_raw"), 1)
                else:
                    act.activation(rawc[ci % 2][:, 518:774], bank(b0 + 2, 256, 256 * it["j"]), ACT.Copy).then_inc(
                        S("conv_raw"), 1)

            def conv_silu(ci):
                it = ITEMS[ci]
                act.wait_ge(S("conv_done"), ci + 1)
                a = acc[ci % 2]
                if it["what"] == "v":
                    act.activation(a[:], a[:], ACT.Silu).then_inc(S("item_ready"), 1)
                    return
                h = it["head"]
                dst = qT if it["what"] == "q" else kTl
                ln(act.activation(dst[:, h, :], a[:, 0:SEQ], ACT.Silu))
                if it["what"] == "k":
                    ln(act.activation(kTc[:, h, :], a[:, 516:772], ACT.Silu))
                    ln(act.activation(a[:, 516:772], kTc[:, h, :], ACT.Square))
                act.activation(a[:, 0:SEQ], dst[:, h, :], ACT.Square).then_inc(S("item_ready"), 1)

            def gdn(slot):
                k, n, pr = slot["kind"], slot["n"], PAIRS[slot["pair"]]
                for d in (0, 1):
                    ps = bank4(4 + 2 * d + slot["i"] % 2)
                    done = S(f"gd{d}")
                    if k == "correct" and n == len(BLOCKS) - 1:
                        act.wait_ge(S(f"gy{d}"), slot["pair"] + 1)
                        for u in range(4):
                            col = unit_col(d, pr["tiles"][d], 4 * pr["half"] + u)
                            ins = act.activation(XX[d][:, u, :], YY[d][:, u, :], ACT.Copy, scale=betar[:, col:col + 1])
                        ins.then_inc(done, 1)
                        continue
                    act.wait_ge(S(f"gp{d}"), slot["i"] + 1)
                    if k == "decay":
                        act.activation(DD[d][:], ps, ACT.Exp).then_inc(done, 1)
                    elif k == "flip":
                        act.activation(XX[d][:], ps, ACT.Copy).then_inc(done, 1)
                    elif k == "at":
                        act.activation(YY[d][:], ps, ACT.Copy).then_inc(done, 1)
                    elif k == "z":
                        act.activation(ZZ[d][:], ps, ACT.Copy).then_inc(done, 1)
                    elif k == "kt":
                        for u in range(4):
                            h, tile = 4 * pr["half"] + u, pr["tiles"][d]
                            ins = act.activation(LL[d][:, u, :], ps[:, u, :], ACT.Copy,
                                                 scale=DEC[:, tile * 2 + d, 1, h:h + 1])
                        ins.then_inc(done, 1)

            def bq_rows(j):
                act.wait_ge(S("w_used"), GROUPS[BQS[j]]["last"] + 1)
                act.wait_ge(S("a_lo"), HEADS)
                for t in range(LT):
                    act.activation(bqr[:, t, 512 * j:512 * j + 512], bank(t), ACT.Copy).then_inc(S("bq_evac"), 1)

            spills = [0]
            def square(i, src):
                act.activation(sqj[:], src, ACT.Square, accum_out=ssq_a[:, i:i + 1]).then_inc(S("qk_ssq"), 1)
                squares[0] += 1
                act.wait_ge(S("qk_ssq"), squares[0])

            squares = [0]

            def modg_rows(k):
                act.wait_ge(S("w_used"), GROUPS[MODGS[k]]["last"] + 1)
                if k == 0:
                    for i in range(2):
                        act.wait_ge(S(f"gate_spill{i}"), 16 * len(GATES))
                else:
                    act.wait_ge(S("modg_cols_mm"), k)
                act.activation(mrow_g[:], bank(4 + k % 2)[0:4], ACT.Copy).then_inc(S("modg_rows"), 1)

            def q_squares(j):
                for t in range(LT):
                    for h in range(4):
                        square(16 * j + 4 * t + h, bqr[:, t, (4 * j + h) * P:(4 * j + h + 1) * P])

            def qk_std(step, a0, a1):
                act.wait_ge(S("qk_var"), step)
                act.activation(ssq_a[:, a0:a1], ssq_a[:, a0:a1], ACT.Sqrt).then_inc(S("qk_std"), 1)

            hi_part(0)
            act.wait_ge(S("cols"), 2)
            act.activation(sc2[:], cols[:, 0:32].rearrange("p (v k) -> p v k", v=2), ACT.Silu).then_inc(S("silu_c"), 1)
            act.wait_ge(S("silu_c"), 1)
            act.activation(c4[:].rearrange("p k (v e) -> p v k e", e=2)[:, :, :, 0], sc2[:], ACT.Copy).then_inc(S("c_hi"), 1)
            for n in range(N_MERGE0):
                p = PIECES[n]
                hi_part(n + 1)
                for t in range(NT):
                    if n == 2 + 2 * t:
                        x_square(t)
                    if n == 3 + 2 * t:
                        x_std(t)
                    if n == 5 + 2 * t:
                        x_columns(t)
                for gi, g in enumerate(MODS):
                    if n == g["last"] + 1:
                        act.wait_ge(S("w_used"), n)
                        if gi:
                            act.wait_ge(S("mod_cols_mm"), gi)
                        act.activation(mrow[:], bank(4 + gi % 2)[0:4], ACT.Copy).then_inc(S("mod_rows"), 1)
                    if n == g["last"] + 3 and g["scale"]:
                        h_hi_parts(g["j"])
                r = n - N_FIN
                if r == 0:
                    for d in (0, 1):
                        act.wait_ge(S(f"gd{d}"), len(SLOTS))
                if 0 <= r < LT:
                    for h in range(HEADS):
                        k = 8 * r + h
                        if k:
                            act.wait_ge(S("o_ssq"), k)
                        act.activation(sqj[:], o_acc[:, r, h * P:(h + 1) * P], ACT.Square,
                                       accum_out=ssq_o[:, k:k + 1]).then_inc(S("o_ssq"), 1)
                if r == 4:
                    act.wait_ge(S("o_var"), 1)
                    act.activation(ssq_o[:], ssq_o[:], ACT.Sqrt).then_inc(S("o_std"), 1)
                    act.wait_ge(S("kv_in"), 16 * NT)
                    for t in range(NT):
                        for kv in range(KV):
                            square(32 + 2 * t + kv, kvr[:, t, kv * P:(kv + 1) * P])
                    qk_std(1, 32, 44)
                if 7 <= r < 11:
                    for h in (2 * (r - 7), 2 * (r - 7) + 1):
                        act.wait_ge(S("a_tmp"), h + 1)
                        act.activation(a_hi[:, h, :], atmp[h % 2][:], ACT.Copy).then_inc(S("a_hi"), 1)
                if n == GROUPS[BQS[0]]["last"] + 1:
                    bq_rows(0)
                if n == GROUPS[BQS[0]]["last"] + 4:
                    q_squares(0)
                    qk_std(2, 0, 16)
                for k, gi in enumerate(MODGS):
                    if n == GROUPS[gi]["last"] + 1:
                        modg_rows(k)
                for gi, g in enumerate(CONVS):
                    e = n - g["last"]
                    if e == 1:
                        conv_raw(2 * gi)
                        conv_raw(2 * gi + 1)
                    if e in (2, 3):
                        conv_silu(2 * gi + e - 2)
                if n == GROUPS[G_BKV]["first"] + 4:
                    act.wait_ge(S("w_used"), GROUPS[G_AB]["last"] + 1)
                    ab = bank(6, NT * 32).rearrange("p (t c) -> p t c", t=NT)
                    act.activation(beta[:].rearrange("p (t c) -> p t c", t=NT), ab[:, :, 0:16], ACT.Sigmoid).then_inc(
                        S("beta"), 1)
                    act.wait_ge(S("negabs"), 1)
                    ln(act.activation(ab_t[1][:], ab_t[1][:], ACT.Exp))
                    ln(act.activation(ab_t[2][:], ab_t[1][:], ACT.Ln, bias=1.0))
                    act.wait_ge(S("alog_in"), 32)
                    act.activation(alog[:], alog[:], ACT.Exp).then_inc(S("ab_exp"), 1)
                    act.wait_ge(S("ssq_eps"), 1)
                    ln(act.activation(rk[:], rk[:], ACT.Sqrt))
                    act.activation(rq[:], rq[:], ACT.Sqrt).then_inc(S("ssq_std"), 1)
                    act.wait_ge(S("cum"), 1)
                    act.activation(DEC[:].rearrange("p a b c -> p (a b c)"), bank(6, NT * 2 * 24), ACT.Exp).then_inc(
                        S("decays"), 1)
                if n == N_GATE0:
                    g = GROUPS[G_BKV]
                    for t in range(NT):
                        if t == 0:
                            act.wait_ge(S("w_used"), g["last"] + 1)
                            act.wait_ge(S("conv_done"), 24)
                            act.wait_ge(S("prep"), 1)
                        act.activation(kvst[t][:], bank(t), ACT.Copy).then_inc(S("kv_evac"), 1)
                    for t in range(NT):
                        act.wait_ge(S("kv_evac"), t + 1)
                        act.dma_start(kv_scr[t], kvst[t][:]).then_inc(S("kv_spill"), 16)
                for q in range(4):
                    s = slot_at(n, q)
                    if s and (s["kind"] in ON_SCALAR or (s["kind"] == "correct" and s["n"] == len(BLOCKS) - 1)):
                        gdn(s)
                    pg = PIECES[n - 1]["g"] if n else 0
                    if q in (0, 2) and n and GROUPS[pg]["kind"] == "gate" and n - 1 == GROUPS[pg]["last"]:
                        j = q // 2
                        k = spills[0]
                        spills[0] += 1
                        row = GROUPS[pg]["row"] + j
                        if j == 0:
                            act.wait_ge(S("w_used"), n)
                        if k == 0:
                            act.wait_ge(S("kv_spill"), 16 * NT)
                        if k >= 2:
                            act.wait_ge(S(f"gate_spill{k % 2}"), 16 * (k // 2))
                        act.activation(gst[k % 2][:], bank(2 * (GATES.index(pg) % 2) + j),
                                       ACT.Silu if row < 16 else ACT.Sigmoid).then_inc(S("gate_evac"), 1)
                        act.wait_ge(S("gate_evac"), k + 1)
                        act.dma_start(gate_scr[row], gst[k % 2][:]).then_inc(S(f"gate_spill{k % 2}"), 16)
            bq_rows(1)
            modg_rows(3)

            def q_columns(h, b):
                act.wait_ge(S("qt_ready"), h + 1)
                act.activation(qhT[:, h, :], bank(b), ACT.Copy).then_inc(S("qt_evac"), 1)

            for h in range(4):
                q_columns(h, h)
            for kv in range(KV):
                act.wait_ge(S("kt_ready"), kv + 1)
                act.activation(khT[:, kv, :], PS[:, (4 + 2 * kv) * 512:(4 + 2 * kv) * 512 + TOK], ACT.Copy).then_inc(
                    S("kt_evac"), 1)

            def att_exp(i):
                act.wait_ge(S("negmax"), i + 1)
                if i >= 2:
                    act.wait_ge(S("pt_ready"), i - 1)
                act.activation(probs[i % 2][:], PS[:, (i % 2) * 1024:(i % 2) * 1024 + TOK], ACT.Exp,
                               bias=nmax[:, i:i + 1], scale=HD ** -0.5, accum_out=rsum[:, i:i + 1]).then_inc(
                    S("exp_done"), 1)

            att_exp(0)
            for i in range(32):
                if i < 31:
                    att_exp(i + 1)
                h, qt = divmod(i, 4)
                if qt == 0 and h >= 1:
                    act.wait_ge(S("pv_done"), h)
                act.wait_ge(S("pt_ready"), i + 1)
                act.activation(PTt[:, :, qt * P:(qt + 1) * P],
                               PS[:, 2048:2048 + TOK].rearrange("p (t n) -> p t n", t=NT), ACT.Copy).then_inc(
                    S("pt_evac"), 1)
                if i == 1:
                    q_squares(1)
                if i == 2:
                    qk_std(3, 16, 32)
                if qt == 2 and 3 <= h < 7:
                    q_columns(h + 1, 6 + (h + 1) % 2)
                if qt == 1 and h >= 1:
                    act.wait_ge(S("b_tmp"), h)
                    act.activation(b_hi[:, h - 1, :], btmp[:], ACT.Copy).then_inc(S("b_hi"), 1)
            act.wait_ge(S("b_tmp"), HEADS)
            act.activation(b_hi[:, HEADS - 1, :], btmp[:], ACT.Copy).then_inc(S("b_hi"), 1)
            for n in range(N_MERGE0, NP):
                hi_part(n + 1)
                for j in (n - N_MERGE0 - 4,):
                    if j >= 0 and j % 4 == 0 and j // 4 < 8:
                        for jj in (0, 1):
                            m = 2 * (j // 4) + jj
                            act.wait_ge(S("m_tmp"), m + 1)
                            act.activation(m_hi[:, m, :], mtmp[2 * (m % 2)][:], ACT.Copy).then_inc(S("m_hi"), 1)

        @block.vector
        def _(dve):
            link = [0]

            def ln(ins):
                link[0] += 1
                ins.then_inc(S("dve_chain"), 1)
                dve.wait_ge(S("dve_chain"), link[0])

            def lo_part(n):
                if n >= NP:
                    return
                dve.wait_ge(S("w_hi"), n + 1)
                p = PIECES[n]
                dve.tensor_tensor(part(wlo[n % 2], p), part(raw_of(n)[0], p), part(whi[n % 2], p).bitcast(f32),
                                  ALU.subtract).then_inc(S("w_lo"), 1)

            dve.wait_ge(S("rowsT"), 2)
            dve.tensor_copy(cols[:], bank(7, 97)).then_inc(S("cols"), 1)
            dve.tensor_copy(convw[:], bank(6, 120)).then_inc(S("cols"), 1)
            dve.wait_ge(S("c_hi"), 1)
            cp = c4[:].rearrange("p k (v e) -> p v k e", e=2)
            dve.tensor_tensor(cp[:, :, :, 1], sc2[:], cp[:, :, :, 0].bitcast(f32), ALU.subtract).then_inc(S("c_lo"), 1)

            def x_var(t):
                dve.wait_ge(S("x_ssq"), t + 1)
                dve.tensor_scalar(stat[:, t:t + 1], stat[:, t:t + 1], 1.0 / DM, EPS, ALU.mult, ALU.add).then_inc(
                    S("x_var"), 1)

            def x_norm(t):
                dve.wait_ge(S("x_std"), t + 1)
                ln(dve.reciprocal(stat[:, 8 + t:9 + t], stat[:, 8 + t:9 + t]))
                dve.tensor_scalar(xt[t % 2][:], xt[t % 2][:], stat[:, 8 + t:9 + t], None, ALU.mult).then_inc(
                    S("xn"), 1)

            def mod_columns(gi):
                g = MODS[gi]
                k0 = 4 * g["j"]
                dve.wait_ge(S("mod_cols_mm"), gi + 1)
                src = bank(6 + gi % 2, 8).rearrange("p (k v) -> p k v", v=2)
                off = 48 + 16 * g["scale"] + k0
                b = cols[:, off:off + 4].unsqueeze(2).to_broadcast([P, 4, 2])
                dst = modv[:, g["scale"], k0:k0 + 4, :]
                if not g["scale"]:
                    dve.tensor_tensor(dst, src, b, ALU.add).then_inc(S("mod_evac"), 1)
                    return
                dve.tensor_tensor(dst, src, b, ALU.add).then_inc(S("mod_evac"), 1)
                dve.wait_ge(S("mod_evac"), gi + 1)
                ln(dve.scalar_tensor_tensor(out=dst, in0=dst, scalar=1.0,
                                            in1=cols[:, 32 + k0:36 + k0].unsqueeze(2).to_broadcast([P, 4, 2]),
                                            op0=ALU.add, op1=ALU.mult))
                dve.wait_ge(S("xt_evac"), 4 * NT)
                for k in range(k0, k0 + 4):
                    for v, (a0, a1) in enumerate(((0, SEQ), (SEQ, TOK))):
                        ins = dve.tensor_scalar(xnT[:, k, a0:a1], xnT[:, k, a0:a1], modv[:, 1, k, v:v + 1],
                                                modv[:, 0, k, v:v + 1], ALU.mult, ALU.add)
                    ins.then_inc(S("h_ready"), 1)

            def h_lo_parts(j):
                for k in range(4 * j, 4 * j + 4):
                    dve.wait_ge(S("h_hi"), k + 1)
                    dve.tensor_tensor(h_lo[:, k, :], xnT[:, k, 0:SEQ], h_hi[:, k, :].bitcast(f32),
                                      ALU.subtract).then_inc(S("h_lo"), 1)
                    dve.tensor_tensor(hc_lo[:, k, :], xnT[:, k, SEQ:TOK], hc_hi[:, k, :].bitcast(f32),
                                      ALU.subtract).then_inc(S("h_lo"), 1)

            def conv(ci):
                it = ITEMS[ci]
                dve.wait_ge(S("conv_raw"), ci + 1)
                if ci >= 2:
                    dve.wait_ge(S("item_pe"), ci - 1)
                ct = {"q": 0, "k": 8, "v": 16}[it["what"]] + it["head"]
                a, r = acc[ci % 2], rawc[ci % 2]
                for tap in range(CONV):
                    w = convw[:, tap * 24 + ct:tap * 24 + ct + 1]
                    if tap == 0:
                        ln(dve.tensor_scalar(a[:], r[:, 0:772], w, None, ALU.mult))
                    else:
                        ins = dve.scalar_tensor_tensor(out=a[:], in0=r[:, tap:tap + 772], scalar=w, in1=a[:],
                                                       op0=ALU.mult, op1=ALU.add)
                        if tap < CONV - 1:
                            ln(ins)
                        else:
                            ins.then_inc(S("conv_done"), 1)

            def v_rows(ci):
                vi = ci - 8
                h = ITEMS[ci]["head"]
                dve.wait_ge(S("item_pe"), ci + 1)
                dve.tensor_copy(vl[:, :, h * P:(h + 1) * P], bank4(6))
                dve.tensor_copy(vc[:, :, h * P:(h + 1) * P], bank(7, 256, 128).rearrange("p (t n) -> p t n", t=CT)).then_inc(
                    S("v_evac"), 1)

            def gdn(slot):
                k, n, pr = slot["kind"], slot["n"], PAIRS[slot["pair"]]
                half = pr["half"]
                for d in (0, 1):
                    tile = pr["tiles"][d]
                    b = 4 + 2 * d + slot["i"] % 2
                    ps = bank4(b)
                    done = S(f"gd{d}")
                    dve.wait_ge(S(f"gp{d}"), slot["i"] + 1)
                    if k == "gram":
                        dve.wait_ge(S(f"dmask{d}"), slot["pair"] + 1)
                        for u in range(4):
                            col = unit_col(d, tile, 4 * half + u)
                            ins = dve.scalar_tensor_tensor(out=LL[d][:, u, :], in0=ps[:, u, :], scalar=crow[:, col:col + 1],
                                                           in1=DD[d][:, u, :], op0=ALU.mult, op1=ALU.mult)
                        ins.then_inc(done, 1)
                    elif k == "qk":
                        dve.tensor_tensor(DD[d][:], ps, DD[d][:], ALU.mult).then_inc(done, 1)
                    elif k == "couple":
                        if n == len(BLOCKS) - 1:
                            r0 = 64 * d
                            dve.tensor_copy(PM[d][r0:r0 + 64], bank4(b, 64)[r0:r0 + 64]).then_inc(done, 1)
                            continue
                        mo = STAGE + (2 * n + d) * 64
                        mask = consts[:, mo:mo + 64].unsqueeze(1).to_broadcast([P, 4, 64])
                        ins = dve.tensor_tensor(PM[d][:], bank4(b, 64), mask, ALU.mult)
                        if n > 0:
                            ins.then_inc(done, 1)
                            continue
                        ln(ins)
                        for e in (0, 1):
                            iv = odd1(ident, 1, d, e).unsqueeze(1).to_broadcast([P, 4, 64, 1])
                            yv = YY[d][:].rearrange("p u (b e s) -> p u b e s", e=2, s=1)[:, :, :, e, :]
                            if e == (0 if d else 1):
                                last = dve.tensor_tensor(yv, iv, PM[d][:].unsqueeze(3), ALU.subtract)
                            else:
                                last = dve.tensor_copy(yv, iv)
                            if e == 0:
                                ln(last)
                        last.then_inc(done, 1)
                    elif k == "correct":
                        if n == len(BLOCKS) - 1:
                            r0, c0 = 64 * d, 64 * (1 - d)
                            yv = YY[d][r0:r0 + 64, :, c0:c0 + 64]
                            dve.tensor_tensor(yv, yv, bank4(b, 64)[r0:r0 + 64], ALU.subtract).then_inc(S(f"gy{d}"), 1)
                            continue
                        yv = odd(YY[d][:], BLOCKS[n], d)
                        pv = bank4(b, 64).rearrange("p u (b s) -> p u b s", s=BLOCKS[n])
                        ins = dve.tensor_tensor(yv, yv, pv, ALU.subtract)
                        ins.then_inc(done, 1)
                    elif k == "ks":
                        for u in range(4):
                            h = 4 * half + u
                            col = unit_col(d, tile, h)
                            ins = dve.scalar_tensor_tensor(out=RR[d][:, u, :], in0=ps[:, u, :], scalar=ngr[:, col:col + 1],
                                                           in1=v_of(h, tile), op0=ALU.mult, op1=ALU.add)
                        ins.then_inc(done, 1)
                    elif k == "qs":
                        if slot["pair"] == 2 * CT:
                            dve.wait_ge(S("oacc0"), 1)
                        for u in range(4):
                            h = 4 * half + u
                            o = o_acc[:, tile, h * P:(h + 1) * P]
                            ins = dve.scalar_tensor_tensor(out=o, in0=ps[:, u, :], scalar=DEC[:, tile * 2 + d, 0, h:h + 1],
                                                           in1=o, op0=ALU.mult, op1=ALU.add)
                        ins.then_inc(done, 1)
                    elif k == "az":
                        o = o_acc[:, tile, 4 * half * P:(4 * half + 4) * P].rearrange("p (u n) -> p u n", u=4)
                        dve.tensor_tensor(o, ps, o, ALU.add).then_inc(done, 1)
                    elif k == "kz":
                        for u in range(4):
                            h = 4 * half + u
                            s = SS[:, d, h, :]
                            ins = dve.scalar_tensor_tensor(out=s, in0=s, scalar=DEC[:, tile * 2 + d, 2, h:h + 1],
                                                           in1=ps[:, u, :], op0=ALU.mult, op1=ALU.add)
                        ins.then_inc(done, 1)

            def out_rows(j):
                dve.wait_ge(S("w_used"), GROUPS[OUTS[j]]["last"] + 1)
                dve.wait_ge(S("x_again"), 16 * LT)
                for t in range(LT):
                    if j:
                        dve.wait_ge(S(f"out_dma{t}"), 16 * j)
                    dve.tensor_tensor(ost[t][:], bank(4 * (j % 2) + t), grow[:, 512 * j:512 * j + 512], ALU.mult).then_inc(
                        S("out_psum"), 1)
                    dve.wait_ge(S("out_psum"), 4 * j + t + 1)
                    dve.tensor_tensor(ost[t][:], ost[t][:], xr[:, t, 512 * j:512 * j + 512], ALU.add).then_inc(
                        S("out_ready"), 1)

            def y_rows():
                dve.wait_ge(S("o_std"), 1)
                ln(dve.reciprocal(ssq_o[:], ssq_o[:]))
                ln(dve.tensor_tensor(ssq_o[:], ssq_o[:], rq[:], ALU.mult))
                for t in range(LT):
                    o = o_acc[:, t, :].rearrange("p (h n) -> p h n", h=8)
                    dve.tensor_tensor(o, o, ssq_o[:, 8 * t:8 * t + 8].unsqueeze(2).to_broadcast([P, 8, P]),
                                      ALU.mult).then_inc(S("y_ready"), 1)

            def a_columns(h):
                dve.wait_ge(S("yt_ready"), h + 1)
                dve.wait_ge(S(f"z_in{h % 2}"), 16 * (h // 2 + 1))
                if h >= 2:
                    dve.wait_ge(S("a_lo"), h - 1)
                dve.scalar_tensor_tensor(out=atmp[h % 2][:], in0=bank(4 + h % 4), scalar=cols[:, 96:97], in1=zst[h % 2][:],
                                         op0=ALU.mult, op1=ALU.mult).then_inc(S("a_tmp"), 1)

            def a_lo_part(h):
                dve.wait_ge(S("a_hi"), h + 1)
                dve.tensor_tensor(a_lo[:, h, :], atmp[h % 2][:], a_hi[:, h, :].bitcast(f32), ALU.subtract).then_inc(
                    S("a_lo"), 1)

            def rope_tables():
                dve.wait_ge(S("tab_in"), 48)
                for w0, tab in ((0, qtab), (128, ktab)):
                    for hf in (0, 1):
                        wv = wrow[:, w0 + 64 * hf:w0 + 64 * hf + 64].unsqueeze(1).to_broadcast([P, LT, 64])
                        for sn in (0, 1):
                            ln(dve.tensor_tensor(tab[:, :, 128 * hf + 64 * sn:128 * hf + 64 * sn + 64],
                                                 cs[:, :, 64 * sn:64 * sn + 64], wv, ALU.mult))

            def rope(rows_t, tab_t, nh):
                x1, x2 = rows_t[:, :, 0:64], rows_t[:, :, 64:128]
                tv = lambda k: tab_t[:, 64 * k:64 * k + 64].unsqueeze(1).to_broadcast([P, nh, 64])
                ln(dve.tensor_tensor(rt[0][:, 0:nh, :], x1, tv(0), ALU.mult))
                ln(dve.tensor_tensor(rt[1][:, 0:nh, :], x2, tv(3), ALU.mult))
                ln(dve.tensor_tensor(rt[2][:, 0:nh, :], x1, tv(1), ALU.mult))
                ln(dve.tensor_tensor(rt[3][:, 0:nh, :], x2, tv(2), ALU.mult))
                ln(dve.tensor_tensor(x1, rt[0][:, 0:nh, :], rt[1][:, 0:nh, :], ALU.subtract))
                return dve.tensor_tensor(x2, rt[2][:, 0:nh, :], rt[3][:, 0:nh, :], ALU.add)

            def qk_var(count, a0, a1):
                dve.wait_ge(S("qk_ssq"), count)
                dve.tensor_scalar(ssq_a[:, a0:a1], ssq_a[:, a0:a1], 1.0 / P, EPS, ALU.mult, ALU.add).then_inc(
                    S("qk_var"), 1)

            def qk_rstd(step, a0, a1):
                dve.wait_ge(S("qk_std"), step)
                ln(dve.reciprocal(ssq_a[:, a0:a1], ssq_a[:, a0:a1]))

            def q_tile(j, t):
                rv = bqr[:, t, 512 * j:512 * j + 512].rearrange("p (h n) -> p h n", h=4)
                sv = ssq_a[:, 16 * j + 4 * t:16 * j + 4 * t + 4].unsqueeze(2).to_broadcast([P, 4, P])
                ln(dve.tensor_tensor(rv, rv, sv, ALU.mult))
                rope(rv, qtab[:, t, :], 4).then_inc(S("q_rot"), 1)
                dve.wait_ge(S("q_rot"), 4 * j + t + 1)

            def k_tile(t):
                rv = kvr[:, t, 0:256].rearrange("p (h n) -> p h n", h=2)
                sv = ssq_a[:, 32 + 2 * t:34 + 2 * t].unsqueeze(2).to_broadcast([P, 2, P])
                ln(dve.tensor_tensor(rv, rv, sv, ALU.mult))
                if t < LT:
                    ln(rope(rv, ktab[:, t, :], 2))
                else:
                    ins = dve.tensor_tensor(rv, rv, wrow[:, 128:256].unsqueeze(1).to_broadcast([P, 2, P]), ALU.mult)
                    ins.then_inc(S("k_ctx_rows"), 1)

            def modg_columns(k):
                dve.wait_ge(S("modg_cols_mm"), k + 1)
                src = bank(6 + k % 2, 8).rearrange("p (k v) -> p k v", v=2)[:, :, 0]
                dve.tensor_tensor(GATE[:, 4 * k:4 * k + 4], src, cols[:, 80 + 4 * k:84 + 4 * k], ALU.add).then_inc(
                    S("modg_cols"), 1)

            lo_part(0)
            for n in range(N_MERGE0):
                lo_part(n + 1)
                for t in range(NT):
                    if n == 3 + 2 * t:
                        x_var(t)
                    if n == 4 + 2 * t:
                        x_norm(t)
                for gi, g in enumerate(MODS):
                    if n == g["last"] + 2:
                        mod_columns(gi)
                    if n == g["last"] + 3 and g["scale"]:
                        h_lo_parts(g["j"])
                r = n - N_FIN
                if r == 4:
                    dve.wait_ge(S("o_ssq"), 32)
                    ln(dve.tensor_tensor(ssq_o[:], ssq_o[:], rq[:], ALU.mult))
                    ln(dve.tensor_tensor(ssq_o[:], ssq_o[:], rq[:], ALU.mult))
                    dve.tensor_scalar(ssq_o[:], ssq_o[:], 1.0 / P, EPS, ALU.mult, ALU.add).then_inc(S("o_var"), 1)
                    qk_var(12, 32, 44)
                if r == 5:
                    y_rows()
                if r == 6:
                    qk_rstd(1, 32, 44)
                    rope_tables()
                if 7 <= r < 11:
                    for h in (2 * (r - 7), 2 * (r - 7) + 1):
                        a_columns(h)
                    for h in (2 * (r - 7), 2 * (r - 7) + 1):
                        a_lo_part(h)
                if 11 <= r < 13:
                    for t in range(3 * (r - 11), 3 * (r - 11) + 3):
                        k_tile(t)
                if n == GROUPS[BQS[0]]["last"] + 4:
                    qk_var(28, 0, 16)
                if n == GROUPS[BQS[0]]["last"] + 5:
                    qk_rstd(2, 0, 16)
                for t in range(LT):
                    if n == GROUPS[BQS[0]]["last"] + 6 + 3 * t:
                        q_tile(0, t)
                for k, gi in enumerate(MODGS):
                    if n == GROUPS[gi]["last"] + 2:
                        modg_columns(k)
                for gi, g in enumerate(CONVS):
                    e = n - g["last"]
                    if e in (1, 2):
                        conv(2 * gi + e - 1)
                    if e in (3, 4) and g["what"] == "v":
                        v_rows(2 * gi + e - 3)
                if n == GROUPS[G_BKV]["first"] + 4:
                    dve.wait_ge(S("w_used"), GROUPS[G_AB]["last"] + 1)
                    dve.wait_ge(S("beta"), 1)
                    ab = bank(6, NT * 32).rearrange("p (t c) -> p t c", t=NT)
                    v3 = lambda t: t[:].rearrange("p (t c) -> p t c", t=NT)
                    dve.wait_ge(S("alog_in"), 32)
                    dve.wait_ge(S("item_pe"), 24)
                    ln(dve.tensor_tensor(v3(ab_t[0]), ab[:, :, 16:32], dtb[:].unsqueeze(1).to_broadcast([P, NT, 16]), ALU.add))
                    ln(dve.tensor_scalar(ab_t[1][:], ab_t[0][:], -1.0, None, ALU.mult))
                    dve.tensor_tensor(ab_t[1][:], ab_t[0][:], ab_t[1][:], ALU.min).then_inc(S("negabs"), 1)
                    dve.wait_ge(S("ab_exp"), 1)
                    ln(dve.tensor_scalar(ab_t[3][:], ab_t[1][:], 1.0, None, ALU.add))
                    ln(dve.tensor_scalar(ab_t[3][:], ab_t[3][:], -1.0, None, ALU.add))
                    ln(dve.tensor_scalar(ab_t[4][:], ab_t[3][:], 0.0, None, ALU.is_equal))
                    ln(dve.tensor_tensor(ab_t[2][:], ab_t[2][:], ab_t[4][:], ALU.add))
                    ln(dve.tensor_tensor(ab_t[3][:], ab_t[3][:], ab_t[4][:], ALU.add))
                    ln(dve.reciprocal(ab_t[3][:], ab_t[3][:]))
                    ln(dve.tensor_tensor(ab_t[1][:], ab_t[1][:], ab_t[2][:], ALU.mult))
                    ln(dve.tensor_tensor(ab_t[1][:], ab_t[1][:], ab_t[3][:], ALU.mult))
                    ln(dve.scalar_tensor_tensor(out=ab_t[0][:], in0=ab_t[0][:], scalar=0.0, in1=ab_t[1][:],
                                                op0=ALU.max, op1=ALU.add))
                    dve.scalar_tensor_tensor(out=v3(gdec), in0=v3(ab_t[0]), scalar=-1.0,
                                             in1=alog[:].unsqueeze(1).to_broadcast([P, NT, 16]),
                                             op0=ALU.mult, op1=ALU.mult).then_inc(S("g_ready"), 1)
                    dve.wait_ge(S("item_pe"), 24)
                    ln(dve.tensor_scalar(rk[:], bank(7, 48), EPS, None, ALU.add))
                    dve.tensor_scalar(rq[:], bank(7, 32, 48), EPS, None, ALU.add).then_inc(S("ssq_eps"), 1)
                    dve.wait_ge(S("ssq_std"), 1)
                    ln(dve.reciprocal(rk[:], rk[:]))
                    ln(dve.reciprocal(rq[:], rq[:]))
                    ln(dve.tensor_scalar(rq[:], rq[:], float(HD ** -0.5), None, ALU.mult))
                    v4 = lambda t: t[:].rearrange("p (t d h) -> p t d h", t=NT, d=2)
                    rkb = rk[:].rearrange("p (t h) -> p t h", t=NT).unsqueeze(2).to_broadcast([P, NT, 2, 8])
                    ln(dve.tensor_tensor(v4(betar), v4(beta), rkb, ALU.mult))
                    ln(dve.tensor_tensor(v4(crow), v4(betar), rkb, ALU.mult))
                    dve.wait_ge(S("decays"), 1)
                    ln(dve.tensor_scalar(ngr[:].rearrange("p (a h) -> p a h", h=8), DEC[:, :, 0, :], -1.0, None, ALU.mult))
                    dve.tensor_tensor(v4(ngr), v4(ngr), rkb, ALU.mult).then_inc(S("prep"), 1)
                for q in range(4):
                    s = slot_at(n, q)
                    if s and s["kind"] not in ON_SCALAR:
                        gdn(s)
            modg_columns(3)

            def att_max(i):
                dve.wait_ge(S("sc_ready"), i + 1)
                ln(dve.reduce_max(nmax[:, i:i + 1], PS[:, (i % 2) * 1024:(i % 2) * 1024 + TOK], axis=AX.X))
                dve.tensor_scalar(nmax[:, i:i + 1], nmax[:, i:i + 1], -float(HD ** -0.5), None, ALU.mult).then_inc(
                    S("negmax"), 1)

            def b_parts(h):
                dve.wait_ge(S("pv_done"), h + 1)
                k = HEADS + h
                dve.wait_ge(S(f"z_in{k % 2}"), 16 * (k // 2 + 1))
                dve.tensor_tensor(btmp[:], bank(6 + h % 2), zst[k % 2][:], ALU.mult).then_inc(S("b_tmp"), 1)
                dve.wait_ge(S("b_hi"), h + 1)
                dve.tensor_tensor(b_lo[:, h, :], btmp[:], b_hi[:, h, :].bitcast(f32), ALU.subtract).then_inc(S("b_lo"), 1)

            att_max(0)
            for i in range(32):
                dve.wait_ge(S("exp_done"), i + 1)
                ln(dve.reciprocal(rsum[:, i:i + 1], rsum[:, i:i + 1]))
                dve.tensor_scalar(probs[i % 2][:], probs[i % 2][:], rsum[:, i:i + 1], None, ALU.mult).then_inc(
                    S("p_norm"), 1)
                if i < 31:
                    att_max(i + 1)
                if i == 2:
                    qk_var(44, 16, 32)
                if i == 3:
                    qk_rstd(3, 16, 32)
                if i in (4, 6, 7, 8):
                    q_tile(1, (4, 6, 7, 8).index(i))
                if i % 4 == 1 and i >= 5:
                    b_parts(i // 4 - 1)
            b_parts(HEADS - 1)
            for n in range(N_MERGE0, NP):
                lo_part(n + 1)
                e = n - N_MERGE0
                if e >= 4 and e % 4 == 0 and e // 4 <= 8:
                    j = e // 4 - 1
                    for jj in (0, 1):
                        m = 2 * j + jj
                        b0 = 4 * (j % 2)
                        dve.wait_ge(S("w_used"), n)
                        dve.wait_ge(S(f"gates_in{m % 4}"), 32 * (m // 4 + 1))
                        if m >= 2:
                            dve.wait_ge(S("m_lo"), m - 1)
                        t0, t1 = mtmp[2 * (m % 2)], mtmp[2 * (m % 2) + 1]
                        ln(dve.tensor_tensor(t0[:], bank(b0 + jj), gsig[m % 4][:, 0, :], ALU.mult))
                        dve.tensor_tensor(t1[:], bank(b0 + 2 + jj), gsig[m % 4][:, 1, :], ALU.mult).then_inc(
                            S("m_psum"), 1)
                        dve.wait_ge(S("m_psum"), m + 1)
                        dve.tensor_tensor(t0[:], t0[:], t1[:], ALU.add).then_inc(S("m_tmp"), 1)
                    for jj in (0, 1):
                        m = 2 * j + jj
                        dve.wait_ge(S("m_hi"), m + 1)
                        dve.tensor_tensor(m_lo[:, m, :], mtmp[2 * (m % 2)][:], m_hi[:, m, :].bitcast(f32),
                                          ALU.subtract).then_inc(S("m_lo"), 1)
                if n == N_MERGE0:
                    for q in range(4):
                        dve.wait_ge(S("grow_mm"), 4 * q + 4)
                        dve.tensor_copy(grow[:, 512 * q:512 * q + 512], bank(4 + q)).then_inc(S("grow_evac"), 1)
                if n > N_OUT0 and (n - N_OUT0) % 8 == 0:
                    out_rows((n - N_OUT0) // 8 - 1)
            out_rows(3)

        @block.tensor
        def _(pe):
            pe.wait_ge(S("const_in"), 16)
            pe.wait_ge(S("rows_in"), 96)
            pe.transpose(bank(7, 97), rows[:], ident[0:97, 0:97]).then_inc(S("rowsT"), 1)
            pe.transpose(bank(6, 120), crows[:], ident[0:120, 0:120]).then_inc(S("rowsT"), 1)

            def x_transposes(t):
                pe.wait_ge(S("xn"), t + 1)
                for q4 in range(4):
                    n = 4 * t + q4
                    if n >= 4:
                        pe.wait_ge(S("xt_evac"), n - 3)
                    for u in range(4):
                        k = 4 * q4 + u
                        ins = pe.transpose(bank4(n % 4)[:, u, :], xt[t % 2][:, k * P:(k + 1) * P], ident)
                    ins.then_inc(S("xt_ready"), 1)

            def mod_cols(rows_t, b, name, count):
                pe.wait_ge(S(f"{name}_rows"), count)
                for q in range(4):
                    ins = pe.matmul(bank(b, 2, 2 * q), rows_t[:, q * P:(q + 1) * P], consts[0:4, SEL:SEL + 2],
                                    start=True, stop=True)
                ins.then_inc(S(f"{name}_cols_mm"), 1)

            def item_work(ci):
                it = ITEMS[ci]
                pe.wait_ge(S("item_ready"), ci + 1)
                a = acc[ci % 2]
                if it["what"] == "v":
                    if ci > 8:
                        pe.wait_ge(S("v_evac"), ci - 8)
                    for t in range(LT):
                        pe.transpose(bank4(6)[:, t, :], a[:, t * P:(t + 1) * P], ident)
                    for t in range(CT):
                        ins = pe.transpose(bank(7, P, 128 + t * P), a[:, 516 + t * P:516 + (t + 1) * P], ident)
                else:
                    if it["what"] == "q":
                        pe.wait_ge(S("v_evac"), 8)
                    off = 48 if it["what"] == "q" else 0
                    for t in range(LT if off else NT):
                        a0 = t * P if t < LT else 516 + (t - LT) * P
                        ins = pe.matmul(bank(7, 1, off + t * 8 + it["head"]), a[:, a0:a0 + P], ones[:, 0:1],
                                        start=True, stop=True)
                ins.then_inc(S("item_pe"), 1)

            def three(out_ap, lhs, rhs, first, last, shared=False):
                (lh, ll), (rh, rl) = lhs, rhs
                pe.matmul(out_ap, lh, rh, start=first, stop=False, skip_group_check=shared)
                pe.matmul(out_ap, lh, rl, start=False, stop=False, skip_group_check=shared)
                return pe.matmul(out_ap, ll, rh, start=False, stop=last, skip_group_check=shared)

            LASTB = len(BLOCKS) - 1

            def gdn(slot):
                k, n, pr, i = slot["kind"], slot["n"], PAIRS[slot["pair"]], slot["i"]
                half = pr["half"]
                for d in (0, 1):
                    tile = pr["tiles"][d]
                    b = 4 + 2 * d + i % 2
                    ps = bank4(b)
                    if i:
                        pe.wait_ge(S(f"gd{d}"), i)
                    if k == "decay":
                        pe.wait_ge(S(f"gm{d}"), slot["pair"] + 1)
                    if slot["pair"] == 0 and k == "ks":
                        pe.wait_ge(S("states0"), 1)
                    for u in range(4):
                        h = 4 * half + u
                        kt = kT_of(h, tile)
                        qt = qT[:, h, tile * P:(tile + 1) * P] if pr["lat"] else None
                        if k == "decay":
                            m = (GT, LT_)[d]
                            ins = pe.matmul(ps[:, u, :], GM[d][:, u, :], consts[:, m:m + P], start=True, stop=True)
                        elif k == "gram":
                            ins = pe.matmul(ps[:, u, :], kt, kt, start=True, stop=True)
                        elif k == "qk":
                            ins = pe.matmul(ps[:, u, :], qt, kt, start=True, stop=True)
                        elif k == "couple" and n == LASTB:
                            r0, c0 = 64 * (1 - d), 64 * d
                            ins = pe.matmul(bank4(b, 64)[c0:c0 + 64, u, :], LL[d][r0:r0 + 64, u, c0:c0 + 64],
                                            YY[d][r0:r0 + 64, u, r0:r0 + 64], start=True, stop=True)
                        elif k == "correct" and n == LASTB:
                            c0 = 64 * d
                            ins = pe.matmul(bank4(b, 64)[c0:c0 + 64, u, :], XX[d][c0:c0 + 64, u, c0:c0 + 64],
                                            PM[d][c0:c0 + 64, u, :], start=True, stop=True)
                        elif k == "couple":
                            rhs = odd1(ident if n == 0 else YY[d][:, u, :], BLOCKS[n], d)
                            dst = bank4(b, 64)[:, u, :].rearrange("p (b s) -> p b s", s=BLOCKS[n])
                            ins = pe.matmul(dst, LL[d][:, u, :], rhs, start=True, stop=True)
                        elif k == "correct":
                            ins = pe.matmul(bank4(b, 64)[:, u, :], XX[d][:, u, :], PM[d][:, u, :], start=True, stop=True)
                        elif k == "flip":
                            ins = pe.transpose(ps[:, u, :], YY[d][:, u, :], ident)
                        elif k == "at":
                            ins = pe.transpose(ps[:, u, :], DD[d][:, u, :], ident)
                        elif k == "kt":
                            ins = pe.transpose(ps[:, u, :], kt, ident)
                        elif k == "ks":
                            ins = pe.matmul(ps[:, u, :], kt, SS[:, d, h, :], start=True, stop=True)
                        elif k == "z":
                            ins = pe.matmul(ps[:, u, :], XX[d][:, u, :], RR[d][:, u, :], start=True, stop=True)
                        elif k == "qs":
                            ins = pe.matmul(ps[:, u, :], qt, SS[:, d, h, :], start=True, stop=True)
                        elif k == "az":
                            ins = pe.matmul(ps[:, u, :], YY[d][:, u, :], ZZ[d][:, u, :], start=True, stop=True)
                        elif k == "kz":
                            ins = pe.matmul(ps[:, u, :], LL[d][:, u, :], ZZ[d][:, u, :], start=True, stop=True)
                    ins.then_inc(S(f"gp{d}"), 1)

            def piece(n):
                p = PIECES[n]
                gi = p["g"]
                g = GROUPS[gi]
                first, last = n == g["first"], n == g["last"]
                ins = None
                if first:
                    accs_free_needed(pe, gi)
                pe.wait_ge(S("w_lo"), n + 1)
                wh, wl = part3(whi[n % 2], p), part3(wlo[n % 2], p)
                kind = p["kind"]
                for kk in range(p["nk"]):
                    k = p["k0"] + kk
                    st, sp_ = first and kk == 0, last and kk == p["nk"] - 1
                    if gi == G_CONV0:
                        pe.wait_ge(S("h_lo"), 2 * (k + 1))
                    if kind in ("mod", "modg"):
                        b0 = 4 + (gi if kind == "mod" else MODGS.index(gi)) % 2
                        pe.matmul(bank(b0)[0:4], c4[:, k, :], wh[:, kk, :], start=st, stop=False)
                        ins = pe.matmul(bank(b0)[0:4], c4[:, k, :], wl[:, kk, :], start=False, stop=sp_)
                    if gi == OUTS[0]:
                        pe.wait_ge(S("m_lo"), k + 1)
                    if kind in ("conv", "gate", "merge"):
                        src = (h_hi, h_lo)
                        b0 = 3 * ((gi - G_CONV0) % 2)
                        if kind == "gate":
                            b0 = 2 * (GATES.index(gi) % 2)
                        if kind == "merge":
                            src = ((a_hi, a_lo), (b_hi, b_lo))[p["branch"]]
                            b0 = 4 * (p["j"] % 2) + 2 * p["branch"]
                        for j in (0, 1):
                            w = (wh[:, kk, j * P:(j + 1) * P], wl[:, kk, j * P:(j + 1) * P])
                            ins = three(bank(b0 + j), w, (src[0][:, k, :], src[1][:, k, :]), st, sp_)
                        if kind == "conv" and g["what"] != "q":
                            for j in (0, 1):
                                w = (wh[:, kk, j * P:(j + 1) * P], wl[:, kk, j * P:(j + 1) * P])
                                ins = three(bank(b0 + 2, 256, 256 * j), w, (hc_hi[:, k, :], hc_lo[:, k, :]),
                                            st and j == 0, sp_, shared=True)
                        if kind == "gate":
                            if kk == p["nk"] - 1:
                                ins.then_inc(S("w_used"), 1)
                            s = slot_at(n, kk)
                            if s:
                                if s["i"] == 0:
                                    pe.wait_ge(S("prep"), 1)
                                gdn(s)
                    elif kind in ("bkv", "bq", "out"):
                        b0 = 4 * ((g["j"]) % 2) if kind == "out" else 0
                        for t in range(NT if kind == "bkv" else LT):
                            if kind == "out":
                                l = (m_hi[:, k, t * P:(t + 1) * P], m_lo[:, k, t * P:(t + 1) * P])
                            elif t < LT:
                                l = (h_hi[:, k, t * P:(t + 1) * P], h_lo[:, k, t * P:(t + 1) * P])
                            else:
                                l = (hc_hi[:, k, (t - LT) * P:(t - LT + 1) * P], hc_lo[:, k, (t - LT) * P:(t - LT + 1) * P])
                            ins = three(bank(b0 + t), l, (wh[:, kk, :], wl[:, kk, :]), st, sp_)
                if kind == "ab":
                    for t in range(NT):
                        for k in range(KT):
                            if t < LT:
                                l = (h_hi[:, k, t * P:(t + 1) * P], h_lo[:, k, t * P:(t + 1) * P])
                            else:
                                l = (hc_hi[:, k, (t - LT) * P:(t - LT + 1) * P], hc_lo[:, k, (t - LT) * P:(t - LT + 1) * P])
                            ins = three(bank(6, 32, t * 32), l, (wh[:, k, :], wl[:, k, :]), k == 0, k == KT - 1)
                if kind != "gate":
                    ins.then_inc(S("w_used"), 1)

            pe.wait_ge(S("c_lo"), 1)
            for n in range(N_MERGE0):
                piece(n)
                for t in range(NT):
                    if n == 4 + 2 * t:
                        x_transposes(t)
                for gi, g in enumerate(MODS):
                    if n == g["last"] + 1:
                        if gi >= 2:
                            pe.wait_ge(S("mod_evac"), gi - 1)
                        mod_cols(mrow, 6 + gi % 2, "mod", gi + 1)
                for k, gi in enumerate(MODGS):
                    if n == GROUPS[gi]["last"] + 1:
                        if k >= 2:
                            pe.wait_ge(S("modg_cols"), k - 1)
                        mod_cols(mrow_g, 6 + k % 2, "modg", k + 1)
                r = n - N_FIN
                if 6 <= r < 10:
                    if r == 6:
                        pe.wait_ge(S("y_ready"), LT)
                    for h in (2 * (r - 6), 2 * (r - 6) + 1):
                        if h >= 4:
                            pe.wait_ge(S("a_tmp"), h - 3)
                        for t in range(LT):
                            ins = pe.transpose(bank4(4 + h % 4)[:, t, :], o_acc[:, t, h * P:(h + 1) * P], ident)
                        ins.then_inc(S("yt_ready"), 1)
                for gi, g in enumerate(CONVS):
                    e = n - g["last"]
                    if e in (3, 4):
                        item_work(2 * gi + e - 3)
                if n == GROUPS[G_BKV]["first"] + 5:
                    pe.wait_ge(S("g_ready"), 1)
                    for t in range(NT):
                        for d in (0, 1):
                            for w, m in enumerate(((LE, GT, ONES), (GE, LT_, ONES))[d]):
                                ins = pe.matmul(bank(6, 8, ((t * 2 + d) * 3 + w) * 8), consts[:, m:m + P],
                                                gdec[:, t * 16 + d * 8:t * 16 + d * 8 + 8], start=True, stop=True)
                    ins.then_inc(S("cum"), 1)
            mod_cols_last = len(MODGS) - 1
            pe.wait_ge(S("modg_cols"), mod_cols_last - 1)
            mod_cols(mrow_g, 6 + mod_cols_last % 2, "modg", mod_cols_last + 1)

            def q_transposes(h, b):
                pe.wait_ge(S("q_rot"), LT if h < 4 else 2 * LT)
                for t in range(LT):
                    ins = pe.transpose(bank4(b)[:, t, :], bqr[:, t, h * P:(h + 1) * P], ident)
                ins.then_inc(S("qt_ready"), 1)

            pe.wait_ge(S("bq_evac"), 8)
            for h in range(4):
                q_transposes(h, h)
            pe.wait_ge(S("k_ctx_rows"), CT)
            pe.wait_ge(S("modg_cols"), 4)
            for kv in range(KV):
                for t in range(NT):
                    ins = pe.transpose(PS[:, (4 + 2 * kv) * 512 + t * P:(4 + 2 * kv) * 512 + (t + 1) * P],
                                       kvr[:, t, kv * P:(kv + 1) * P], ident)
                ins.then_inc(S("kt_ready"), 1)
            pe.wait_ge(S("qt_evac"), 4)
            pe.wait_ge(S("kt_evac"), KV)

            def scores(i):
                h, qt = divmod(i, 4)
                if i >= 2:
                    pe.wait_ge(S("exp_done"), i - 1)
                if h >= 4 and qt == 0:
                    pe.wait_ge(S("qt_evac"), h + 1)
                b = 2 * (i % 2)
                q = qhT[:, h, qt * P:(qt + 1) * P]
                kv = h // (HEADS // KV)
                pe.matmul(bank(b), q, khT[:, kv, 0:512], start=True, stop=True)
                pe.matmul(bank(b + 1, 256), q, khT[:, kv, 512:TOK], start=True, stop=True).then_inc(S("sc_ready"), 1)

            scores(0)
            for i in range(32):
                if i < 31:
                    scores(i + 1)
                h, qt = divmod(i, 4)
                if qt == 2 and 3 <= h < 7:
                    pe.wait_ge(S("b_tmp"), h)
                    q_transposes(h + 1, 6 + (h + 1) % 2)
                pe.wait_ge(S("p_norm"), i + 1)
                if i:
                    pe.wait_ge(S("pt_evac"), i)
                for t in range(NT):
                    ins = pe.transpose(PS[:, 2048 + t * P:2048 + (t + 1) * P], probs[i % 2][:, t * P:(t + 1) * P], ident)
                ins.then_inc(S("pt_ready"), 1)
                if qt == 3:
                    pe.wait_ge(S("pt_evac"), i + 1)
                    if h >= 2:
                        pe.wait_ge(S("b_tmp"), h - 1)
                    kv = h // (HEADS // KV)
                    for t in range(NT):
                        ins = pe.matmul(bank(6 + h % 2), kvr[:, t, 256 + kv * P:256 + (kv + 1) * P], PTt[:, t, :],
                                        start=(t == 0), stop=(t == NT - 1))
                    ins.then_inc(S("pv_done"), 1)
            pe.wait_ge(S("pt_evac"), 32)
            pe.wait_ge(S("b_tmp"), HEADS)
            for k in range(KT):
                pe.wait_ge(S("gcb"), k + 1)
                pe.matmul(bank(4 + k // 4, P, (k % 4) * P), gcb[k % 4][:], ident, start=True, stop=True).then_inc(
                    S("grow_mm"), 1)
            for n in range(N_MERGE0, NP):
                if n in (N_MERGE0, N_MERGE0 + 2):
                    pe.wait_ge(S("a_lo" if n == N_MERGE0 else "b_lo"), HEADS)
                piece(n)


INPUTS = ["x", "c", "ctx", "c_ctx", "w_mod", "b_mod", "norm_w", "w_in", "conv_w", "a_log", "dt_bias", "a_norm_w",
          "q_norm_w", "k_norm_w", "w_proj_a", "w_proj_b", "w_out"]


def kernel(**inputs):
    import concourse.bacc as bacc
    from concourse.bass_utils import run_bass_kernel_spmd

    nc = bacc.Bacc("TRN2", target_bir_lowering=False, num_devices=1)
    arrays = {f"{name}_dram": np.ascontiguousarray(inputs[name]) for name in INPUTS}
    arrays["consts_dram"], arrays["rope_dram"] = shape_constants()
    args = [nc.dram_tensor(name, a.shape, mybir.dt.float32, kind="ExternalInput").ap() for name, a in arrays.items()]
    out = nc.dram_tensor("out_dram", (1, SEQ, DM), mybir.dt.float32, kind="ExternalOutput").ap()
    build(nc, *args, out)
    return run_bass_kernel_spmd(nc, [arrays], core_ids=[0]).results[0]["out_dram"]
```

```python
from contextlib import ExitStack

import numpy as np

import concourse.bass as bass
from concourse import mybir

P = 128
DM = 2048
SEQ = 512
CTX = 256
TOK = SEQ + CTX
HEADS = 8
CONV = 5
KV = 2
HD = 128
KT = DM // P
LT = SEQ // P
CT = CTX // P
NT = LT + CT
EPS = 1e-6
GRID_W = 64
ROPE_THETA = 10000.0

COL_AQ, COL_AK, COL_AV, COL_AZ = 0, 1024, 2048, 3072
COL_AB = 4096
COL_BQ, COL_BKV, COL_BZ, COL_BR = 4128, 5152, 5664, 6688

IDENT, LE, GE, GT, LT_, ONES, STAGE = 0, 128, 256, 384, 512, 640, 768
BLOCKS = [1, 2, 4, 8, 16, 32, 64]
MASKED = BLOCKS[:-2]
NCONST = STAGE + len(MASKED) * 2 * 64


def shape_constants():
    a = np.arange(P)
    t, i = a[:, None], a[None, :]
    parts = [t == i, t <= i, t >= i, t > i, t < i, np.ones((P, P), bool)]
    for s in MASKED:
        block = a // s
        for backward in (0, 1):
            cols = a[(block % 2) == (0 if backward else 1)]
            want = cols // s + (1 if backward else -1)
            parts.append(block[:, None] == want[None, :])
    consts = np.concatenate(parts, axis=1).astype(np.float32)
    assert consts.shape == (P, NCONST)
    tok = np.arange(SEQ)
    inv = ROPE_THETA ** (-np.arange(HD // 4) / (HD // 4))
    ang = np.concatenate([(tok // GRID_W)[:, None] * inv, (tok % GRID_W)[:, None] * inv], axis=-1)
    rope = np.concatenate([np.cos(ang), np.sin(ang)], axis=1).astype(np.float32)
    return consts, rope


def projection_plan():
    groups, pieces = [], []

    def group(kind, col, width, per_piece, **more):
        g = dict(kind=kind, col=col, width=width, first=len(pieces), **more)
        for k0 in range(0, KT, per_piece):
            pieces.append(dict(g=len(groups), kind=kind, k0=k0, nk=per_piece, col=col, width=width))
        g["last"] = len(pieces) - 1
        groups.append(g)

    for j in range(4):
        group("mod", 512 * j, 512, 2, j=j, scale=0)
        group("mod", DM + 512 * j, 512, 2, j=j, scale=1)
    for what, col in (("k", COL_AK), ("v", COL_AV), ("q", COL_AQ)):
        for j in range(4):
            group("conv", col + 256 * j, 256, 4, what=what, pair=j)
    group("ab", COL_AB, 32, 16)
    group("bkv", COL_BKV, 512, 2)
    for first, col, n in ((0, COL_AZ, 4), (8, COL_BZ, 4), (16, COL_BR, 16)):
        for j in range(n):
            group("gate", col + 256 * j, 256, 4, row=first + 2 * j)
    for j in (0, 1):
        group("bq", COL_BQ + 512 * j, 512, 2, half=j)
    for j in range(4):
        group("modg", 2 * DM + 512 * j, 512, 2, j=j)
    for j in range(8):
        for branch in (0, 1):
            g = dict(kind="merge", first=len(pieces), j=j, branch=branch)
            for k0 in (0, 4):
                pieces.append(dict(g=len(groups), kind="merge", k0=k0, nk=4, col=256 * j, width=256, branch=branch, j=j))
            g["last"] = len(pieces) - 1
            groups.append(g)
    for j in range(4):
        group("out", 512 * j, 512, 2, j=j)
    return groups, pieces


def scan_plan():
    pairs, slots = [], []
    fwd = [LT, LT + 1] + list(range(LT))
    bwd = [LT + 1, LT] + list(range(LT))[::-1]
    for step in range(NT):
        for half in range(2):
            lat, last = step >= CT, step == NT - 1
            pairs.append(dict(tiles=(fwd[step], bwd[step]), half=half, lat=lat, last=last, first=len(slots)))
            p = len(pairs) - 1
            early = p > 0
            kinds = [("decay", 0)] + [("ks", 0)] * early + [("gram", 0)] + [("qk", 0)] * lat
            for n in range(len(BLOCKS)):
                kinds += [("couple", n)] + [("correct", n)] * (n > 0) + [("flip", n)] * (n == len(BLOCKS) - 2)
            kinds += [("at", 0)] * lat + [("kt", 0)] * (not last) + [("ks", 0)] * (not early) + [("z", 0)]
            kinds += [("qs", 0), ("az", 0)] * lat + [("kz", 0)] * (not last)
            slots += [dict(kind=k, n=n, pair=p, i=len(slots) + m) for m, (k, n) in enumerate(kinds)]
            pairs[-1]["end"] = len(slots)
    return pairs, slots


ON_SCALAR = ("decay", "flip", "at", "kt", "z")


def build(nc, x, c, ctx, c_ctx, w_mod, b_mod, norm_w, w_in, conv_w, a_log, dt_bias, a_norm_w, q_norm_w,
          k_norm_w, w_proj_a, w_proj_b, w_out, consts_in, rope_in, out):
    f32, f32r = mybir.dt.float32, mybir.dt.float32r
    ALU, ACT, AX = mybir.AluOpType, mybir.ActivationFunctionType, mybir.AxisListType
    GROUPS, PIECES = projection_plan()
    PAIRS, SLOTS = scan_plan()
    NP = len(PIECES)
    CONVS = [g for g in GROUPS if g["kind"] == "conv"]
    ITEMS = [dict(what=g["what"], head=2 * g["pair"] + j, g=gi, j=j) for gi, g in enumerate(CONVS) for j in (0, 1)]
    G_CONV0 = [g["kind"] for g in GROUPS].index("conv")
    G_AB = G_CONV0 + len(CONVS)
    MODS = [g for g in GROUPS if g["kind"] == "mod"]
    NM = MODS[-1]["last"] + 1
    MODGS = [gi for gi, g in enumerate(GROUPS) if g["kind"] == "modg"]
    G_BKV = G_AB + 1
    GATES = [gi for gi, g in enumerate(GROUPS) if g["kind"] == "gate"]
    BQS = [gi for gi, g in enumerate(GROUPS) if g["kind"] == "bq"]
    OUTS = [gi for gi, g in enumerate(GROUPS) if g["kind"] == "out"]
    N_GATE0 = GROUPS[GATES[0]]["first"]
    N_BQ0 = GROUPS[BQS[0]]["first"]
    N_MODG0 = GROUPS[MODGS[0]]["first"]
    N_MERGE0 = GROUPS[MODGS[-1]]["last"] + 1
    N_OUT0 = GROUPS[OUTS[0]]["first"]
    N_FIN = N_GATE0 + 1 + -(-len(SLOTS) // 4)
    assert N_FIN + 15 <= N_BQ0, N_FIN - N_BQ0

    whole = [p["kind"] in ("mod", "modg") for p in PIECES]
    parts_made = np.cumsum([not w for w in whole]).tolist()
    SPLIT = [n for n in range(NP) if not whole[n]]

    MODG_STEPS = (0, 2, 1, 1, 0, 2, 2, 0)
    MODG_END = len(MODG_STEPS) - 1
    assert sum(MODG_STEPS) == 8

    def modg_pieces(i):
        n = N_MODG0 + 8 * (i // 8) + sum(MODG_STEPS[:i % 8])
        return range(n, n + MODG_STEPS[i % 8])

    X_AT = [1 + 4 * t for t in range(NT)]
    H_AT = [max(g["last"] + 2, X_AT[-1] + 5) for g in MODS if g["scale"]]

    def slot_at(n, q):
        i = 4 * (n - N_GATE0 - 1) + q
        return SLOTS[i] if N_GATE0 < n < N_BQ0 and i < len(SLOTS) else None

    base = 16512
    A_CONST, A_SMALL, A_RING = 0, 6688, 11104
    A_MASKS = 4 * NCONST
    assert A_MASKS + 1024 <= A_SMALL
    A_H = A_RING + 24576
    A_C = A_H + 65536
    A_G = A_C + 32768
    A_T = A_G + 65536

    def at(name, shape, off, dt=f32):
        return nc.alloc_sbuf_tensor_at(name, shape, dt, offset=base + off)

    consts = at("consts", [P, NCONST], A_CONST)
    tri_r = [at(f"triangle{d}", [P, P], A_MASKS + 512 * d, f32r) for d in (0, 1)]
    small_top = [A_SMALL]

    def small(name, shape):
        n = int(np.prod(shape[1:])) * 4
        n = (n + 31) // 32 * 32
        t = at(name, shape, small_top[0])
        small_top[0] += n
        assert small_top[0] <= A_RING, small_top[0] - A_RING
        return t

    cols = small("cols", [P, 97])
    convw = small("convw", [P, 120])
    GATE = small("gate_cols", [P, KT])
    stat = small("stat", [P, 16])
    beta = small("beta", [P, NT * 16])
    betar = beta
    off_wrow = small_top[0]
    gdec = small("gdec", [P, NT * 16])
    crow = small("crow", [P, NT * 16])
    ngr = small("ngr", [P, NT * 16])
    off_dec = small_top[0]
    DEC = small("decays", [P, NT * 2, 3, 8])
    rk = small("rk", [P, 48])
    rq = small("rq", [P, 32])
    alog = small("alog", [P, 16])
    dtb = small("dt_bias_rows", [P, 16])
    sc2 = small("silu_c", [P, KT, 2])
    wrow = at("w_rows", [P, 256], off_wrow)
    ssq_o = at("ssq_o", [P, 32], off_dec)
    ssq_a = at("ssq_a", [P, 44], off_dec + 128)
    nmax = at("neg_max", [P, 32], off_dec + 320)
    rsum = at("row_sum", [P, 32], off_dec + 448)

    raw = [at(f"w_raw{i}", [P, 1024], A_RING + 4096 * i) for i in range(2)]
    whi = [at(f"w_hi{i}", [P, 1024], A_RING + 8192 + 4096 * i, f32r) for i in range(2)]
    wlo = [at(f"w_lo{i}", [P, 1024], A_RING + 16384 + 4096 * i, f32r) for i in range(2)]
    h_hi = at("h_hi", [P, KT, SEQ], A_H, f32r)
    h_lo = at("h_lo", [P, KT, SEQ], A_H + 32768, f32r)
    raw_mod = [at(f"w_raw_mod{i}", [P, 1024], A_H + 32768 * (i // 2) + 24576 + 4096 * (i % 2)) for i in range(4)]
    hc_hi = at("hc_hi", [P, KT, CTX], A_C, f32r)
    hc_lo = at("hc_lo", [P, KT, CTX], A_C + 16384, f32r)
    xnT = at("xnT", [P, KT, TOK], A_G)
    xt = [at(f"x_rows{i}", [P, DM], A_G + 49152 + 8192 * i) for i in range(2)]
    junk = at("junk", [P, DM], A_T)
    rows = at("rows", [97, P], A_T + 8192)
    crows = at("conv_rows", [120, P], A_T + 8704)
    modv = at("mod_vec", [P, 2, KT, 2], A_T + 9216)
    mrow = at("mod_rows", [2, 512], A_T + 9728)
    G_Q, G_K, G_V, G_O = A_G, A_G + 16384, A_G + 32768, A_G + 49152
    qT = at("qT", [P, HEADS, SEQ], G_Q)
    kTl = at("kT_latent", [P, HEADS, SEQ], G_K)
    vl = at("v_latent", [P, LT, 1024], G_V)
    kTc = at("kT_context", [P, HEADS, CTX], G_O)
    vc = at("v_context", [P, CT, 1024], G_O + 8192)
    RAWW = 776
    rawc = [at(f"conv_in{i}", [P, RAWW], A_T + 4 * RAWW * i) for i in range(2)]
    ab_c = at("ab_columns", [32, TOK], A_T)
    acc = [at(f"conv_acc{i}", [P, 772], A_T + 8 * RAWW + 3104 * i) for i in range(2)]
    ab_t = [at(f"logit_tmp{i}", [P, NT * 16], A_T + 8 * RAWW + 384 * i) for i in range(5)]
    kvst = [at(f"kv_stage{i}", [P, 512], A_T + 2048 * i) for i in range(NT)]
    GMH = [at(f"decay_rhs_hi{b}", [P, 4, P], A_C + 14336 * b, f32r) for b in (0, 1)]
    DD, LL, XX, YY, RR, ZZ = ([at(f"{n}{b}", [P, 4, P], A_C + 14336 * b + 2048 * (o + 1)) for b in (0, 1)]
                              for o, n in enumerate(("decay", "L", "inv", "invT", "resid", "zval")))
    GML = [at(f"decay_rhs_lo{b}", [P, 4, P], A_C + 14336 * b + 2048, f32r) for b in (0, 1)]
    g_hi = at("g_hi", [P, NT * 16], A_T + 12288, f32r)
    g_lo = at("g_lo", [P, NT * 16], A_T + 12672, f32r)
    PM = [at(f"couple{b}", [P, 4, 64], A_C + 28672 + 1024 * b) for b in (0, 1)]
    SS = at("states", [P, 2, HEADS, P], A_T)
    gst = [at(f"gate_stage{i}", [P, 512], A_T + 8192 + 2048 * i) for i in range(2)]
    o_acc = at("o_acc", [P, LT, 1024], G_O)
    bqr = at("bq_rows", [P, LT, 1024], A_C)
    kvr = at("kv_rows", [P, NT, 512], A_C + 16384)
    mrow_g = at("mod_gate_rows", [2, 512], A_T + 8192)
    sqj = at("square_out", [P, P], A_T + 12288)
    qhT = at("att_qT", [P, HEADS, SEQ], A_H)
    khT = at("att_kT", [P, KV, TOK], A_H + 16384)
    PTt = at("probsT", [P, NT, SEQ], A_H + 34816)
    atmp = [at(f"a_tmp{i}", [P, 512], A_C + 2048 * i) for i in range(2)]
    probs = [at(f"probs{i}", [P, TOK], A_H + 47104 + 3072 * i) for i in range(2)]
    cs = at("cos_sin", [P, LT, 128], G_V)
    qtab = at("q_tab", [P, LT, 256], G_V + 2048)
    ktab = at("k_tab", [P, LT, 256], G_V + 6144)
    btmp = at("b_tmp", [P, 512], A_H + 63488)
    rt = [at(f"rope{i}", [P, 8, 64], A_T + 2048 * i) for i in range(4)]
    zst = [at(f"z_stage{i}", [P, 512], A_C + 28672 + 2048 * i) for i in range(2)]
    a_hi = at("a_hi", [P, 8, SEQ], A_G, f32r)
    a_lo = at("a_lo", [P, 8, SEQ], A_G + 16384, f32r)
    b_hi = at("b_hi", [P, 8, SEQ], A_G + 32768, f32r)
    b_lo = at("b_lo", [P, 8, SEQ], A_G + 49152, f32r)
    m_hi = at("m_hi", [P, KT, SEQ], A_H, f32r)
    m_lo = at("m_lo", [P, KT, SEQ], A_H + 32768, f32r)
    gsig = [at(f"gates{i}", [P, 2, 512], A_C + 4096 * i) for i in range(4)]
    mtmp = [at(f"m_tmp{i}", [P, 512], A_T + 2048 * i) for i in range(4)]
    gcb = [at(f"gate_lhs{i}", [P, P], A_T + 8192 + 512 * i) for i in range(4)]
    grow = at("gate_rows", [P, DM], A_C + 16384)
    xr = at("x_again", [P, LT, DM], A_G + 8192)
    ost = [at(f"out_stage{i}", [P, 512], A_G + 40960 + 2048 * i) for i in range(4)]

    gate_scr = nc.dram_tensor("gate_scratch", [48, P, SEQ], f32, kind="Internal").ap()
    kv_scr = nc.dram_tensor("kv_scratch", [NT, P, 512], f32, kind="Internal").ap()

    with ExitStack() as stack:
        PS = stack.enter_context(nc.psum_tensor("psum", [P, 8 * 512], f32))
        sems = {}

        def S(name):
            if name not in sems:
                sems[name] = stack.enter_context(nc.semaphore(name))
            return sems[name]

        def bank(b, n=512, off=0):
            return PS[:, b * 512 + off:b * 512 + off + n]

        def bank4(b, w=128):
            return PS[:, b * 512:b * 512 + 4 * w].rearrange("p (u n) -> p u n", u=4)

        ident = consts[:, IDENT:IDENT + P]
        ones = consts[:, ONES:ONES + P]

        def odd(tile4, s, d):
            e = 0 if d else 1
            return tile4.rearrange("p u (b e s) -> p u b e s", e=2, s=s)[:, :, :, e, :]

        def odd1(t, s, d, e=None):
            e = (0 if d else 1) if e is None else e
            return t.rearrange("p (b e s) -> p b e s", e=2, s=s)[:, :, e, :]

        def kT_of(head, tile):
            if tile < LT:
                return kTl[:, head, tile * P:(tile + 1) * P]
            return kTc[:, head, (tile - LT) * P:(tile - LT + 1) * P]

        def v_of(head, tile):
            t = vl[:, tile] if tile < LT else vc[:, tile - LT]
            return t[:, head * P:(head + 1) * P]

        HALF_BLOCKS = [[(64 * b + 32 * d, 64 * b + 32 * (1 - d)) for b in (0, 1)] for d in (0, 1)]

        def unit_col(d, tile, head):
            return tile * 16 + d * 8 + head

        def src_of(p):
            w = {"merge": (w_proj_a, w_proj_b)[p.get("branch", 0)], "out": w_out, "mod": w_mod, "modg": w_mod}.get(p["kind"], w_in)
            return w[0, p["k0"] * P:(p["k0"] + p["nk"]) * P, p["col"]:p["col"] + p["width"]].rearrange(
                "(t p) n -> p t n", p=P)

        def part(t, p):
            return t[:, 0:p["nk"] * p["width"]]

        def part3(t, p):
            return part(t, p).rearrange("p (t n) -> p t n", n=p["width"])

        def raw_of(n):
            if n < NM:
                return raw_mod[n % 4], S(f"w_in_mod{n % 4}"), 16 * (n // 4 + 1)
            return raw[n % 2], S(f"w_in{n % 2}"), 16 * ((n - NM) // 2 + 1)

        def accs_free_needed(eng, gi):
            g = GROUPS[gi]
            if g["kind"] == "mod" and gi >= 2:
                eng.wait_ge(S("mod_rows"), gi - 1)
            if g["kind"] == "modg" and gi > MODGS[0]:
                eng.wait_ge(S("modg_cols"), MODGS.index(gi))
            if g["kind"] == "conv" and gi - G_CONV0 >= 2:
                eng.wait_ge(S("conv_raw"), 2 * (gi - G_CONV0 - 1))
            if g["kind"] == "ab":
                eng.wait_ge(S("v_evac"), 8)
            if g["kind"] == "bkv":
                eng.wait_ge(S("conv_raw"), 24)
            if g["kind"] == "gate":
                k = GATES.index(gi)
                if k < 2:
                    eng.wait_ge(S("kv_evac"), 2 * k + 2)
                else:
                    eng.wait_ge(S("gate_evac"), 2 * (k - 1))
            if g["kind"] == "bq":
                k = BQS.index(gi)
                if k == 0:
                    eng.wait_ge(S("gate_evac"), 2 * len(GATES) - 2)
                else:
                    eng.wait_ge(S("a_tmp"), HEADS)
            if g["kind"] == "merge" and g["branch"] == 0:
                if g["j"] == 1:
                    eng.wait_ge(S("grow_evac"), 4)
                if g["j"] >= 2:
                    eng.wait_ge(S("m_psum"), 2 * (g["j"] - 1))
            if g["kind"] == "out":
                k = g["j"]
                if k < 2:
                    eng.wait_ge(S("m_psum"), 14 + 2 * k)
                else:
                    eng.wait_ge(S("out_psum"), 4 * (k - 1))

        block = stack.enter_context(nc.Block())

        @block.sync
        def _(sp):
            sp.dma_start(consts[:], consts_in).then_inc(S("const_in"), 16)
            for r0, n, src in ((0, 16, c[0, :]), (16, 16, c_ctx), (32, 16, norm_w[0, :]), (48, 48, b_mod[0, :]),
                               (96, 1, a_norm_w[0, :])):
                sp.dma_start(rows[r0:r0 + n, :], src.rearrange("(t p) -> t p", p=P)).then_inc(S("rows_in"), 16)
            sp.dma_start(crows[:], conv_w[0].rearrange("t (c p) -> (t c) p", p=P)).then_inc(S("rows_in"), 16)
            for n, p in enumerate(PIECES):
                before = n - 4 if n < NM else n - 2
                if before >= (0 if n < NM else NM):
                    if whole[before]:
                        sp.wait_ge(S("w_used"), before + 1)
                    else:
                        sp.wait_ge(S("w_hi"), parts_made[before])
                        sp.wait_ge(S("w_lo"), parts_made[before])
                place, loaded, _ = raw_of(n)
                sp.dma_start(part3(place, p), src_of(p)).then_inc(loaded, 16)
            for i in range(4):
                sp.wait_ge(S(f"out_dma{i}"), 16 * 4)

        @block.gpsimd
        def _(pool):
            for t in range(NT):
                if t >= 2:
                    pool.wait_ge(S("xt_ready"), 4 * (t - 1))
                src = x[0, t * P:(t + 1) * P, :] if t < LT else ctx[0, (t - LT) * P:(t - LT + 1) * P, :]
                pool.dma_start(xt[t % 2][:], src).then_inc(S(f"x_in{t % 2}"), 16)
            pool.dma_start(alog[:], a_log[0].rearrange("d h -> (d h)").partition_broadcast(P)).then_inc(S("alog_in"), 16)
            pool.dma_start(dtb[:], dt_bias[0].rearrange("d h -> (d h)").partition_broadcast(P)).then_inc(S("alog_in"), 16)
            pool.wait_ge(S("h_lo"), 2 * KT)
            for i in range(2):
                pool.memset(rawc[i][:], 0.0).then_inc(S("pads"), 1)
            pool.wait_ge(S("prep"), 1)
            pool.wait_ge(S("w_used"), N_GATE0)
            for pi, pr in enumerate(PAIRS):
                for d in (0, 1):
                    col = unit_col(d, pr["tiles"][d], 4 * pr["half"])
                    m = (GT, LT_)[d]
                    mask = consts[:, m:m + P].unsqueeze(1).to_broadcast([P, 4, P])
                    if pi:
                        last_read = ("at", "gram")[not PAIRS[pi - 1]["lat"]]
                        pool.wait_ge(S(f"gd{d}"), [s["i"] for s in SLOTS if s["pair"] == pi - 1 and s["kind"] == last_read][0] + 1)
                    for part_t, g_t in ((GMH, g_hi), (GML, g_lo)):
                        ins = pool.tensor_tensor(part_t[d][:], mask,
                                                 g_t[:, col:col + 4].bitcast(f32).unsqueeze(2).to_broadcast([P, 4, P]), ALU.mult)
                    ins.then_inc(S(f"gm{d}"), 1)
                if pi == 0:
                    pool.wait_ge(S("kv_spill"), 16 * NT)
                    pool.memset(SS[:], 0.0).then_inc(S("states0"), 1)
                if pr["lat"] and not PAIRS[pi - 1]["lat"]:
                    for d in (0, 1):
                        pool.wait_ge(S(f"gd{d}"), pr["first"])
                    pool.memset(o_acc[:], 0.0).then_inc(S("oacc0"), 1)
                for d in (0, 1):
                    pool.wait_ge(S(f"gd{d}"), pr["first"] + 1)
                    m = (GE, LE)[d]
                    pool.tensor_tensor(DD[d][:], DD[d][:], consts[:, m:m + P].unsqueeze(1).to_broadcast([P, 4, P]),
                                       ALU.mult).then_inc(S(f"dmask{d}"), 1)

            for d in (0, 1):
                pool.wait_ge(S(f"gd{d}"), len(SLOTS))
            pool.dma_start(wrow[:, 0:P], q_norm_w[0].partition_broadcast(P)).then_inc(S("tab_in"), 16)
            pool.dma_start(wrow[:, P:2 * P], k_norm_w[0].partition_broadcast(P)).then_inc(S("tab_in"), 16)
            pool.dma_start(cs[:], rope_in.rearrange("(t p) n -> p t n", p=P)).then_inc(S("tab_in"), 16)
            for t in range(NT):
                pool.dma_start(kvr[:, t, :], kv_scr[t]).then_inc(S("kv_in"), 16)
            for i in range(2):
                pool.wait_ge(S(f"gate_spill{i}"), 16 * HEADS)

            def z_load(k):
                if k >= 2:
                    if k - 2 < HEADS:
                        pool.wait_ge(S("a_tmp"), k - 1)
                    else:
                        pool.wait_ge(S("b_tmp"), k - 1 - HEADS)
                pool.dma_start(zst[k % 2][:], gate_scr[k]).then_inc(S(f"z_in{k % 2}"), 16)

            def gates_load(m):
                if m >= 4:
                    pool.wait_ge(S("m_psum"), m - 3)
                for r in (0, 1):
                    pool.dma_start(gsig[m % 4][:, r, :], gate_scr[16 + 16 * r + m]).then_inc(S(f"gates_in{m % 4}"), 16)

            for k in range(HEADS + 2):
                z_load(k)
            for k in range(HEADS + 2, 2 * HEADS):
                z_load(k)
            pool.wait_ge(S("qt_ready"), HEADS)
            for i in range(2):
                pool.wait_ge(S(f"gate_spill{i}"), 16 * len(GATES))
            for m in range(4):
                gates_load(m)
            pool.wait_ge(S("modg_cols"), 4)
            for k in range(KT):
                if k >= 4:
                    pool.wait_ge(S("grow_mm"), k - 3)
                pool.tensor_scalar(gcb[k % 4][:], ones, GATE[:, k:k + 1], None, ALU.mult).then_inc(S("gcb"), 1)
            for m in range(4, KT):
                gates_load(m)
            pool.wait_ge(S("w_used"), N_OUT0)
            for t in range(LT):
                pool.dma_start(xr[:, t, :], x[0, t * P:(t + 1) * P, :]).then_inc(S("x_again"), 16)
            for j in range(4):
                for t in range(LT):
                    pool.wait_ge(S("out_ready"), 4 * j + t + 1)
                    pool.dma_start(out[0, t * P:(t + 1) * P, 512 * j:512 * j + 512], ost[t][:]).then_inc(
                        S(f"out_dma{t}"), 16)

        @block.scalar
        def _(act):
            link = [0]

            def ln(ins):
                link[0] += 1
                ins.then_inc(S("act_chain"), 1)
                act.wait_ge(S("act_chain"), link[0])

            def hi_part(n):
                if n >= NP or whole[n]:
                    return
                p, i = PIECES[n], parts_made[n] - 1
                place, loaded, count = raw_of(n)
                act.wait_ge(loaded, count)
                if i >= 2:
                    act.wait_ge(S("w_used"), SPLIT[i - 2] + 1)
                act.activation(part(whi[i % 2], p), part(place, p), ACT.Copy).then_inc(S("w_hi"), 1)

            def x_square(t):
                act.wait_ge(S(f"x_in{t % 2}"), 16 * (t // 2 + 1))
                if t > 0:
                    act.wait_ge(S("x_ssq"), t)
                act.activation(junk[:], xt[t % 2][:], ACT.Square, accum_out=stat[:, t:t + 1]).then_inc(S("x_ssq"), 1)

            def x_std(t):
                act.wait_ge(S("x_var"), t + 1)
                act.activation(stat[:, 8 + t:9 + t], stat[:, t:t + 1], ACT.Sqrt).then_inc(S("x_std"), 1)

            def x_columns(t):
                for q4 in range(4):
                    n = 4 * t + q4
                    act.wait_ge(S("xt_ready"), n + 1)
                    act.activation(xnT[:, 4 * q4:4 * q4 + 4, t * P:(t + 1) * P], bank4(n % 4), ACT.Copy).then_inc(
                        S("xt_evac"), 1)

            def h_hi_parts(j):
                for k in range(4 * j, 4 * j + 4):
                    act.wait_ge(S("h_ready"), k + 1)
                    act.activation(h_hi[:, k, :], xnT[:, k, 0:SEQ], ACT.Copy)
                    act.activation(hc_hi[:, k, :], xnT[:, k, SEQ:TOK], ACT.Copy).then_inc(S("h_hi"), 1)

            def conv_raw(ci):
                it = ITEMS[ci]
                g = CONVS[it["g"]]
                act.wait_ge(S("w_used"), g["last"] + 1)
                if ci == 0:
                    act.wait_ge(S("pads"), 2)
                if ci >= 2:
                    act.wait_ge(S("conv_done"), ci - 1)
                b0 = 3 * (it["g"] % 2)
                lat = act.activation(rawc[ci % 2][:, 2:2 + SEQ], bank(b0 + it["j"]), ACT.Copy)
                if it["what"] == "q":
                    lat.then_inc(S("conv_raw"), 1)
                else:
                    act.activation(rawc[ci % 2][:, 518:774], bank(b0 + 2, 256, 256 * it["j"]), ACT.Copy).then_inc(
                        S("conv_raw"), 1)

            def conv_silu(ci):
                it = ITEMS[ci]
                act.wait_ge(S("conv_done"), ci + 1)
                a = acc[ci % 2]
                if it["what"] == "v":
                    act.activation(a[:], a[:], ACT.Silu).then_inc(S("item_ready"), 1)
                    return
                h = it["head"]
                dst = qT if it["what"] == "q" else kTl
                ln(act.activation(dst[:, h, :], a[:, 0:SEQ], ACT.Silu))
                if it["what"] == "k":
                    ln(act.activation(kTc[:, h, :], a[:, 516:772], ACT.Silu))
                    ln(act.activation(a[:, 516:772], kTc[:, h, :], ACT.Square))
                act.activation(a[:, 0:SEQ], dst[:, h, :], ACT.Square).then_inc(S("item_ready"), 1)

            def gdn(slot):
                k, n, pr = slot["kind"], slot["n"], PAIRS[slot["pair"]]
                for d in (0, 1):
                    ps = bank4(4 + 2 * d + slot["i"] % 2)
                    done = S(f"gd{d}")
                    if k == "correct" and n == len(BLOCKS) - 1:
                        act.wait_ge(S(f"gy{d}"), slot["pair"] + 1)
                        for u in range(4):
                            col = unit_col(d, pr["tiles"][d], 4 * pr["half"] + u)
                            ins = act.activation(XX[d][:, u, :], YY[d][:, u, :], ACT.Copy, scale=betar[:, col:col + 1])
                        ins.then_inc(done, 1)
                        continue
                    act.wait_ge(S(f"gp{d}"), slot["i"] + 1)
                    if k == "decay":
                        act.activation(DD[d][:], ps, ACT.Exp).then_inc(done, 1)
                    elif k == "flip":
                        c0 = 64 * d
                        act.activation(XX[d][c0:c0 + 64, :, c0:c0 + 64], ps[c0:c0 + 64, :, c0:c0 + 64],
                                       ACT.Copy).then_inc(done, 1)
                    elif k == "at":
                        act.activation(YY[d][:], ps, ACT.Copy).then_inc(done, 1)
                    elif k == "z":
                        act.activation(ZZ[d][:], ps, ACT.Copy).then_inc(done, 1)
                    elif k == "kt":
                        for u in range(4):
                            h, tile = 4 * pr["half"] + u, pr["tiles"][d]
                            ins = act.activation(LL[d][:, u, :], ps[:, u, :], ACT.Copy,
                                                 scale=DEC[:, tile * 2 + d, 1, h:h + 1])
                        ins.then_inc(done, 1)

            def bq_rows(j):
                act.wait_ge(S("w_used"), GROUPS[BQS[j]]["last"] + 1)
                act.wait_ge(S("a_lo"), HEADS)
                for t in range(LT):
                    act.activation(bqr[:, t, 512 * j:512 * j + 512], bank(4 * j + t), ACT.Copy).then_inc(S("bq_evac"), 1)

            spills = [0]
            def square(i, src):
                act.activation(sqj[:], src, ACT.Square, accum_out=ssq_a[:, i:i + 1]).then_inc(S("qk_ssq"), 1)
                squares[0] += 1
                act.wait_ge(S("qk_ssq"), squares[0])

            squares = [0]

            def modg_rows(k):
                act.wait_ge(S("w_used"), GROUPS[MODGS[k]]["last"] + 1)
                if k == 0:
                    for i in range(2):
                        act.wait_ge(S(f"gate_spill{i}"), 16 * len(GATES))
                else:
                    act.wait_ge(S("modg_cols_mm"), k)
                act.activation(mrow_g[:], bank(7)[0:2], ACT.Copy).then_inc(S("modg_rows"), 1)

            def q_squares(j):
                act.wait_ge(S("bq_evac"), 4 * (j + 1))
                for t in range(LT):
                    for h in range(4):
                        square(16 * j + 4 * t + h, bqr[:, t, (4 * j + h) * P:(4 * j + h + 1) * P])

            def qk_std(step, a0, a1):
                act.wait_ge(S("qk_var"), step)
                act.activation(ssq_a[:, a0:a1], ssq_a[:, a0:a1], ACT.Sqrt).then_inc(S("qk_std"), 1)

            act.wait_ge(S("cols"), 2)
            act.activation(sc2[:].rearrange("p k v -> p v k"), cols[:, 0:32].rearrange("p (v k) -> p v k", v=2),
                           ACT.Silu).then_inc(S("silu_c"), 1)
            for n in range(N_MODG0):
                hi_part(n + 1)
                for t in range(NT):
                    if n == X_AT[t]:
                        x_square(t)
                    if n == X_AT[t] + 1:
                        x_std(t)
                    if n == X_AT[t] + 3:
                        x_columns(t)
                for gi, g in enumerate(MODS):
                    if n == g["last"] + 1:
                        act.wait_ge(S("w_used"), n)
                        if gi:
                            act.wait_ge(S("mod_cols_mm"), gi)
                        act.activation(mrow[:], bank(4 + gi % 2)[0:2], ACT.Copy).then_inc(S("mod_rows"), 1)
                for j in range(4):
                    if n == H_AT[j] + 1:
                        h_hi_parts(j)
                r = n - N_FIN
                if r == 0:
                    for d in (0, 1):
                        act.wait_ge(S(f"gd{d}"), len(SLOTS))
                if 0 <= r < LT:
                    for h in range(HEADS):
                        k = 8 * r + h
                        if k:
                            act.wait_ge(S("o_ssq"), k)
                        act.activation(sqj[:], o_acc[:, r, h * P:(h + 1) * P], ACT.Square,
                                       accum_out=ssq_o[:, k:k + 1]).then_inc(S("o_ssq"), 1)
                if r == 4:
                    act.wait_ge(S("o_var"), 1)
                    act.activation(ssq_o[:], ssq_o[:], ACT.Sqrt).then_inc(S("o_std"), 1)
                if r == 11:
                    act.wait_ge(S("kv_in"), 16 * NT)
                    for t in range(NT):
                        for kv in range(KV):
                            square(32 + 2 * t + kv, kvr[:, t, kv * P:(kv + 1) * P])
                    qk_std(1, 32, 44)
                if 7 <= r < 11:
                    for h in (2 * (r - 7), 2 * (r - 7) + 1):
                        act.wait_ge(S("a_tmp"), h + 1)
                        act.activation(a_hi[:, h, :], atmp[h % 2][:], ACT.Copy).then_inc(S("a_hi"), 1)
                if n == GROUPS[BQS[0]]["last"] + 1:
                    bq_rows(0)
                if n == GROUPS[BQS[0]]["last"] + 2:
                    q_squares(0)
                    qk_std(2, 0, 16)
                for gi, g in enumerate(CONVS):
                    e = n - g["last"]
                    if e == 1:
                        conv_raw(2 * gi)
                        conv_raw(2 * gi + 1)
                    if e in (2, 3):
                        conv_silu(2 * gi + e - 2)
                if n == GROUPS[G_BKV]["first"] + 4:
                    act.wait_ge(S("w_used"), GROUPS[G_AB]["last"] + 1)
                    act.wait_ge(S("conv_done"), 24)
                    act.activation(ab_c[:, 0:SEQ], bank(6)[0:32], ACT.Copy)
                    act.activation(ab_c[:, SEQ:TOK], bank(7, 256, 256)[0:32], ACT.Copy).then_inc(S("ab_cols"), 1)
                if n == GROUPS[G_BKV]["first"] + 5:
                    act.wait_ge(S("ab_rows"), 1)
                    ab = bank(6, NT * 32).rearrange("p (t c) -> p t c", t=NT)
                    act.activation(beta[:].rearrange("p (t c) -> p t c", t=NT), ab[:, :, 0:16], ACT.Sigmoid).then_inc(
                        S("beta"), 1)
                    act.wait_ge(S("negabs"), 1)
                    ln(act.activation(ab_t[1][:], ab_t[1][:], ACT.Exp))
                    ln(act.activation(ab_t[2][:], ab_t[1][:], ACT.Ln, bias=1.0))
                    act.wait_ge(S("alog_in"), 32)
                    act.activation(alog[:], alog[:], ACT.Exp).then_inc(S("ab_exp"), 1)
                    act.wait_ge(S("ssq_eps"), 1)
                    ln(act.activation(rk[:], rk[:], ACT.Sqrt))
                    act.activation(rq[:], rq[:], ACT.Sqrt).then_inc(S("ssq_std"), 1)
                if n == GROUPS[G_BKV]["first"] + 6:
                    act.wait_ge(S("cum"), 1)
                    act.activation(DEC[:].rearrange("p a b c -> p (a b c)"), bank(6, NT * 2 * 24), ACT.Exp).then_inc(
                        S("decays"), 1)
                if n == N_GATE0:
                    g = GROUPS[G_BKV]
                    for t in range(NT):
                        if t == 0:
                            act.wait_ge(S("w_used"), g["last"] + 1)
                            act.wait_ge(S("conv_done"), 24)
                            act.wait_ge(S("prep"), 1)
                        act.activation(kvst[t][:], bank(t), ACT.Copy).then_inc(S("kv_evac"), 1)
                    for t in range(NT):
                        act.wait_ge(S("kv_evac"), t + 1)
                        act.dma_start(kv_scr[t], kvst[t][:]).then_inc(S("kv_spill"), 16)
                for q in range(4):
                    s = slot_at(n, q)
                    if s and (s["kind"] in ON_SCALAR or (s["kind"] == "correct" and s["n"] == len(BLOCKS) - 1)):
                        gdn(s)
                    pg = PIECES[n - 1]["g"] if n else 0
                    if q in (0, 2) and n and GROUPS[pg]["kind"] == "gate" and n - 1 == GROUPS[pg]["last"]:
                        j = q // 2
                        k = spills[0]
                        spills[0] += 1
                        row = GROUPS[pg]["row"] + j
                        if j == 0:
                            act.wait_ge(S("w_used"), n)
                        if k == 0:
                            act.wait_ge(S("kv_spill"), 16 * NT)
                        if k >= 2:
                            act.wait_ge(S(f"gate_spill{k % 2}"), 16 * (k // 2))
                        act.activation(gst[k % 2][:], bank(2 * (GATES.index(pg) % 2) + j),
                                       ACT.Silu if row < 16 else ACT.Sigmoid).then_inc(S("gate_evac"), 1)
                        act.wait_ge(S("gate_evac"), k + 1)
                        act.dma_start(gate_scr[row], gst[k % 2][:]).then_inc(S(f"gate_spill{k % 2}"), 16)
            bq_rows(1)

            def q_columns(h, b):
                act.wait_ge(S("qt_ready"), h + 1)
                act.activation(qhT[:, h, :], bank(b), ACT.Copy).then_inc(S("qt_evac"), 1)

            for kv in range(KV):
                q_columns(2 * kv, 2 * kv)
                q_columns(2 * kv + 1, 2 * kv + 1)
                act.wait_ge(S("kt_ready"), kv + 1)
                act.activation(khT[:, kv, :], PS[:, (4 + 2 * kv) * 512:(4 + 2 * kv) * 512 + TOK], ACT.Copy).then_inc(
                    S("kt_evac"), 1)

            def att_exp(i):
                act.wait_ge(S("negmax"), i + 1)
                if i >= 2:
                    act.wait_ge(S("pt_ready"), i - 1)
                act.activation(probs[i % 2][:], PS[:, (i % 2) * 1024:(i % 2) * 1024 + TOK], ACT.Exp,
                               bias=nmax[:, i:i + 1], scale=HD ** -0.5, accum_out=rsum[:, i:i + 1]).then_inc(
                    S("exp_done"), 1)

            att_exp(0)
            for i in range(32):
                if i % 8 == MODG_END:
                    modg_rows(i // 8)
                if i < 31:
                    att_exp(i + 1)
                h, qt = divmod(i, 4)
                if qt == 0 and h >= 1:
                    act.wait_ge(S("pv_done"), h)
                act.wait_ge(S("pt_ready"), i + 1)
                act.activation(PTt[:, :, qt * P:(qt + 1) * P],
                               PS[:, 2048:2048 + TOK].rearrange("p (t n) -> p t n", t=NT), ACT.Copy).then_inc(
                    S("pt_evac"), 1)
                if i == 1:
                    q_squares(1)
                if i == 2:
                    qk_std(3, 16, 32)
                if qt == 2 and 3 <= h < 7:
                    q_columns(h + 1, 6)
                if qt == 1 and h >= 1:
                    act.wait_ge(S("b_tmp"), h)
                    act.activation(b_hi[:, h - 1, :], btmp[:], ACT.Copy).then_inc(S("b_hi"), 1)
            hi_part(N_MERGE0)
            hi_part(N_MERGE0 + 1)
            act.wait_ge(S("b_tmp"), HEADS)
            act.activation(b_hi[:, HEADS - 1, :], btmp[:], ACT.Copy).then_inc(S("b_hi"), 1)
            for n in range(N_MERGE0, NP):
                if n > N_MERGE0:
                    hi_part(n + 1)
                for j in (n - N_MERGE0 - 4,):
                    if j >= 0 and j % 4 == 0 and j // 4 < 8:
                        for jj in (0, 1):
                            m = 2 * (j // 4) + jj
                            act.wait_ge(S("m_tmp"), m + 1)
                            act.activation(m_hi[:, m, :], mtmp[2 * (m % 2)][:], ACT.Copy).then_inc(S("m_hi"), 1)

        @block.vector
        def _(dve):
            link = [0]

            def ln(ins):
                link[0] += 1
                ins.then_inc(S("dve_chain"), 1)
                dve.wait_ge(S("dve_chain"), link[0])

            def lo_part(n):
                if n >= NP or whole[n]:
                    return
                p, i = PIECES[n], parts_made[n] - 1
                dve.wait_ge(S("w_hi"), i + 1)
                dve.tensor_tensor(part(wlo[i % 2], p), part(raw_of(n)[0], p), part(whi[i % 2], p).bitcast(f32),
                                  ALU.subtract).then_inc(S("w_lo"), 1)

            dve.wait_ge(S("const_in"), 16)
            for d, m in enumerate((LE, GE)):
                dve.tensor_copy(tri_r[d][:], consts[:, m:m + P]).then_inc(S("triangles"), 1)
            dve.wait_ge(S("rowsT"), 2)
            dve.tensor_copy(cols[:], bank(7, 97)).then_inc(S("cols"), 1)
            dve.tensor_copy(convw[:], bank(6, 120)).then_inc(S("cols"), 1)

            def x_var(t):
                dve.wait_ge(S("x_ssq"), t + 1)
                dve.tensor_scalar(stat[:, t:t + 1], stat[:, t:t + 1], 1.0 / DM, EPS, ALU.mult, ALU.add).then_inc(
                    S("x_var"), 1)

            def x_norm(t):
                dve.wait_ge(S("x_std"), t + 1)
                ln(dve.reciprocal(stat[:, 8 + t:9 + t], stat[:, 8 + t:9 + t]))
                dve.tensor_scalar(xt[t % 2][:], xt[t % 2][:], stat[:, 8 + t:9 + t], None, ALU.mult).then_inc(
                    S("xn"), 1)

            def mod_columns(gi):
                g = MODS[gi]
                k0 = 4 * g["j"]
                dve.wait_ge(S("mod_cols_mm"), gi + 1)
                src = bank(6 + gi % 2, 8).rearrange("p (k v) -> p k v", v=2)
                off = 48 + 16 * g["scale"] + k0
                b = cols[:, off:off + 4].unsqueeze(2).to_broadcast([P, 4, 2])
                dst = modv[:, g["scale"], k0:k0 + 4, :]
                if not g["scale"]:
                    dve.tensor_tensor(dst, src, b, ALU.add).then_inc(S("mod_evac"), 1)
                    return
                dve.tensor_tensor(dst, src, b, ALU.add).then_inc(S("mod_evac"), 1)
                dve.wait_ge(S("mod_evac"), gi + 1)
                ln(dve.scalar_tensor_tensor(out=dst, in0=dst, scalar=1.0,
                                            in1=cols[:, 32 + k0:36 + k0].unsqueeze(2).to_broadcast([P, 4, 2]),
                                            op0=ALU.add, op1=ALU.mult))

            def h_columns(j):
                dve.wait_ge(S("xt_evac"), 4 * NT)
                for k in range(4 * j, 4 * j + 4):
                    for v, (a0, a1) in enumerate(((0, SEQ), (SEQ, TOK))):
                        ins = dve.tensor_scalar(xnT[:, k, a0:a1], xnT[:, k, a0:a1], modv[:, 1, k, v:v + 1],
                                                modv[:, 0, k, v:v + 1], ALU.mult, ALU.add)
                    ins.then_inc(S("h_ready"), 1)

            def h_lo_parts(j):
                for k in range(4 * j, 4 * j + 4):
                    dve.wait_ge(S("h_hi"), k + 1)
                    dve.tensor_tensor(h_lo[:, k, :], xnT[:, k, 0:SEQ], h_hi[:, k, :].bitcast(f32),
                                      ALU.subtract).then_inc(S("h_lo"), 1)
                    dve.tensor_tensor(hc_lo[:, k, :], xnT[:, k, SEQ:TOK], hc_hi[:, k, :].bitcast(f32),
                                      ALU.subtract).then_inc(S("h_lo"), 1)

            def conv(ci):
                it = ITEMS[ci]
                dve.wait_ge(S("conv_raw"), ci + 1)
                if ci >= 2:
                    dve.wait_ge(S("item_pe"), ci - 1)
                ct = {"q": 0, "k": 8, "v": 16}[it["what"]] + it["head"]
                a, r = acc[ci % 2], rawc[ci % 2]
                for tap in range(CONV):
                    w = convw[:, tap * 24 + ct:tap * 24 + ct + 1]
                    if tap == 0:
                        ln(dve.tensor_scalar(a[:], r[:, 0:772], w, None, ALU.mult))
                    else:
                        ins = dve.scalar_tensor_tensor(out=a[:], in0=r[:, tap:tap + 772], scalar=w, in1=a[:],
                                                       op0=ALU.mult, op1=ALU.add)
                        if tap < CONV - 1:
                            ln(ins)
                        else:
                            ins.then_inc(S("conv_done"), 1)

            def v_rows(ci):
                h = ITEMS[ci]["head"]
                dve.wait_ge(S("item_pe"), ci + 1)
                dve.tensor_copy(vl[:, :, h * P:(h + 1) * P], bank4(6))
                dve.tensor_copy(vc[:, :, h * P:(h + 1) * P], bank(7, 256, 128).rearrange("p (t n) -> p t n", t=CT)).then_inc(
                    S("v_evac"), 1)

            def flip_blocks(d):
                return dve.transpose(XX[d][:].rearrange("p u n -> p (u n)"), YY[d][:].rearrange("p u n -> p (u n)"))

            def gdn(slot):
                k, n, pr = slot["kind"], slot["n"], PAIRS[slot["pair"]]
                half = pr["half"]
                for d in (0, 1):
                    tile = pr["tiles"][d]
                    b = 4 + 2 * d + slot["i"] % 2
                    ps = bank4(b)
                    done = S(f"gd{d}")
                    dve.wait_ge(S(f"gp{d}"), slot["i"] + 1)
                    if k == "gram":
                        dve.wait_ge(S(f"dmask{d}"), slot["pair"] + 1)
                        for u in range(4):
                            col = unit_col(d, tile, 4 * half + u)
                            ins = dve.scalar_tensor_tensor(out=LL[d][:, u, :], in0=ps[:, u, :], scalar=crow[:, col:col + 1],
                                                           in1=DD[d][:, u, :], op0=ALU.mult, op1=ALU.mult)
                        ins.then_inc(done, 1)
                    elif k == "qk":
                        dve.tensor_tensor(DD[d][:], ps, DD[d][:], ALU.mult).then_inc(done, 1)
                    elif k == "couple":
                        if n == len(BLOCKS) - 1:
                            r0 = 64 * d
                            dve.tensor_copy(PM[d][r0:r0 + 64], bank4(b, 64)[r0:r0 + 64]).then_inc(done, 1)
                            continue
                        if n == len(BLOCKS) - 2:
                            for c0, _ in HALF_BLOCKS[d]:
                                ins = dve.tensor_copy(PM[d][c0:c0 + 32, :, 0:32], bank4(b, 32)[c0:c0 + 32])
                            ins.then_inc(done, 1)
                            continue
                        mo = STAGE + (2 * n + d) * 64
                        mask = consts[:, mo:mo + 64].unsqueeze(1).to_broadcast([P, 4, 64])
                        if n == 0:
                            upd = 0 if d else 1
                            y_of = lambda e: YY[d][:].rearrange("p u (b e s) -> p u b e s", e=2, s=1)[:, :, :, e, :]
                            i_of = lambda e: odd1(ident, 1, d, e).unsqueeze(1).to_broadcast([P, 4, 64, 1])
                            dve.tensor_copy(y_of(1 - upd), i_of(1 - upd))
                            src = ps.rearrange("p u (b e) -> p u b e", e=2)[:, :, :, 0 if d else 1]
                        else:
                            src = bank4(b, 64)
                        ins = dve.tensor_tensor(PM[d][:], src, mask, ALU.mult)
                        if n > 0:
                            ins.then_inc(done, 1)
                            continue
                        ln(ins)
                        ln(dve.tensor_tensor(y_of(upd), i_of(upd), PM[d][:].unsqueeze(3), ALU.subtract))
                        flip_blocks(d).then_inc(done, 1)
                    elif k == "correct":
                        if n == len(BLOCKS) - 1:
                            r0, c0 = 64 * d, 64 * (1 - d)
                            yv = YY[d][r0:r0 + 64, :, c0:c0 + 64]
                            dve.tensor_tensor(yv, yv, bank4(b, 64)[r0:r0 + 64], ALU.subtract).then_inc(S(f"gy{d}"), 1)
                            continue
                        if n == len(BLOCKS) - 2:
                            for c0, r0 in HALF_BLOCKS[d]:
                                yv = YY[d][c0:c0 + 32, :, r0:r0 + 32]
                                ins = dve.tensor_tensor(yv, yv, bank4(b, 32)[c0:c0 + 32], ALU.subtract)
                            ins.then_inc(done, 1)
                            continue
                        yv = odd(YY[d][:], BLOCKS[n], d)
                        pv = bank4(b, 64).rearrange("p u (b s) -> p u b s", s=BLOCKS[n])
                        ln(dve.tensor_tensor(yv, yv, pv, ALU.subtract))
                        flip_blocks(d).then_inc(done, 1)
                    elif k == "ks":
                        for u in range(4):
                            h = 4 * half + u
                            col = unit_col(d, tile, h)
                            ins = dve.scalar_tensor_tensor(out=RR[d][:, u, :], in0=ps[:, u, :], scalar=ngr[:, col:col + 1],
                                                           in1=v_of(h, tile), op0=ALU.mult, op1=ALU.add)
                        ins.then_inc(done, 1)
                    elif k == "qs":
                        if slot["pair"] == 2 * CT:
                            dve.wait_ge(S("oacc0"), 1)
                        for u in range(4):
                            h = 4 * half + u
                            o = o_acc[:, tile, h * P:(h + 1) * P]
                            ins = dve.scalar_tensor_tensor(out=o, in0=ps[:, u, :], scalar=DEC[:, tile * 2 + d, 0, h:h + 1],
                                                           in1=o, op0=ALU.mult, op1=ALU.add)
                        ins.then_inc(done, 1)
                    elif k == "az":
                        o = o_acc[:, tile, 4 * half * P:(4 * half + 4) * P].rearrange("p (u n) -> p u n", u=4)
                        dve.tensor_tensor(o, ps, o, ALU.add).then_inc(done, 1)
                    elif k == "kz":
                        for u in range(4):
                            h = 4 * half + u
                            s = SS[:, d, h, :]
                            ins = dve.scalar_tensor_tensor(out=s, in0=s, scalar=DEC[:, tile * 2 + d, 2, h:h + 1],
                                                           in1=ps[:, u, :], op0=ALU.mult, op1=ALU.add)
                        ins.then_inc(done, 1)

            def out_rows(j):
                dve.wait_ge(S("w_used"), GROUPS[OUTS[j]]["last"] + 1)
                dve.wait_ge(S("x_again"), 16 * LT)
                for t in range(LT):
                    if j:
                        dve.wait_ge(S(f"out_dma{t}"), 16 * j)
                    dve.tensor_tensor(ost[t][:], bank(4 * (j % 2) + t), grow[:, 512 * j:512 * j + 512], ALU.mult).then_inc(
                        S("out_psum"), 1)
                    dve.wait_ge(S("out_psum"), 4 * j + t + 1)
                    dve.tensor_tensor(ost[t][:], ost[t][:], xr[:, t, 512 * j:512 * j + 512], ALU.add).then_inc(
                        S("out_ready"), 1)

            def y_rows():
                dve.wait_ge(S("o_std"), 1)
                ln(dve.reciprocal(ssq_o[:], ssq_o[:]))
                ln(dve.tensor_tensor(ssq_o[:], ssq_o[:], rq[:], ALU.mult))
                for t in range(LT):
                    o = o_acc[:, t, :].rearrange("p (h n) -> p h n", h=8)
                    dve.tensor_tensor(o, o, ssq_o[:, 8 * t:8 * t + 8].unsqueeze(2).to_broadcast([P, 8, P]),
                                      ALU.mult).then_inc(S("y_ready"), 1)

            def a_columns(h):
                dve.wait_ge(S("yt_ready"), h + 1)
                dve.wait_ge(S(f"z_in{h % 2}"), 16 * (h // 2 + 1))
                if h >= 2:
                    dve.wait_ge(S("a_lo"), h - 1)
                dve.scalar_tensor_tensor(out=atmp[h % 2][:], in0=bank(4 + h % 4), scalar=cols[:, 96:97], in1=zst[h % 2][:],
                                         op0=ALU.mult, op1=ALU.mult).then_inc(S("a_tmp"), 1)

            def a_lo_part(h):
                dve.wait_ge(S("a_hi"), h + 1)
                dve.tensor_tensor(a_lo[:, h, :], atmp[h % 2][:], a_hi[:, h, :].bitcast(f32), ALU.subtract).then_inc(
                    S("a_lo"), 1)

            def rope_tables():
                dve.wait_ge(S("tab_in"), 48)
                for w0, tab in ((0, qtab), (128, ktab)):
                    for hf in (0, 1):
                        wv = wrow[:, w0 + 64 * hf:w0 + 64 * hf + 64].unsqueeze(1).to_broadcast([P, LT, 64])
                        for sn in (0, 1):
                            ln(dve.tensor_tensor(tab[:, :, 128 * hf + 64 * sn:128 * hf + 64 * sn + 64],
                                                 cs[:, :, 64 * sn:64 * sn + 64], wv, ALU.mult))

            def rope(rows_t, tab_t, nh):
                x1, x2 = rows_t[:, :, 0:64], rows_t[:, :, 64:128]
                tv = lambda k: tab_t[:, 64 * k:64 * k + 64].unsqueeze(1).to_broadcast([P, nh, 64])
                ln(dve.tensor_tensor(rt[0][:, 0:nh, :], x1, tv(0), ALU.mult))
                ln(dve.tensor_tensor(rt[1][:, 0:nh, :], x2, tv(3), ALU.mult))
                ln(dve.tensor_tensor(rt[2][:, 0:nh, :], x1, tv(1), ALU.mult))
                ln(dve.tensor_tensor(rt[3][:, 0:nh, :], x2, tv(2), ALU.mult))
                ln(dve.tensor_tensor(x1, rt[0][:, 0:nh, :], rt[1][:, 0:nh, :], ALU.subtract))
                return dve.tensor_tensor(x2, rt[2][:, 0:nh, :], rt[3][:, 0:nh, :], ALU.add)

            def qk_var(count, a0, a1):
                dve.wait_ge(S("qk_ssq"), count)
                dve.tensor_scalar(ssq_a[:, a0:a1], ssq_a[:, a0:a1], 1.0 / P, EPS, ALU.mult, ALU.add).then_inc(
                    S("qk_var"), 1)

            def qk_rstd(step, a0, a1):
                dve.wait_ge(S("qk_std"), step)
                ln(dve.reciprocal(ssq_a[:, a0:a1], ssq_a[:, a0:a1]))

            def q_tile(j, t):
                rv = bqr[:, t, 512 * j:512 * j + 512].rearrange("p (h n) -> p h n", h=4)
                sv = ssq_a[:, 16 * j + 4 * t:16 * j + 4 * t + 4].unsqueeze(2).to_broadcast([P, 4, P])
                ln(dve.tensor_tensor(rv, rv, sv, ALU.mult))
                rope(rv, qtab[:, t, :], 4).then_inc(S("q_rot"), 1)
                dve.wait_ge(S("q_rot"), 4 * j + t + 1)

            def k_tile(t):
                rv = kvr[:, t, 0:256].rearrange("p (h n) -> p h n", h=2)
                sv = ssq_a[:, 32 + 2 * t:34 + 2 * t].unsqueeze(2).to_broadcast([P, 2, P])
                ln(dve.tensor_tensor(rv, rv, sv, ALU.mult))
                if t < LT:
                    ln(rope(rv, ktab[:, t, :], 2))
                else:
                    ins = dve.tensor_tensor(rv, rv, wrow[:, 128:256].unsqueeze(1).to_broadcast([P, 2, P]), ALU.mult)
                    ins.then_inc(S("k_ctx_rows"), 1)

            def modg_columns(k):
                dve.wait_ge(S("modg_cols_mm"), k + 1)
                src = bank(7, 8).rearrange("p (k v) -> p k v", v=2)[:, :, 0]
                dve.tensor_tensor(GATE[:, 4 * k:4 * k + 4], src, cols[:, 80 + 4 * k:84 + 4 * k], ALU.add).then_inc(
                    S("modg_cols"), 1)

            for n in range(N_MODG0):
                lo_part(n + 1)
                for t in range(NT):
                    if n == X_AT[t] + 1:
                        x_var(t)
                    if n == X_AT[t] + 2:
                        x_norm(t)
                for gi, g in enumerate(MODS):
                    if n == g["last"] + 2:
                        mod_columns(gi)
                for j in range(4):
                    if n == H_AT[j]:
                        h_columns(j)
                    if n == H_AT[j] + 1:
                        h_lo_parts(j)
                r = n - N_FIN
                if r == 4:
                    dve.wait_ge(S("o_ssq"), 32)
                    ln(dve.tensor_tensor(ssq_o[:], ssq_o[:], rq[:], ALU.mult))
                    ln(dve.tensor_tensor(ssq_o[:], ssq_o[:], rq[:], ALU.mult))
                    dve.tensor_scalar(ssq_o[:], ssq_o[:], 1.0 / P, EPS, ALU.mult, ALU.add).then_inc(S("o_var"), 1)
                if r == 5:
                    y_rows()
                if r == 6:
                    rope_tables()
                if r == 11:
                    qk_var(12, 32, 44)
                if r == 12:
                    qk_rstd(1, 32, 44)
                if 7 <= r < 11:
                    for h in (2 * (r - 7), 2 * (r - 7) + 1):
                        a_columns(h)
                    for h in (2 * (r - 7), 2 * (r - 7) + 1):
                        a_lo_part(h)
                if 13 <= r < 15:
                    for t in range(3 * (r - 13), 3 * (r - 13) + 3):
                        k_tile(t)
                if n == GROUPS[BQS[0]]["last"] + 2:
                    qk_var(28, 0, 16)
                if n == GROUPS[BQS[0]]["last"] + 3:
                    qk_rstd(2, 0, 16)
                for t in range(LT):
                    if n == GROUPS[BQS[0]]["last"] + 4 + t:
                        q_tile(0, t)
                for gi, g in enumerate(CONVS):
                    e = n - g["last"]
                    if e in (1, 2):
                        conv(2 * gi + e - 1)
                    if e in (3, 4) and g["what"] == "v":
                        v_rows(2 * gi + e - 3)
                if n == GROUPS[G_BKV]["first"] + 5:
                    dve.wait_ge(S("ab_rows"), 1)
                    dve.wait_ge(S("beta"), 1)
                    ab = bank(6, NT * 32).rearrange("p (t c) -> p t c", t=NT)
                    v3 = lambda t: t[:].rearrange("p (t c) -> p t c", t=NT)
                    dve.wait_ge(S("alog_in"), 32)
                    dve.wait_ge(S("item_pe"), 24)
                    ln(dve.tensor_tensor(v3(ab_t[0]), ab[:, :, 16:32], dtb[:].unsqueeze(1).to_broadcast([P, NT, 16]), ALU.add))
                    ln(dve.tensor_scalar(ab_t[1][:], ab_t[0][:], -1.0, None, ALU.mult))
                    dve.tensor_tensor(ab_t[1][:], ab_t[0][:], ab_t[1][:], ALU.min).then_inc(S("negabs"), 1)
                    dve.wait_ge(S("ab_exp"), 1)
                    ln(dve.tensor_scalar(ab_t[3][:], ab_t[1][:], 1.0, None, ALU.add))
                    ln(dve.tensor_scalar(ab_t[3][:], ab_t[3][:], -1.0, None, ALU.add))
                    ln(dve.tensor_scalar(ab_t[4][:], ab_t[3][:], 0.0, None, ALU.is_equal))
                    ln(dve.tensor_tensor(ab_t[2][:], ab_t[2][:], ab_t[4][:], ALU.add))
                    ln(dve.tensor_tensor(ab_t[3][:], ab_t[3][:], ab_t[4][:], ALU.add))
                    ln(dve.reciprocal(ab_t[3][:], ab_t[3][:]))
                    ln(dve.tensor_tensor(ab_t[1][:], ab_t[1][:], ab_t[2][:], ALU.mult))
                    ln(dve.tensor_tensor(ab_t[1][:], ab_t[1][:], ab_t[3][:], ALU.mult))
                    ln(dve.scalar_tensor_tensor(out=ab_t[0][:], in0=ab_t[0][:], scalar=0.0, in1=ab_t[1][:],
                                                op0=ALU.max, op1=ALU.add))
                    dve.scalar_tensor_tensor(out=v3(gdec), in0=v3(ab_t[0]), scalar=-1.0,
                                             in1=alog[:].unsqueeze(1).to_broadcast([P, NT, 16]),
                                             op0=ALU.mult, op1=ALU.mult).then_inc(S("g_ready"), 1)
                    dve.wait_ge(S("item_pe"), 24)
                    ln(dve.tensor_scalar(rk[:], bank(7, 48), EPS, None, ALU.add))
                    dve.tensor_scalar(rq[:], bank(7, 32, 48), EPS, None, ALU.add).then_inc(S("ssq_eps"), 1)
                    dve.wait_ge(S("ssq_std"), 1)
                    ln(dve.reciprocal(rk[:], rk[:]))
                    ln(dve.reciprocal(rq[:], rq[:]))
                    ln(dve.tensor_scalar(rq[:], rq[:], float(HD ** -0.5), None, ALU.mult))
                    v4 = lambda t: t[:].rearrange("p (t d h) -> p t d h", t=NT, d=2)
                    rkb = rk[:].rearrange("p (t h) -> p t h", t=NT).unsqueeze(2).to_broadcast([P, NT, 2, 8])
                    ln(dve.tensor_tensor(v4(betar), v4(beta), rkb, ALU.mult))
                    ln(dve.tensor_tensor(v4(crow), v4(betar), rkb, ALU.mult))
                if n == GROUPS[G_BKV]["first"] + 7:
                    dve.wait_ge(S("decays"), 1)
                    ln(dve.tensor_scalar(ngr[:].rearrange("p (a h) -> p a h", h=8), DEC[:, :, 0, :], -1.0, None, ALU.mult))
                    ln(dve.tensor_tensor(v4(ngr), v4(ngr), rkb, ALU.mult))
                    ln(dve.tensor_copy(g_hi[:], gdec[:]))
                    dve.tensor_tensor(g_lo[:], gdec[:], g_hi[:].bitcast(f32), ALU.subtract).then_inc(S("prep"), 1)
                for q in range(4):
                    s = slot_at(n, q)
                    if s and s["kind"] not in ON_SCALAR:
                        gdn(s)
            def att_max(i):
                dve.wait_ge(S("sc_ready"), i + 1)
                ln(dve.reduce_max(nmax[:, i:i + 1], PS[:, (i % 2) * 1024:(i % 2) * 1024 + TOK], axis=AX.X))
                dve.tensor_scalar(nmax[:, i:i + 1], nmax[:, i:i + 1], -float(HD ** -0.5), None, ALU.mult).then_inc(
                    S("negmax"), 1)

            def b_parts(h):
                dve.wait_ge(S("pv_done"), h + 1)
                k = HEADS + h
                dve.wait_ge(S(f"z_in{k % 2}"), 16 * (k // 2 + 1))
                dve.tensor_tensor(btmp[:], bank(6), zst[k % 2][:], ALU.mult).then_inc(S("b_tmp"), 1)
                dve.wait_ge(S("b_hi"), h + 1)
                dve.tensor_tensor(b_lo[:, h, :], btmp[:], b_hi[:, h, :].bitcast(f32), ALU.subtract).then_inc(S("b_lo"), 1)

            att_max(0)
            for i in range(32):
                dve.wait_ge(S("exp_done"), i + 1)
                ln(dve.reciprocal(rsum[:, i:i + 1], rsum[:, i:i + 1]))
                dve.tensor_scalar(probs[i % 2][:], probs[i % 2][:], rsum[:, i:i + 1], None, ALU.mult).then_inc(
                    S("p_norm"), 1)
                if i < 31:
                    att_max(i + 1)
                if i % 8 == MODG_END:
                    modg_columns(i // 8)
                if i == 2:
                    qk_var(44, 16, 32)
                if i == 3:
                    qk_rstd(3, 16, 32)
                if i in (4, 6, 7, 8):
                    q_tile(1, (4, 6, 7, 8).index(i))
                if i % 4 == 1 and i >= 5:
                    b_parts(i // 4 - 1)
            lo_part(N_MERGE0)
            lo_part(N_MERGE0 + 1)
            b_parts(HEADS - 1)
            for n in range(N_MERGE0, NP):
                if n > N_MERGE0:
                    lo_part(n + 1)
                e = n - N_MERGE0
                if e >= 4 and e % 4 == 0 and e // 4 <= 8:
                    j = e // 4 - 1
                    for jj in (0, 1):
                        m = 2 * j + jj
                        b0 = 4 * (j % 2)
                        dve.wait_ge(S("w_used"), n)
                        dve.wait_ge(S(f"gates_in{m % 4}"), 32 * (m // 4 + 1))
                        if m >= 2:
                            dve.wait_ge(S("m_lo"), m - 1)
                        t0, t1 = mtmp[2 * (m % 2)], mtmp[2 * (m % 2) + 1]
                        ln(dve.tensor_tensor(t0[:], bank(b0 + jj), gsig[m % 4][:, 0, :], ALU.mult))
                        dve.tensor_tensor(t1[:], bank(b0 + 2 + jj), gsig[m % 4][:, 1, :], ALU.mult).then_inc(
                            S("m_psum"), 1)
                        dve.wait_ge(S("m_psum"), m + 1)
                        dve.tensor_tensor(t0[:], t0[:], t1[:], ALU.add).then_inc(S("m_tmp"), 1)
                    for jj in (0, 1):
                        m = 2 * j + jj
                        dve.wait_ge(S("m_hi"), m + 1)
                        dve.tensor_tensor(m_lo[:, m, :], mtmp[2 * (m % 2)][:], m_hi[:, m, :].bitcast(f32),
                                          ALU.subtract).then_inc(S("m_lo"), 1)
                if n == N_MERGE0 + 3:
                    for q in range(4):
                        dve.wait_ge(S("grow_mm"), 4 * q + 4)
                        dve.tensor_copy(grow[:, 512 * q:512 * q + 512], bank(4 + q)).then_inc(S("grow_evac"), 1)
                if n > N_OUT0 and (n - N_OUT0) % 8 == 0:
                    out_rows((n - N_OUT0) // 8 - 1)
            out_rows(3)

        @block.tensor
        def _(pe):
            pe.wait_ge(S("const_in"), 16)
            pe.wait_ge(S("rows_in"), 96)
            pe.transpose(bank(7, 97), rows[:], ident[0:97, 0:97]).then_inc(S("rowsT"), 1)
            pe.transpose(bank(6, 120), crows[:], ident[0:120, 0:120]).then_inc(S("rowsT"), 1)

            def x_transposes(t):
                pe.wait_ge(S("xn"), t + 1)
                for q4 in range(4):
                    n = 4 * t + q4
                    if n >= 4:
                        pe.wait_ge(S("xt_evac"), n - 3)
                    for u in range(4):
                        k = 4 * q4 + u
                        ins = pe.transpose(bank4(n % 4)[:, u, :], xt[t % 2][:, k * P:(k + 1) * P], ident)
                    ins.then_inc(S("xt_ready"), 1)

            def mod_cols(rows_t, b, name, count):
                pe.wait_ge(S(f"{name}_rows"), count)
                for q in range(4):
                    ins = pe.transpose(bank(b, 2, 2 * q), rows_t[:, q * P:(q + 1) * P], ident[0:2, 0:2])
                ins.then_inc(S(f"{name}_cols_mm"), 1)

            def item_work(ci):
                it = ITEMS[ci]
                pe.wait_ge(S("item_ready"), ci + 1)
                a = acc[ci % 2]
                if it["what"] == "v":
                    if ci > 8:
                        pe.wait_ge(S("v_evac"), ci - 8)
                    for t in range(LT):
                        pe.transpose(bank4(6)[:, t, :], a[:, t * P:(t + 1) * P], ident)
                    for t in range(CT):
                        ins = pe.transpose(bank(7, P, 128 + t * P), a[:, 516 + t * P:516 + (t + 1) * P], ident)
                else:
                    if it["what"] == "q":
                        pe.wait_ge(S("v_evac"), 8)
                    off = 48 if it["what"] == "q" else 0
                    for t in range(LT if off else NT):
                        a0 = t * P if t < LT else 516 + (t - LT) * P
                        ins = pe.matmul(bank(7, 1, off + t * 8 + it["head"]), a[:, a0:a0 + P], ones[:, 0:1],
                                        start=True, stop=True)
                ins.then_inc(S("item_pe"), 1)

            def three(out_ap, lhs, rhs, first, last, shared=False):
                (lh, ll), (rh, rl) = lhs, rhs
                pe.matmul(out_ap, lh, rh, start=first, stop=False, skip_group_check=shared)
                pe.matmul(out_ap, lh, rl, start=False, stop=False, skip_group_check=shared)
                return pe.matmul(out_ap, ll, rh, start=False, stop=last, skip_group_check=shared)

            LASTB = len(BLOCKS) - 1

            def gdn(slot):
                k, n, pr, i = slot["kind"], slot["n"], PAIRS[slot["pair"]], slot["i"]
                half = pr["half"]
                for d in (0, 1):
                    tile = pr["tiles"][d]
                    b = 4 + 2 * d + i % 2
                    ps = bank4(b)
                    if i:
                        pe.wait_ge(S(f"gd{d}"), i)
                    if k == "decay":
                        pe.wait_ge(S(f"gm{d}"), slot["pair"] + 1)
                    if slot["pair"] == 0 and k == "ks":
                        pe.wait_ge(S("states0"), 1)
                    if k == "decay":
                        pe.matmul(ps, tri_r[d][:], GMH[d][:], start=True, stop=False)
                        pe.matmul(ps, tri_r[d][:], GML[d][:], start=False, stop=True).then_inc(S(f"gp{d}"), 1)
                        continue
                    for u in range(4):
                        h = 4 * half + u
                        kt = kT_of(h, tile)
                        qt = qT[:, h, tile * P:(tile + 1) * P] if pr["lat"] else None
                        if k == "gram":
                            ins = pe.matmul(ps[:, u, :], kt, kt, start=True, stop=True)
                        elif k == "qk":
                            ins = pe.matmul(ps[:, u, :], qt, kt, start=True, stop=True)
                        elif k == "couple" and n == LASTB:
                            r0, c0 = 64 * (1 - d), 64 * d
                            ins = pe.matmul(bank4(b, 64)[c0:c0 + 64, u, :], LL[d][r0:r0 + 64, u, c0:c0 + 64],
                                            YY[d][r0:r0 + 64, u, r0:r0 + 64], start=True, stop=True)
                        elif k == "correct" and n == LASTB:
                            c0 = 64 * d
                            ins = pe.matmul(bank4(b, 64)[c0:c0 + 64, u, :], XX[d][c0:c0 + 64, u, c0:c0 + 64],
                                            PM[d][c0:c0 + 64, u, :], start=True, stop=True)
                        elif k in ("couple", "correct") and n == LASTB - 1:
                            for c0, r0 in HALF_BLOCKS[d]:
                                lhs, rhs = ((LL[d][r0:r0 + 32, u, c0:c0 + 32], YY[d][r0:r0 + 32, u, r0:r0 + 32]) if k == "couple"
                                            else (XX[d][c0:c0 + 32, u, c0:c0 + 32], PM[d][c0:c0 + 32, u, 0:32]))
                                ins = pe.matmul(bank4(b, 32)[c0:c0 + 32, u, :], lhs, rhs, start=True, stop=True)
                        elif k == "couple" and n == 0:
                            ins = pe.transpose(ps[:, u, :], LL[d][:, u, :], ident)
                        elif k == "couple":
                            rhs = odd1(YY[d][:, u, :], BLOCKS[n], d)
                            dst = bank4(b, 64)[:, u, :].rearrange("p (b s) -> p b s", s=BLOCKS[n])
                            ins = pe.matmul(dst, LL[d][:, u, :], rhs, start=True, stop=True)
                        elif k == "correct":
                            ins = pe.matmul(bank4(b, 64)[:, u, :], XX[d][:, u, :], PM[d][:, u, :], start=True, stop=True)
                        elif k == "flip":
                            ins = pe.transpose(ps[:, u, :], YY[d][:, u, :], ident)
                        elif k == "at":
                            ins = pe.transpose(ps[:, u, :], DD[d][:, u, :], ident)
                        elif k == "kt":
                            ins = pe.transpose(ps[:, u, :], kt, ident)
                        elif k == "ks":
                            ins = pe.matmul(ps[:, u, :], kt, SS[:, d, h, :], start=True, stop=True)
                        elif k == "z":
                            ins = pe.matmul(ps[:, u, :], XX[d][:, u, :], RR[d][:, u, :], start=True, stop=True)
                        elif k == "qs":
                            ins = pe.matmul(ps[:, u, :], qt, SS[:, d, h, :], start=True, stop=True)
                        elif k == "az":
                            ins = pe.matmul(ps[:, u, :], YY[d][:, u, :], ZZ[d][:, u, :], start=True, stop=True)
                        elif k == "kz":
                            ins = pe.matmul(ps[:, u, :], LL[d][:, u, :], ZZ[d][:, u, :], start=True, stop=True)
                    ins.then_inc(S(f"gp{d}"), 1)

            def piece(n):
                p = PIECES[n]
                gi = p["g"]
                g = GROUPS[gi]
                first, last = n == g["first"], n == g["last"]
                ins = None
                if first:
                    accs_free_needed(pe, gi)
                kind = p["kind"]
                if whole[n]:
                    place, loaded, count = raw_of(n)
                    pe.wait_ge(loaded, count)
                    b0 = 4 + gi % 2 if kind == "mod" else 7
                    for kk in range(p["nk"]):
                        ins = pe.matmul(bank(b0)[0:2], sc2[:, p["k0"] + kk, :], part3(place, p)[:, kk, :],
                                        start=first and kk == 0, stop=last and kk == p["nk"] - 1)
                    ins.then_inc(S("w_used"), 1)
                    return
                i = parts_made[n] - 1
                pe.wait_ge(S("w_lo"), i + 1)
                wh, wl = part3(whi[i % 2], p), part3(wlo[i % 2], p)
                for kk in range(p["nk"]):
                    k = p["k0"] + kk
                    st, sp_ = first and kk == 0, last and kk == p["nk"] - 1
                    if gi == G_CONV0:
                        pe.wait_ge(S("h_lo"), 2 * (k + 1))
                    if gi == OUTS[0]:
                        pe.wait_ge(S("m_lo"), k + 1)
                    if kind in ("conv", "gate", "merge"):
                        src = (h_hi, h_lo)
                        b0 = 3 * ((gi - G_CONV0) % 2)
                        if kind == "gate":
                            b0 = 2 * (GATES.index(gi) % 2)
                        if kind == "merge":
                            src = ((a_hi, a_lo), (b_hi, b_lo))[p["branch"]]
                            b0 = 4 * (p["j"] % 2) + 2 * p["branch"]
                        for j in (0, 1):
                            w = (wh[:, kk, j * P:(j + 1) * P], wl[:, kk, j * P:(j + 1) * P])
                            ins = three(bank(b0 + j), w, (src[0][:, k, :], src[1][:, k, :]), st, sp_)
                        if kind == "conv" and g["what"] != "q":
                            for j in (0, 1):
                                w = (wh[:, kk, j * P:(j + 1) * P], wl[:, kk, j * P:(j + 1) * P])
                                ins = three(bank(b0 + 2, 256, 256 * j), w, (hc_hi[:, k, :], hc_lo[:, k, :]),
                                            st and j == 0, sp_, shared=True)
                        if kind == "gate":
                            if kk == p["nk"] - 1:
                                ins.then_inc(S("w_used"), 1)
                            s = slot_at(n, kk)
                            if s:
                                if s["i"] == 0:
                                    pe.wait_ge(S("prep"), 1)
                                    pe.wait_ge(S("triangles"), 2)
                                    pe.wait_ge(S("kv_evac"), NT)
                                gdn(s)
                    elif kind in ("bkv", "bq", "out"):
                        b0 = {"out": 4 * (g.get("j", 0) % 2), "bq": 4 * g.get("half", 0)}.get(kind, 0)
                        for t in range(NT if kind == "bkv" else LT):
                            if kind == "bq" and st:
                                if gi == BQS[0] and t == 2:
                                    pe.wait_ge(S("gate_evac"), 2 * len(GATES))
                            if kind == "out":
                                l = (m_hi[:, k, t * P:(t + 1) * P], m_lo[:, k, t * P:(t + 1) * P])
                            elif t < LT:
                                l = (h_hi[:, k, t * P:(t + 1) * P], h_lo[:, k, t * P:(t + 1) * P])
                            else:
                                l = (hc_hi[:, k, (t - LT) * P:(t - LT + 1) * P], hc_lo[:, k, (t - LT) * P:(t - LT + 1) * P])
                            ins = three(bank(b0 + t), l, (wh[:, kk, :], wl[:, kk, :]), st, sp_)
                if kind == "ab":
                    for dst, (src_h, src_l) in ((bank(6), (h_hi, h_lo)), (bank(7, 256, 256), (hc_hi, hc_lo))):
                        for k in range(KT):
                            ins = three(dst[0:32], (wh[:, k, :], wl[:, k, :]), (src_h[:, k, :], src_l[:, k, :]),
                                        k == 0, k == KT - 1)
                if kind != "gate":
                    ins.then_inc(S("w_used"), 1)

            pe.wait_ge(S("silu_c"), 1)
            for n in range(N_MODG0):
                piece(n)
                for t in range(NT):
                    if n == X_AT[t] + 3:
                        x_transposes(t)
                for gi, g in enumerate(MODS):
                    if n == g["last"] + 1:
                        if gi >= 2:
                            pe.wait_ge(S("mod_evac"), gi - 1)
                        mod_cols(mrow, 6 + gi % 2, "mod", gi + 1)
                r = n - N_FIN
                if 6 <= r < 10:
                    if r == 6:
                        pe.wait_ge(S("y_ready"), LT)
                    for h in (2 * (r - 6), 2 * (r - 6) + 1):
                        if h >= 4:
                            pe.wait_ge(S("a_tmp"), h - 3)
                        for t in range(LT):
                            ins = pe.transpose(bank4(4 + h % 4)[:, t, :], o_acc[:, t, h * P:(h + 1) * P], ident)
                        ins.then_inc(S("yt_ready"), 1)
                for gi, g in enumerate(CONVS):
                    e = n - g["last"]
                    if e in (3, 4):
                        item_work(2 * gi + e - 3)
                if n == GROUPS[G_BKV]["first"] + 4:
                    pe.wait_ge(S("ab_cols"), 1)
                    for t in range(NT):
                        ins = pe.transpose(bank(6, 32, 32 * t), ab_c[:, t * P:(t + 1) * P], ident[0:32, 0:32])
                    ins.then_inc(S("ab_rows"), 1)
                if n == GROUPS[G_BKV]["first"] + 6:
                    pe.wait_ge(S("g_ready"), 1)
                    sums = bank(6, NT * 2 * 24).rearrange("p (t d w h) -> p t d w h", d=2, w=3, h=8)
                    logs = gdec[:].rearrange("p (t d h) -> p t d h", d=2, h=8)
                    for d in (0, 1):
                        for w, m in enumerate(((LE, GT, ONES), (GE, LT_, ONES))[d]):
                            ins = pe.matmul(sums[:, :, d, w, :], consts[:, m:m + P], logs[:, :, d, :], start=True, stop=True)
                    ins.then_inc(S("cum"), 1)
            def q_transposes(h, b):
                pe.wait_ge(S("q_rot"), LT if h < 4 else 2 * LT)
                for t in range(LT):
                    ins = pe.transpose(bank4(b)[:, t, :], bqr[:, t, h * P:(h + 1) * P], ident)
                ins.then_inc(S("qt_ready"), 1)

            pe.wait_ge(S("bq_evac"), 4)
            for h in range(4):
                q_transposes(h, h)
            pe.wait_ge(S("k_ctx_rows"), CT)
            for kv in range(KV):
                pe.wait_ge(S("bq_evac"), 6 + 2 * kv)
                for t in range(NT):
                    ins = pe.transpose(PS[:, (4 + 2 * kv) * 512 + t * P:(4 + 2 * kv) * 512 + (t + 1) * P],
                                       kvr[:, t, kv * P:(kv + 1) * P], ident)
                ins.then_inc(S("kt_ready"), 1)

            def scores(i):
                h, qt = divmod(i, 4)
                if i < 2:
                    pe.wait_ge(S("qt_evac"), 2 * i + 2)
                    pe.wait_ge(S("kt_evac"), i + 1)
                else:
                    pe.wait_ge(S("exp_done"), i - 1)
                if h >= 4 and qt == 0:
                    pe.wait_ge(S("qt_evac"), h + 1)
                b = 2 * (i % 2)
                q = qhT[:, h, qt * P:(qt + 1) * P]
                kv = h // (HEADS // KV)
                pe.matmul(bank(b), q, khT[:, kv, 0:512], start=True, stop=True)
                pe.matmul(bank(b + 1, 256), q, khT[:, kv, 512:TOK], start=True, stop=True).then_inc(S("sc_ready"), 1)

            def values(h):
                pe.wait_ge(S("pt_evac"), 4 * h + 4)
                if h >= 1:
                    pe.wait_ge(S("b_tmp"), h)
                if 3 <= h < 7:
                    pe.wait_ge(S("qt_evac"), h + 2)
                kv = h // (HEADS // KV)
                for t in range(NT):
                    ins = pe.matmul(bank(6), kvr[:, t, 256 + kv * P:256 + (kv + 1) * P], PTt[:, t, :],
                                    start=(t == 0), stop=(t == NT - 1))
                ins.then_inc(S("pv_done"), 1)

            scores(0)
            for i in range(32):
                if i < 31:
                    scores(i + 1)
                h, qt = divmod(i, 4)
                if qt == 0 and h >= 1:
                    values(h - 1)
                for n in modg_pieces(i):
                    piece(n)
                if i % 8 == MODG_END:
                    mod_cols(mrow_g, 7, "modg", i // 8 + 1)
                if qt == 2 and 3 <= h < 7:
                    pe.wait_ge(S("b_tmp"), h)
                    q_transposes(h + 1, 6)
                pe.wait_ge(S("p_norm"), i + 1)
                if i:
                    pe.wait_ge(S("pt_evac"), i)
                for t in range(NT):
                    ins = pe.transpose(PS[:, 2048 + t * P:2048 + (t + 1) * P], probs[i % 2][:, t * P:(t + 1) * P], ident)
                ins.then_inc(S("pt_ready"), 1)
            values(HEADS - 1)
            for n in range(N_MERGE0, NP):
                if n in (N_MERGE0, N_MERGE0 + 2):
                    pe.wait_ge(S("a_lo" if n == N_MERGE0 else "b_lo"), HEADS)
                piece(n)
                if n == N_MERGE0 + 1:
                    pe.wait_ge(S("pt_evac"), 32)
                    pe.wait_ge(S("b_tmp"), HEADS)
                    pe.wait_ge(S("modg_cols"), 4)
                    for k in range(KT):
                        pe.wait_ge(S("gcb"), k + 1)
                        pe.matmul(bank(4 + k // 4, P, (k % 4) * P), gcb[k % 4][:], ident, start=True, stop=True).then_inc(
                            S("grow_mm"), 1)


INPUTS = ["x", "c", "ctx", "c_ctx", "w_mod", "b_mod", "norm_w", "w_in", "conv_w", "a_log", "dt_bias", "a_norm_w",
          "q_norm_w", "k_norm_w", "w_proj_a", "w_proj_b", "w_out"]


def kernel(**inputs):
    import concourse.bacc as bacc
    from concourse.bass_utils import run_bass_kernel_spmd

    nc = bacc.Bacc("TRN2", target_bir_lowering=False, num_devices=1)
    arrays = {f"{name}_dram": np.ascontiguousarray(inputs[name]) for name in INPUTS}
    arrays["consts_dram"], arrays["rope_dram"] = shape_constants()
    args = [nc.dram_tensor(name, a.shape, mybir.dt.float32, kind="ExternalInput").ap() for name, a in arrays.items()]
    out = nc.dram_tensor("out_dram", (1, SEQ, DM), mybir.dt.float32, kind="ExternalOutput").ap()
    build(nc, *args, out)
    return run_bass_kernel_spmd(nc, [arrays], core_ids=[0]).results[0]["out_dram"]
```
